# Optimizing a Trainium2 kernel written in Bass

```python
import math
import jax, jax.numpy as jnp
from jax import lax
import numpy as np

D_MODEL = 2048
BATCH = 1
SEQ = 256
DEPTH = 1
DEC_BATCH = 8
DEC_SEQ = 4
PAST_LEN = 2048
PAGE_SIZE = 128

GDN_HEADS = 8
GDN_DK = 128
GDN_DV = 128
GDN_CONV = 4
MLSTM_HEADS = 8
MLSTM_DK = 128
MLSTM_DV = 128
D_FF = 5632
FFN_CONV = 3
CHUNK = 64
EPS = 1e-6

GDN_QK = GDN_HEADS * GDN_DK
GDN_V = GDN_HEADS * GDN_DV
GDN_QKV = 2 * GDN_QK + GDN_V
ML_QK = MLSTM_HEADS * MLSTM_DK
ML_V = MLSTM_HEADS * MLSTM_DV
ML_QKV = 2 * ML_QK + ML_V
IN_SIZES = (GDN_QKV, GDN_V, GDN_HEADS, GDN_HEADS, ML_QKV, MLSTM_HEADS, MLSTM_HEADS, ML_V, D_MODEL, D_MODEL)
IN_COLS = sum(IN_SIZES)

kernel_name = 'hybrid_gdn_mlstm_convffn_step'

def _rmsnorm(x, w):
    xf = x.astype(jnp.float32)
    y = xf * lax.rsqrt(jnp.mean(xf * xf, axis=-1, keepdims=True) + EPS)
    return y * w.astype(jnp.float32)

def _l2norm(x):
    return x * lax.rsqrt(jnp.sum(x * x, axis=-1, keepdims=True) + EPS)

def _causal_dwconv(x, buf, w):
    K = w.shape[0]
    T = x.shape[1]
    xp = jnp.concatenate([buf.astype(x.dtype), x], axis=1)
    y = sum(xp[:, j:j + T] * w[j] for j in range(K))
    return y, xp[:, T:]

def _gated_delta_chunked(q, k, v, g, beta, S0):
    B, H, T, DK = q.shape
    DV = v.shape[-1]
    L = math.gcd(T, CHUNK)
    N = T // L

    def blk(a):
        return a.reshape(B, H, N, L, *a.shape[3:])

    q, k, v, g, beta = blk(q), blk(k), blk(v), blk(g), blk(beta)
    G = jnp.cumsum(g, axis=-1)
    incl = jnp.tril(jnp.ones((L, L), dtype=bool))
    strict = jnp.tril(jnp.ones((L, L), dtype=bool), -1)
    decay = jnp.exp(jnp.where(incl, G[..., :, None] - G[..., None, :], -jnp.inf))
    a_strict = jnp.where(strict, beta[..., :, None] * jnp.einsum('bhnid,bhnjd->bhnij', k, k) * decay, 0.0)
    ut = jnp.eye(L, dtype=q.dtype) + a_strict
    u = lax.linalg.triangular_solve(ut, v * beta[..., None], left_side=True, lower=True, unit_diagonal=True)
    w = lax.linalg.triangular_solve(ut, k * (beta * jnp.exp(G))[..., None], left_side=True, lower=True, unit_diagonal=True)
    qk = jnp.einsum('bhnid,bhnjd->bhnij', q, k) * decay

    def step(S, xs):
        qc, kc, uc, wc, qkc, Gc = xs
        v_new = uc - jnp.einsum('bhld,bhdv->bhlv', wc, S)
        o = (jnp.einsum('bhld,bhdv->bhlv', qc * jnp.exp(Gc)[..., None], S)
             + jnp.einsum('bhij,bhjv->bhiv', qkc, v_new))
        g_last = Gc[..., -1]
        S = (S * jnp.exp(g_last)[..., None, None]
             + jnp.einsum('bhld,bhlv->bhdv', kc * jnp.exp(g_last[..., None] - Gc)[..., None], v_new))
        return S, o

    xs = tuple(jnp.moveaxis(a, 2, 0) for a in (q, k, u, w, qk, G))
    S, o = lax.scan(step, S0, xs)
    return jnp.moveaxis(o, 0, 2).reshape(B, H, T, DV), S

def _mlstm_chunked(q, k, v, ig, lf, C0, n0, m0):
    B, H, T, DK = q.shape
    DV = v.shape[-1]
    L = math.gcd(T, CHUNK)
    N = T // L

    def blk(a):
        return a.reshape(B, H, N, L, *a.shape[3:])

    q, k, v, ig, lf = blk(q), blk(k), blk(v), blk(ig), blk(lf)
    b = jnp.cumsum(lf, axis=-1)
    incl = jnp.tril(jnp.ones((L, L), dtype=bool))
    d_log = jnp.where(incl, b[..., :, None] - b[..., None, :] + ig[..., None, :], -jnp.inf)
    d_max = jnp.max(d_log, axis=-1)
    e_log = b[..., -1:] - b + ig
    e_max = jnp.max(e_log, axis=-1)
    qk = jnp.einsum('bhnid,bhnjd->bhnij', q, k)

    def step(carry, xs):
        C, n, m = carry
        qc, kc, vc, bc, dc, dmc, ec, emc, qkc = xs
        inter = bc + m[..., None]
        mt = jnp.maximum(inter, dmc)
        wi = jnp.exp(inter - mt)
        p = jnp.exp(dc - mt[..., None]) * qkc
        num = (wi[..., None] * jnp.einsum('bhvd,bhld->bhlv', C, qc)
               + jnp.einsum('bhls,bhsv->bhlv', p, vc))
        den = wi * jnp.einsum('bhd,bhld->bhl', n, qc) + jnp.sum(p, axis=-1)
        h = num / jnp.maximum(jnp.abs(den), jnp.exp(-mt))[..., None]
        b_last = bc[..., -1]
        m_new = jnp.maximum(b_last + m, emc)
        fw = jnp.exp(b_last + m - m_new)
        sw = jnp.exp(ec - m_new[..., None])
        C = fw[..., None, None] * C + jnp.einsum('bhl,bhlv,bhld->bhvd', sw, vc, kc)
        n = fw[..., None] * n + jnp.einsum('bhl,bhld->bhd', sw, kc)
        return (C, n, m_new), h

    xs = tuple(jnp.moveaxis(a, 2, 0) for a in (q, k, v, b, d_log, d_max, e_log, e_max, qk))
    (C, n, m), h = lax.scan(step, (C0, n0, m0), xs)
    return jnp.moveaxis(h, 0, 2).reshape(B, H, T, DV), C, n, m

def _hybrid_layer(x, gdn_conv_buf, gdn_S, ml_C, ml_n, ml_m, ffn_conv_buf,
                  norm_mix_w, w_in, gdn_conv_w, gdn_A_log, gdn_dt_bias, gdn_norm_w, w_branch_a,
                  ml_b_i, ml_b_f, w_branch_b, w_out, norm_ffn_w, w_up, ffn_conv_w, w_down):
    B, T, _ = x.shape
    f32 = jnp.float32
    h = _rmsnorm(x, norm_mix_w).astype(x.dtype)
    proj = h @ w_in
    idx = [int(i) for i in np.cumsum(IN_SIZES)[:-1]]
    g_qkv, g_z, g_a, g_b, m_qkv, m_i, m_f, m_o, gate_a, gate_b = jnp.split(proj, idx, axis=-1)

    def heads(a, n_heads, d):
        return a.reshape(B, T, n_heads, d).transpose(0, 2, 1, 3).astype(f32)

    c, new_gdn_conv = _causal_dwconv(g_qkv, gdn_conv_buf, gdn_conv_w)
    c = jax.nn.silu(c)
    gq, gk, gv = jnp.split(c, [GDN_QK, 2 * GDN_QK], axis=-1)
    gq = _l2norm(heads(gq, GDN_HEADS, GDN_DK)) * (GDN_DK ** -0.5)
    gk = _l2norm(heads(gk, GDN_HEADS, GDN_DK))
    gv = heads(gv, GDN_HEADS, GDN_DV)
    g = (-jnp.exp(gdn_A_log.astype(f32)) * jax.nn.softplus(g_a.astype(f32) + gdn_dt_bias.astype(f32))).transpose(0, 2, 1)
    beta = jax.nn.sigmoid(g_b.astype(f32)).transpose(0, 2, 1)
    go, new_gdn_S = _gated_delta_chunked(gq, gk, gv, g, beta, gdn_S.astype(f32))
    go = _rmsnorm(go.transpose(0, 2, 1, 3), gdn_norm_w) * jax.nn.silu(g_z.astype(f32).reshape(B, T, GDN_HEADS, GDN_DV))
    y_a = go.reshape(B, T, GDN_V).astype(x.dtype) @ w_branch_a

    mq, mk, mv = jnp.split(m_qkv, [ML_QK, 2 * ML_QK], axis=-1)
    mq = heads(mq, MLSTM_HEADS, MLSTM_DK)
    mk = heads(mk, MLSTM_HEADS, MLSTM_DK) * (MLSTM_DK ** -0.5)
    mv = heads(mv, MLSTM_HEADS, MLSTM_DV)
    ig = (m_i.astype(f32) + ml_b_i.astype(f32)).transpose(0, 2, 1)
    lf = jax.nn.log_sigmoid(m_f.astype(f32) + ml_b_f.astype(f32)).transpose(0, 2, 1)
    mh, new_C, new_n, new_m = _mlstm_chunked(mq, mk, mv, ig, lf, ml_C.astype(f32), ml_n.astype(f32), ml_m.astype(f32))
    mh = mh.transpose(0, 2, 1, 3).reshape(B, T, ML_V) * jax.nn.sigmoid(m_o.astype(f32))
    y_b = mh.astype(x.dtype) @ w_branch_b

    mixed = jax.nn.sigmoid(gate_a) * y_a + jax.nn.sigmoid(gate_b) * y_b
    x = x + mixed @ w_out

    h = _rmsnorm(x, norm_ffn_w).astype(x.dtype)
    u, new_ffn_conv = _causal_dwconv(h @ w_up, ffn_conv_buf, ffn_conv_w)
    u_gate, u_val = jnp.split(u, 2, axis=-1)
    x = x + (jax.nn.silu(u_gate) * u_val) @ w_down
    return x, (new_gdn_conv, new_gdn_S, new_C, new_n, new_m, new_ffn_conv)

def setup_inputs(seed: int = 0) -> dict:
    key = jax.random.key(seed)
    ks = jax.random.split(key, 26)
    f32 = jnp.float32

    def nrm(k, shape, scale):
        return jax.random.normal(k, shape, f32) * scale

    x_prompt = nrm(ks[0], (BATCH, SEQ, D_MODEL), 1.0)
    x_sample = nrm(ks[1], (DEC_BATCH, DEC_SEQ, D_MODEL), 1.0)
    state_gdn_conv = nrm(ks[2], (DEPTH, DEC_BATCH, GDN_CONV - 1, GDN_QKV), 1.0)
    state_gdn_S = nrm(ks[3], (DEPTH, DEC_BATCH, GDN_HEADS, GDN_DK, GDN_DV), 0.3)
    state_ml_C = nrm(ks[4], (DEPTH, DEC_BATCH, MLSTM_HEADS, MLSTM_DV, MLSTM_DK), 0.3)
    state_ml_n = nrm(ks[5], (DEPTH, DEC_BATCH, MLSTM_HEADS, MLSTM_DK), 0.3)
    state_ml_m = jax.random.uniform(ks[6], (DEPTH, DEC_BATCH, MLSTM_HEADS), f32, 0.0, 4.0)
    state_ffn_conv = nrm(ks[7], (DEPTH, DEC_BATCH, FFN_CONV - 1, 2 * D_FF), 1.0)

    norm_mix_w = 1.0 + nrm(ks[8], (DEPTH, D_MODEL), 0.02)
    w_in = nrm(ks[9], (DEPTH, D_MODEL, IN_COLS), D_MODEL ** -0.5)
    gdn_conv_w = nrm(ks[10], (DEPTH, GDN_CONV, GDN_QKV), GDN_CONV ** -0.5)
    gdn_A_log = jnp.log(jax.random.uniform(ks[11], (DEPTH, GDN_HEADS), f32, 1.0, 16.0))
    dt = jnp.exp(jax.random.uniform(ks[12], (DEPTH, GDN_HEADS), f32, math.log(1e-3), math.log(1e-1)))
    gdn_dt_bias = dt + jnp.log(-jnp.expm1(-dt))
    gdn_norm_w = 1.0 + nrm(ks[13], (DEPTH, GDN_DV), 0.02)
    w_branch_a = nrm(ks[14], (DEPTH, GDN_V, D_MODEL), GDN_V ** -0.5)
    ml_b_i = nrm(ks[15], (DEPTH, MLSTM_HEADS), 0.1)
    ml_b_f = jnp.linspace(3.0, 6.0, MLSTM_HEADS, dtype=f32)[None, :] + nrm(ks[16], (DEPTH, MLSTM_HEADS), 0.1)
    w_branch_b = nrm(ks[17], (DEPTH, ML_V, D_MODEL), ML_V ** -0.5)
    w_out = nrm(ks[18], (DEPTH, D_MODEL, D_MODEL), D_MODEL ** -0.5)
    norm_ffn_w = 1.0 + nrm(ks[19], (DEPTH, D_MODEL), 0.02)
    w_up = nrm(ks[20], (DEPTH, D_MODEL, 2 * D_FF), D_MODEL ** -0.5)
    ffn_conv_w = nrm(ks[21], (DEPTH, FFN_CONV, 2 * D_FF), FFN_CONV ** -0.5)
    w_down = nrm(ks[22], (DEPTH, D_FF, D_MODEL), D_FF ** -0.5)
    norm_final_w = 1.0 + nrm(ks[23], (D_MODEL,), 0.02)
    return {
        'x_prompt': x_prompt, 'x_sample': x_sample,
        'state_gdn_conv': state_gdn_conv, 'state_gdn_S': state_gdn_S,
        'state_ml_C': state_ml_C, 'state_ml_n': state_ml_n, 'state_ml_m': state_ml_m,
        'state_ffn_conv': state_ffn_conv,
        'norm_mix_w': norm_mix_w, 'w_in': w_in, 'gdn_conv_w': gdn_conv_w, 'gdn_A_log': gdn_A_log,
        'gdn_dt_bias': gdn_dt_bias, 'gdn_norm_w': gdn_norm_w, 'w_branch_a': w_branch_a,
        'ml_b_i': ml_b_i, 'ml_b_f': ml_b_f, 'w_branch_b': w_branch_b, 'w_out': w_out,
        'norm_ffn_w': norm_ffn_w, 'w_up': w_up, 'ffn_conv_w': ffn_conv_w, 'w_down': w_down,
        'norm_final_w': norm_final_w,
    }

def reference(x_prompt, x_sample, state_gdn_conv, state_gdn_S, state_ml_C, state_ml_n, state_ml_m, state_ffn_conv,
              norm_mix_w, w_in, gdn_conv_w, gdn_A_log, gdn_dt_bias, gdn_norm_w, w_branch_a,
              ml_b_i, ml_b_f, w_branch_b, w_out, norm_ffn_w, w_up, ffn_conv_w, w_down, norm_final_w):
    f32 = jnp.float32
    bp = x_prompt.shape[0]
    yp, ys = x_prompt, x_sample
    new_p, new_s = [], []
    for l in range(DEPTH):
        w = (norm_mix_w[l], w_in[l], gdn_conv_w[l], gdn_A_log[l], gdn_dt_bias[l], gdn_norm_w[l], w_branch_a[l],
             ml_b_i[l], ml_b_f[l], w_branch_b[l], w_out[l], norm_ffn_w[l], w_up[l], ffn_conv_w[l], w_down[l])
        p_init = (jnp.zeros((bp, GDN_CONV - 1, GDN_QKV), x_prompt.dtype),
                  jnp.zeros((bp, GDN_HEADS, GDN_DK, GDN_DV), f32),
                  jnp.zeros((bp, MLSTM_HEADS, MLSTM_DV, MLSTM_DK), f32),
                  jnp.zeros((bp, MLSTM_HEADS, MLSTM_DK), f32),
                  jnp.zeros((bp, MLSTM_HEADS), f32),
                  jnp.zeros((bp, FFN_CONV - 1, 2 * D_FF), x_prompt.dtype))
        yp, sp = _hybrid_layer(yp, *p_init, *w)
        ys, ss = _hybrid_layer(ys, state_gdn_conv[l], state_gdn_S[l], state_ml_C[l], state_ml_n[l], state_ml_m[l],
                               state_ffn_conv[l], *w)
        new_p.append(sp)
        new_s.append(ss)
    y_prompt = _rmsnorm(yp, norm_final_w).astype(x_prompt.dtype)
    y_sample = _rmsnorm(ys, norm_final_w).astype(x_sample.dtype)

    def stack(states, i):
        return jnp.stack([s[i] for s in states])

    return (y_prompt, y_sample,
            stack(new_p, 0), stack(new_p, 1), stack(new_p, 2), stack(new_p, 3), stack(new_p, 4), stack(new_p, 5),
            stack(new_s, 0), stack(new_s, 1), stack(new_s, 2), stack(new_s, 3), stack(new_s, 4), stack(new_s, 5))


_drawn_inputs = setup_inputs


def setup_inputs(seed=0):
    import zlib

    import numpy as np

    out = dict(_drawn_inputs(seed))
    spreads = {}
    factors = {'gdn_norm_w': 8.0, 'norm_ffn_w': 2.948, 'norm_final_w': 2.866}
    for name, (base, spread) in spreads.items():
        noise = np.random.default_rng([zlib.crc32(name.encode()), seed]).standard_normal(out[name].shape)
        drawn = base * np.exp(spread * noise) if base else spread * noise
        out[name] = __import__('jax').numpy.asarray(drawn.astype(out[name].dtype))
    for name, factor in factors.items():
        out[name] = (out[name] * factor).astype(out[name].dtype)
    return out
```

```python
import concourse.bass as bass
from concourse import mybir
from concourse.alu_op_type import AluOpType as ALU
from contextlib import ExitStack

P = 128
F32 = mybir.dt.float32
F32R = mybir.dt.float32r
ACT = mybir.ActivationFunctionType
EPS = 1e-6
NEG = -1e30
SIG_MIN = -40.0
GDN_STAGES, MLSTM_STAGES = 29, 8
EXP_LN = "natural_log_exp_and_others"


class Steps:

    def __init__(self, sem, names):
        self.sem, self.names, self.at = sem, names.split(), 0
        assert len(set(self.names)) == len(self.names)

    def done(self, name):
        assert self.names[self.at % len(self.names)] == name, (name, self.names[self.at % len(self.names)])
        self.at += 1
        return self.sem, 1

    def after(self, name, r=0):
        return self.sem, r * len(self.names) + self.names.index(name) + 1

    def before(self, r):
        return self.sem, r * len(self.names)


def build(nc, a, o):
    D = a["w_in"].shape[1]
    KT = D // P
    TP = a["x_prompt"].shape[1]
    NB, L = a["x_sample"].shape[0], a["x_sample"].shape[1]
    TS = NB * L
    T = TP + TS
    CH = 64
    NCH = TP // CH
    H = a["state_gdn_S"].shape[2]
    FT = a["w_down"].shape[1] // P
    GC, QKV = a["gdn_conv_w"].shape[1:]
    FC = a["ffn_conv_w"].shape[1]
    GPAD, FPAD = GC - 1, FC - 1
    GS, FS = GPAD + L, FPAD + L
    GW, FW = GPAD + TP + NB * GS, FPAD + TP + NB * FS
    GV, FV = GW - GPAD, FW - FPAD
    c_z = QKV
    c_ga = c_z + H * P
    c_gb = c_ga + H
    c_mqkv = c_gb + H
    c_mi = c_mqkv + 3 * H * P
    c_mf = c_mi + H
    c_mo = c_mf + H
    c_gate = c_mo + H * P
    assert (D, T, H, NCH, FT, GC, FC) == (2048, 288, 8, 4, 44, 4, 3) and c_gate + 2 * D == a["w_in"].shape[2]
    QSCALE = float(P) ** -0.5
    PARTS = [(P, 0, 0), (P, P, 1), (TS, TP, 2)]
    TB = T * 4
    NG = 512
    NLEV = 6

    def row_tiles(w):
        return w[0].rearrange("(k p) n -> p k n", p=P)

    w_in, w_ba, w_bb, w_out, w_up, w_down = (
        row_tiles(a[n]) for n in ("w_in", "w_branch_a", "w_branch_b", "w_out", "w_up", "w_down"))
    xp_rows = a["x_prompt"][0].rearrange("(c p) d -> p c d", p=P)
    xs_rows = a["x_sample"].rearrange("b t d -> (b t) d")

    q_z, q_heads, q_gate, q_branch, q_out, q_ffn = 6, 8, 16, 24, 28, 32
    g_z, g_heads, g_gate, g_branch, g_out, g_ffn = 6, 8, 16, 24, 32, 36
    CHUNKS = [4, 4, 3]
    N_BLOCKS = 65 * 16
    N_CONST = 5 + 4 * 2 - 2 + 4 * 6 + 3 + 1
    N_STORED, N_LROW = 4, 4 + 4 * sum(CHUNKS)

    ctx = ExitStack()
    with ctx:
        end = nc.sbuf_usable_end
        top = (nc.sbuf_base + 31) // 32 * 32

        def size_of(shape):
            n = 4
            for s in shape[1:]:
                n *= s
            return (n + 31) // 32 * 32

        class Region:

            def __init__(self, at, nbytes):
                self.at, self.end = at, at + nbytes
                assert self.end <= end, (self.end, end)

            def put(self, name, shape, dt=F32):
                n = size_of(shape)
                assert self.at + n <= self.end, (name, self.at + n - self.end)
                t = nc.alloc_sbuf_tensor_at(name, shape, dt, offset=self.at)
                self.at += n
                return t

        b_raw = top
        b_hi = b_raw + 4 * 4 * NG * 4
        b_lo = b_hi + 4 * 4 * P * 4
        b_gq = b_lo + 4 * 4 * P * 4
        b_x1 = b_gq + 3 * H * GW * 4
        b_zm = b_x1 + 6 * TB
        b_e = b_zm + 4 * H * TB
        b_h = b_e + 2 * H * TB
        b_mx = b_h + 2 * KT * TB
        raw = nc.alloc_sbuf_tensor_at("w_raw", [P, 4, KT, P], F32, offset=b_raw)
        whi = nc.alloc_sbuf_tensor_at("w_hi", [P, 4, 4, P], F32R, offset=b_hi)
        wlo = nc.alloc_sbuf_tensor_at("w_lo", [P, 4, 4, P], F32R, offset=b_lo)
        whi2 = nc.alloc_sbuf_tensor_at("w_hi_2", [P, 4, 4, P], F32R, offset=b_zm)
        wlo2 = nc.alloc_sbuf_tensor_at("w_lo_2", [P, 4, 4, P], F32R, offset=b_zm + 4 * 4 * P * 4)

        def tiles(name, at, n, dt=F32):
            return nc.alloc_sbuf_tensor_at(name, [P, n, T], dt, offset=at)

        gq = nc.alloc_sbuf_tensor_at("gdn_qkv", [P, 3 * H, GW], F32, offset=b_gq)
        zm = tiles("mqkv_z", b_zm, 4 * H)
        h_hi, h_lo = tiles("h_hi", b_h, KT, F32R), tiles("h_lo", b_h + KT * TB, KT, F32R)
        go_hi, go_lo = tiles("go_hi", b_e, H, F32R), tiles("go_lo", b_e + H * TB, H, F32R)
        mh_hi, mh_lo = tiles("mh_hi", b_zm, H, F32R), tiles("mh_lo", b_zm + H * TB, H, F32R)
        gates = tiles("gates", b_gq, 2 * KT)
        mix_hi, mix_lo = tiles("mix_hi", b_h, KT, F32R), tiles("mix_lo", b_h + KT * TB, KT, F32R)
        mix_a, mix_b = tiles("mix_a", b_zm + 3 * H * TB, 4), tiles("mix_b", b_zm + (3 * H + 4) * TB, 4)
        x2 = tiles("x2", b_zm + 2 * H * TB, KT)
        f_hi, f_lo = tiles("f_hi", b_gq, KT, F32R), tiles("f_lo", b_gq + KT * TB, KT, F32R)
        u_hi, u_lo = tiles("u_hi", b_h, KT, F32R), tiles("u_lo", b_h + KT * TB, KT, F32R)
        x_rows = nc.alloc_sbuf_tensor_at("x_rows", [P, 3, D], F32, offset=b_zm)
        e0 = Region(b_e, 2 * H * TB)
        conv_rows = e0.put("conv_rows", [NB * GPAD, QKV])
        w_rows = e0.put("w_rows", [GC * 3 * H, P])
        norm_rows = e0.put("norm_rows", [3 * KT, P])
        n_rows = e0.put("n_rows", [NB * H, P])
        y_rows = nc.alloc_sbuf_tensor_at("y_rows", [P, 3, D], F32, offset=b_h)
        yt = tiles("y_tiles", b_gq, 8)

        mx = Region(b_mx, end - b_mx)
        ident = mx.put("ident", [P, P])
        ones = mx.put("ones", [P, P])
        incl = mx.put("mask_chunk", [P, P])
        incl_s = mx.put("mask_seq", [TS, TS])
        lev = mx.put("mask_level", [P, NLEV, P])
        seq = mx.put("seq_of", [TS, NB])
        gcw = mx.put("gdn_conv_w_t", [P, GC, 3 * H])
        cols = mx.put("token_cols", [P, 5, 3, H])
        nbeta = mx.put("minus_beta", [P, 3, H])
        rows = mx.put("token_rows", [32 + H, 3 * T + NCH + NB])
        wn = mx.put("norm_w", [P, 3, KT])
        wgn = mx.put("gdn_norm_w_t", [P, 1])
        eps = mx.put("eps_col", [P, 1])
        rstd = mx.put("rstd", [P, 3])
        n_s = mx.put("n_sample", [P, NB, H])
        n_p = mx.put("n_prompt", [P, H])
        b_scr, n_scr = mx.at, mx.end - mx.at
        g_row = rows[0:H, 0:2 * T].rearrange("h (r t) -> h r t", r=2)
        m_row = rows[32:32 + H, :]

        s0 = Region(b_scr, n_scr)
        sm_raw = nc.alloc_sbuf_tensor_at("small_w", [P, KT, P], F32, offset=b_zm + size_of([P, 3, D]))
        sm_hi, sm_lo = s0.put("small_w_hi", [P, KT, P], F32R), s0.put("small_w_lo", [P, KT, P], F32R)
        s1 = Region(b_scr, n_scr)
        sp_in, sp_out = s1.put("sp_in", [H, 3, T]), s1.put("sp_out", [H, 3, T])
        cum = [s1.put(f"cum{i}", [H, 2, T]) for i in range(2)]
        cmx = [s1.put(f"cum_max{i}", [H, T]) for i in range(2)]
        c_row, e_row = s1.put("c_row", [H, T]), s1.put("e_row", [H, T])
        sw_row = s1.put("sw_row", [H, T])
        ig, mmx = s1.put("ig", [H, T]), s1.put("m_max", [H, T])
        NC = NCH + NB
        bl, cl = s1.put("b_last", [H, NC]), s1.put("c_last", [H, NC])
        m_in, m_new, f_row = s1.put("m_in", [H, NC]), s1.put("m_new", [H, NC]), s1.put("fw_row", [H, NC])
        hcol = s1.put("head_cols", [H, 8])
        s2, s3 = Region(b_x1, 6 * TB), Region(b_x1, 6 * TB)
        cv = s2.put("conv_out", [P, 3 * GV])
        dec, bd, at_, nt0, nt1, psb = (s3.put(n, [P, T]) for n in ("decay", "beta_decay", "at", "nt0", "nt1", "p_sb"))
        s4 = Region(b_x1, 6 * TB)
        vnm = s4.put("v_new_by_seq", [TS, NB, P])
        gout = s4.put("gdn_out", [P, T])
        s5 = Region(b_scr, n_scr)
        sgz_at = s5.at
        sg = s5.put("sig", [P, 3 * GV + T])
        s6 = Region(sgz_at, size_of([P, 3 * GV + T]))
        rn = s6.put("rn", [P, 2, T])
        sq = s6.put("sq", [P, 2, T])
        s7 = Region(sgz_at, size_of([P, 3 * GV + T]))
        xx = s7.put("x_xt", [P, 2, T])
        rso = s7.put("rs_o", [P, T])
        qkv = s5.put("qkv", [P, 3, T])
        zz = s5.put("z_silu", [P, T])
        qe, ke = s5.put("qe", [P, T]), s5.put("ke", [P, T])
        eg = s5.put("eg", [P, T])
        kg_at = s5.at
        kg, bv = s5.put("kg", [P, 3, P]), s5.put("bv", [P, 3, P])
        rsel = nc.alloc_sbuf_tensor_at("row_sel", [H, 2, T], F32, offset=kg_at)
        pt = s5.put("pt", [P, T])
        S = s5.put("S", [P, P])
        rr, vn = s5.put("resid", [P, P]), s5.put("v_new", [P, P])
        ks_s, r_s, vn_s = s5.put("ks_sample", [P, TS]), s5.put("resid_s", [TS, P]), s5.put("v_new_s", [TS, P])
        ss = s5.put("S_sample", [P, NB, P])
        sqo = nc.alloc_sbuf_tensor_at("sq_o", [P, T], F32, offset=kg_at + size_of([P, 3, P]))
        s8 = Region(b_scr, n_scr)
        mk, mv = s8.put("mk", [P, T]), s8.put("mv", [P, T])
        qw, prd = s8.put("qw", [P, T]), s8.put("qw_n", [P, T])
        kw, vt = s8.put("kw", [P, 3, P]), s8.put("vt", [P, 3, P + 1])
        md, mpt = s8.put("m_decay", [P, T]), s8.put("m_pt", [P, T])
        emt = s8.put("emt_fw", [P, T + NC])
        ctn = s8.put("ct_n", [P, P + 1])
        so = s8.put("sig_o", [P, T])
        dn, mh = s8.put("den", [P, T]), s8.put("mh", [P, T])
        cs = s8.put("C_sample", [P, NB, P])
        cts_at = s8.at
        cts = s8.put("Ct_sample", [P, NB, P])
        km = nc.alloc_sbuf_tensor_at("kw_by_seq", [TS, NB, P], F32, offset=cts_at)
        cout = nc.alloc_sbuf_tensor_at("C_prompt", [P, P], F32, offset=cts_at)
        mrsel = nc.alloc_sbuf_tensor_at("m_row_sel", [32 + H, 3 * T + NC], F32, offset=cts_at)
        s9 = Region(b_scr, n_scr)
        g_last = s9.put("gdn_last_cols", [P, 12, GPAD * (1 + NB)])
        g_lrow = s9.put("gdn_last_rows", [GPAD * (1 + NB), 3, NG])
        s10 = Region(b_scr, n_scr)
        xg = s10.put("x_group", [P, 3, NG])
        st_rows = s10.put("ffn_old_rows", [NB * FPAD, 2, NG])
        u_out = s10.put("ffn_last_sel", [P, 8, FPAD * (1 + NB)])
        u_lrow = s10.put("ffn_last_rows", [FPAD * (1 + NB), 2, NG])
        ssq, sqt, r2 = s10.put("ssq", [P, T]), s10.put("sq_t", [P, T]), s10.put("r2", [P, T])
        ac = s10.put("act", [P, 2, T])
        fw_rows = s10.put("ffn_w_rows", [2 * FT, FC, P])
        n_out = s10.put("n_rows_out", [NB * H, 2, P])
        e1 = Region(b_e, 2 * H * TB)
        uu = e1.put("u_padded", [P, 4, FW])
        ug, uv = e1.put("u_gate", [P, 4, FV]), e1.put("u_val", [P, 4, FV])
        u_last = e1.put("u_last", [P, 4 * 2 * 4, FPAD * (1 + NB)])
        fcw = e1.put("ffn_conv_w_t", [P, FC, 2 * FT])

        ps = ctx.enter_context(nc.psum_tensor("products", [P, 4, NG], F32))
        pm = ctx.enter_context(nc.psum_tensor("mixer", [P, 4, NG], F32))

        def sem(name):
            return ctx.enter_context(nc.semaphore(name))

        landed = [sem(f"unit_landed_{s}") for s in range(4)]
        hi_ready, lo_ready = sem("block_hi_ready"), sem("block_lo_ready")
        blocks, bank_free = sem("blocks_multiplied"), sem("bank_free")
        x_in, rows_in, small_in = sem("x_rows_in"), sem("const_rows_in"), sem("small_w_in")
        consts = sem("constants_made")
        x_in2, old_in, ss_in, cs_in = sem("x_group_in"), sem("ffn_old_rows_in"), sem("S_in"), sem("C_in")
        fw_in = sem("ffn_w_rows_in")
        stored, ss_out, cs_out = sem("outputs_stored"), sem("S_stored"), sem("C_stored")
        lrow_out, y_out = sem("last_rows_stored"), sem("y_stored")

        st_a = Steps(sem("start_act"), "sq0 sq1 sq2 lnp lns expp exps smhi " + " ".join(f"hi{f}" for f in range(KT)))
        st_d = Steps(sem("start_dve"), "xs0 xs1 xs2 smlo cw nw ns old0 old1 old2 " + " ".join(f"lo{f}" for f in range(KT)))
        st_t = Steps(sem("start_pe"), "consts old " + " ".join(f"x{f}" for f in range(KT)) + " small")

        LEVELS = range(1, NLEV)
        ga = Steps(sem("gdn_act"), "c0 c1 c2 sg1 sg2 sg3 rn1 rn2 eg d1 d2 kg0 kg1 kg2 x0a x0b psb1s "
                   + " ".join(f"psb{l}" for l in LEVELS) + " vn0 ks_s vn_s vn1 vn2 vn3 sqo rs1 rs2 hi")
        gd = Steps(sem("gdn_dve"), "rsel " + " ".join(f"cv{t}{j}" for j in range(1, GC) for t in range(3))
                   + " clampz qkv1 qkv2 k q ke qe d0 d1 d2 bv0 bv1 bv2 bd1 bd2 at1 at2 pt1 pt2 n0a n0b xt1 xt2 n1a n1b xx1s "
                   + " ".join(f"xx{l} n{l + 1}" for l in LEVELS[:-1]) + " xx5 S0 rs R1 S1 R2 S2 R3 S3 go ss lo")
        gp = Steps(sem("gdn_pool"), "clamp zz sq vnm sse goz")
        gt = Steps(sem("gdn_pe"), "norm tr kk kq x0 " + " ".join(f"p{l} xx{l}" for l in LEVELS)
                   + " T0 ksS u0 trS k1 TS T1 oS u1 k2 T2 u2 k3 T3 u3 Ss nrm")
        ma = Steps(sem("mlstm_act"), "so1 so2 so3 kw0 kw1 kw2 d1 d2 emt v0 v1 v2 ct0 ct1 abs hi cp")
        md_ = Steps(sem("mlstm_dve"), "so sel k v D0 D1 D2 qw prs pt1 pt2 C0 pr1 C1 pr2 C2 pr3 C3 np ns ns2 mx rc h ho cs1 cs2 lo")
        mp = Steps(sem("mlstm_pool"), "km cs")
        mt = Steps(sem("mlstm_pe"), "rows ktr vtr kq c0 u0 c1 u1 u2 u3 ns so C cp")
        gate_a = Steps(sem("gates_act"), "expA abs exp ln beta er wi emt fw sw")
        gate_d = Steps(sem("gates_dve"), "ga gb mf mi sp g lf "
                       + " ".join(f"s{k}a s{k}b s{k}c" + (f" s{k}d" if k < 2 else "") for k in range(6)) + " G gl1 gl2 c "
                       + " ".join(f"x{k}a x{k}b x{k}c" + (f" x{k}d" if k < 2 else "") for k in range(6))
                       + " bl1 bl2 cl1 cl2 emc z0 m0 n0 m1 n1 m2 n2 m3 ms1 ms2 mm1 mm2 negmx wi1 wi2 emt fw1 fw2"
                       " sw0 sw1 sw2 colsA colsB nbA nbB")
        gate_t = Steps(sem("gates_pe"), "cols")
        lst_p = Steps(sem("last_pool"), "a b")
        lst_t = Steps(sem("last_pe"), "tr")
        lst_a = Steps(sem("last_act"), "r0 r1 r2")
        no_t, no_a = Steps(sem("n_pe"), "tr"), Steps(sem("n_act"), "s p")
        br_a = Steps(sem("branch_act"), "sa0 sa1 sb0 sb1 hi0 hi1 sa2 sa3 sb2 sb3 hi2 hi3")
        vt_ones, uu_zero = sem("vt_ones_set"), sem("u_pads_zero")
        br_d = Steps(sem("branch_dve"), "s0 s1 lo0 lo1 s2 s3 lo2 lo3")
        ot_t = Steps(sem("out_pe"), "x0 x1 x2 x3")
        ot_a = Steps(sem("out_act"), "x0 x1 x2 x3 hi0 hi1 hi2 hi3")
        ot_d = Steps(sem("out_dve"), "lo0 lo1 lo2 lo3")
        ot_p = Steps(sem("out_pool"), "s0 a0 s1 a1 s2 a2 s3 a3")
        n2_t, n2_a = Steps(sem("norm2_pe"), "w sum"), Steps(sem("norm2_act"), "ln exp")
        n2_d = Steps(sem("norm2_dve"), "w")
        up_t = Steps(sem("up_pe"), "old0 old1")
        up_d = Steps(sem("up_dve"), "og " + " ".join(f"g{m} gc{m}a gc{m}b" for m in range(4)) + " ov "
                     + " ".join(f"v{m} vc{m}a vc{m}b ac{m}a ac{m}b lo{m}" for m in range(4)))
        up_a = Steps(sem("up_act"), " ".join(f"g{m} sg{m}" for m in range(4)) + " "
                     + " ".join(f"v{m} hi{m}" for m in range(4)))
        up_p = Steps(sem("up_pool"), "g1 g2 v1 v2")
        dn_p = Steps(sem("down_pool"), "sel")
        dn_t = Steps(sem("down_pe"), "tr")
        dn_a = Steps(sem("down_act"), "r0 r1")
        fin_p = Steps(sem("final_pool"), "sq add")
        y_t, y_a = Steps(sem("y_pe"), "sum t0 t1 t2 t3"), Steps(sem("y_act"), "ln exp r0 r1 r2 r3")
        y_d = Steps(sem("y_dve"), " ".join(f"y{f}" for f in range(KT)))

        def seqs(ap, step, lo, hi):
            return ap.rearrange("p (b s) -> p b s", s=step)[:, :, lo:hi]

        def seqs3(ap, step, lo, hi):
            return ap.rearrange("p t (b s) -> p t b s", s=step)[:, :, :, lo:hi]

        def spaced(ap, step):
            return bass.AP(tensor=ap.tensor, offset=ap.offset, ap=list(ap.ap)[:-1] + [[step, NB], [1, L]])

        def one(t, i):
            return t[:, bass.ds(i, 1)].rearrange("p a t -> p (a t)")

        def apart(eng):
            eng.nop(nofuse=True)

        def freed(g, m):
            return bank_free, 4 * g + (m + 5)

        block = ctx.enter_context(nc.Block())

        @block.sync
        def _(sp):
            def unit(src, k, nk, n, q, s, first=False):
                if not first:
                    sp.wait_ge(lo_ready, 16 * q + 4 * s - 12)
                sp.dma_start(raw[:, s, 0:nk], src[:, k:k + nk, bass.ds(n, P)]).then_inc(landed[s], 16)

            def quad(src, n, q, k=0, first=False):
                for s in range(4):
                    unit(src, k, KT, n + s * P, q, s, first)

            sp.dma_start(x_rows[:, 0:2], xp_rows).then_inc(x_in, 16)
            sp.dma_start(x_rows[0:TS, 2], xs_rows).then_inc(x_in, 16)
            quad(w_in, 0, 0, first=True)
            with sp.Fori(1, 8) as i:
                quad(w_in, NG * i, i)
            with sp.Fori(0, 6) as i:
                quad(w_in, NG * i + c_mqkv, i + q_heads)
            with sp.Fori(0, 2) as i:
                quad(w_in, NG * i + c_mo, i + (q_heads + 6))
            with sp.Fori(0, 8) as i:
                quad(w_in, NG * i + c_gate, i + q_gate)
            with sp.Fori(0, 4) as i:
                for s in range(4):
                    sp.wait_ge(lo_ready, 16 * (i + q_branch) + (4 * s - 12))
                    sp.dma_start(raw[:, s].rearrange("p (k c) n -> p k (c n)", c=2),
                                 (w_ba, w_bb)[s % 2][:, :, bass.ds(NG * i + 2 * P * (s // 2), 2 * P)]).then_inc(landed[s], 16)

            def x_group(i):
                sp.dma_start(xg[:, 0:2], xp_rows[:, :, bass.ds(i * NG, NG)]).then_inc(x_in2, 16)
                sp.dma_start(xg[0:TS, 2], xs_rows[:, bass.ds(i * NG, NG)]).then_inc(x_in2, 16)

            sp.wait_ge(*md_.before(H))
            sp.wait_ge(cs_out, 32 * H)
            sp.wait_ge(*mt.before(H))
            sp.wait_ge(*ma.before(H))
            sp.dma_start(fw_rows[:], a["ffn_conv_w"][0].rearrange("j (t p) -> t j p", p=P)).then_inc(fw_in, 16)
            with sp.Fori(0, 4) as i:
                sp.wait_ge(*ot_t.before(i))
                x_group(i)
                quad(w_out, NG * i, i + q_out)
            q, first_group = q_ffn, 0
            old = a["state_ffn_conv"][0].rearrange("b j n -> (b j) n")
            for c, n in enumerate(CHUNKS):
                with sp.Fori(0, n) as i:
                    for half in range(2):
                        n0 = (i + first_group) * NG + half * FT * P
                        sp.wait_ge(*up_t.before(i + first_group))
                        sp.dma_start(st_rows[:, half], old[:, bass.ds(n0, NG)]).then_inc(old_in, 16)
                        quad(w_up, n0, 2 * i + q + half)
                q += 2 * n
                if n == 4:
                    with sp.Fori(0, 4) as i:
                        quad(w_down, NG * i, i + q, 4 * first_group)
                else:
                    for u in range(KT):
                        sp.wait_ge(lo_ready, 16 * q + (4 * u - 12 if u < 4 else n * (u - 3)))
                        sp.dma_start(raw[:, u % 4, 0:4 * n], w_down[:, 4 * first_group:4 * (first_group + n), u * P:(u + 1) * P])\
                            .then_inc(landed[u % 4], 16)
                q += n
                first_group += n
            sp.wait_ge(stored, 16 * N_STORED)
            sp.wait_ge(ss_out, 32 * H)
            sp.wait_ge(cs_out, 32 * H)
            sp.wait_ge(lrow_out, 16 * N_LROW)
            sp.wait_ge(y_out, 16 * 8)

        @block.gpsimd
        def _(pool):
            made = [0]

            def done(instruction):
                made[0] += 1
                instruction.then_inc(consts, 1)
                pool.wait_ge(consts, made[0])

            def keep(t, pattern, base, channel, fill=0.0, op=ALU.is_ge):
                done(pool.affine_select(out=t, in_=t, compare_op=op, fill=fill, base=base,
                                        pattern=pattern, channel_multiplier=channel))

            done(pool.memset(eps[:], EPS))
            done(pool.memset(sm_raw[:], 0.0))
            pool.dma_start(sm_raw[:, :, 0:H], w_in[:, :, c_ga:c_ga + H]).then_inc(small_in, 16)
            pool.dma_start(sm_raw[:, :, 32:32 + H], w_in[:, :, c_gb:c_gb + H]).then_inc(small_in, 16)
            pool.dma_start(sm_raw[:, :, 64:64 + H], w_in[:, :, c_mi:c_mi + H]).then_inc(small_in, 16)
            pool.dma_start(sm_raw[:, :, 96:96 + H], w_in[:, :, c_mf:c_mf + H]).then_inc(small_in, 16)
            done(pool.memset(ident[:], 0.0))
            keep(ident[:], [[-1, P]], 0, 1, 1.0, ALU.not_equal)
            done(pool.memset(ones[:], 1.0))
            done(pool.memset(gq[:, :, 0:GPAD], 0.0))
            for m, n, b in ((incl, P, CH), (incl_s, TS, L)):
                done(pool.memset(m[:], 0.0))
                keep(m[:], [[1, n]], 0, -1, NEG)
                view = m[:].rearrange("j (b t) -> j b t", t=b)
                keep(view, [[-b, n // b], [0, b]], 0, 1, NEG)
            for k in range(NLEV):
                s = 1 << k
                done(pool.memset(lev[:, k], 0.0))
                half = lev[:, k].rearrange("j (b h t) -> j b h t", h=2, t=s)[:, :, 1]
                done(pool.memset(half, 1.0))
                keep(half, [[-2 * s, P // (2 * s)], [0, s]], 0, 1)
                keep(half, [[2 * s, P // (2 * s)], [0, s]], s - 1, -1)
            done(pool.memset(seq[:], 1.0))
            keep(seq[:], [[-L, NB]], 0, 1)
            keep(seq[:], [[L, NB]], L - 1, -1)
            assert made[0] == N_CONST

            pool.wait_ge(*freed(5, 3))
            pool.wait_ge(*gate_d.after("nbB"))
            pool.wait_ge(stored, 32)
            with pool.Fori(0, 2) as i:
                pool.wait_ge(*lst_t.before(i))
                pool.tensor_copy(g_last[:, :, 0:GPAD], gq[:, bass.ds(i * 12, 12), TP:TP + GPAD]).then_inc(*lst_p.done("a"))
                pool.tensor_copy(g_last[:, :, GPAD:].rearrange("p t (b s) -> p t b s", s=GPAD),
                                 seqs3(gq[:, bass.ds(i * 12, 12), GPAD + TP:], GS, L, GS)).then_inc(*lst_p.done("b"))

            with pool.Fori(0, H) as i:
                pool.wait_ge(*gd.after(f"cv2{GC - 1}", i))
                pool.wait_ge(*ga.before(i))
                apart(pool)
                pool.tensor_scalar(sg[:, 0:3 * GV], cv[:], SIG_MIN, None, ALU.max).then_inc(*gp.done("clamp"))
                z_t = one(zm, i + 3 * H)
                pool.wait_ge(*ga.after("sg3", i))
                apart(pool)
                pool.tensor_tensor(zz[:], z_t, sg[:, 3 * GV:], ALU.mult).then_inc(*gp.done("zz"))
                pool.wait_ge(*gd.after("qkv2", i))
                pool.wait_ge(*gp.after("zz", i))
                pool.tensor_tensor(sq[:], qkv[:, 0:2], qkv[:, 0:2], ALU.mult).then_inc(*gp.done("sq"))
                pool.wait_ge(*ga.after("vn_s", i))
                pool.tensor_tensor(vnm[:], vn_s[:].unsqueeze(1).to_broadcast([TS, NB, P]),
                                   seq[:].unsqueeze(2).to_broadcast([TS, NB, P]), ALU.mult).then_inc(*gp.done("vnm"))
                pool.wait_ge(*gt.after("oS", i))
                g_end = seqs(eg[:, TP:T], L, L - 1, L)
                pool.tensor_tensor(ss[:], ss[:], g_end.to_broadcast([P, NB, P]), ALU.mult).then_inc(*gp.done("sse"))
                pool.wait_ge(*gd.after("go", i))
                pool.tensor_tensor(gout[:], gout[:], zz[:], ALU.mult).then_inc(*gp.done("goz"))

            with pool.Fori(0, H) as i:
                pool.wait_ge(*mt.after("so", i))
                pool.tensor_tensor(km[:], kw[0:TS, 2].unsqueeze(1).to_broadcast([TS, NB, P]),
                                   seq[:].unsqueeze(2).to_broadcast([TS, NB, P]), ALU.mult).then_inc(*mp.done("km"))
                pool.tensor_tensor(cs[:], cs[:], emt[:, T + NCH:].unsqueeze(2).to_broadcast([P, NB, P]),
                                   ALU.mult).then_inc(*mp.done("cs"))

            pool.wait_ge(*md_.before(H))
            pool.wait_ge(*mt.before(H))
            pool.wait_ge(cs_out, 32 * H)
            pool.memset(ssq[:], 0.0).then_inc(consts, 1)
            pool.wait_ge(consts, N_CONST + 1)

            def add_square(steps, tile, r, names, y_done):
                pool.wait_ge(*y_done)
                t = x2[:, tile].rearrange("p a t -> p (a t)")
                pool.tensor_tensor(sqt[:], t, t, ALU.mult).then_inc(*steps.done(names[0]))
                pool.wait_ge(*steps.after(names[0], r))
                pool.tensor_tensor(ssq[:], ssq[:], sqt[:], ALU.add).then_inc(*steps.done(names[1]))
                pool.wait_ge(*steps.after(names[1], r))

            with pool.Fori(0, 4) as i:
                for m in range(4):
                    add_square(ot_p, bass.ds(4 * i + m, 1), i, (f"s{m}", f"a{m}"), freed(i + g_out, m))
            g, g0 = g_ffn, 0
            for c, n in enumerate(CHUNKS):
                with pool.Fori(0, n) as i:
                    r = i + g0
                    pool.wait_ge(*dn_t.before(4 * c))
                    for half, name in enumerate("gv"):
                        pool.wait_ge(*freed(2 * i + (g + half), 3))
                        u_t = u_last[:, bass.ds(8 * i + 4 * half, 4)]
                        pool.tensor_copy(u_t[:, :, 0:FPAD], uu[:, :, TP:TP + FPAD]).then_inc(*up_p.done(f"{name}1"))
                        pool.tensor_copy(u_t[:, :, FPAD:].rearrange("p t (b s) -> p t b s", s=FPAD),
                                         seqs3(uu[:, :, FPAD + TP:], FS, L, FS)).then_inc(*up_p.done(f"{name}2"))
                g, g0 = g + 2 * n, g0 + n
                if c == 0:
                    pool.wait_ge(*n2_t.after("sum"))
                    pool.memset(ssq[:], 0.0).then_inc(consts, 1)
                    pool.wait_ge(consts, N_CONST + 2)
                if n == 4:
                    with pool.Fori(0, 4) as i:
                        pool.wait_ge(*up_p.before(g0))
                        pool.wait_ge(*dn_t.before(i + 4 * c))
                        pool.tensor_copy(u_out[:], u_last[:, bass.ds(8 * i, 8)]).then_inc(*dn_p.done("sel"))
                    g += 4
                else:
                    for i in range(4):
                        if i < n:
                            pool.wait_ge(*up_p.before(g0))
                            pool.wait_ge(*dn_t.before(i + 4 * c))
                            pool.tensor_copy(u_out[:], u_last[:, 8 * i:8 * i + 8]).then_inc(*dn_p.done("sel"))
                        for m in range(4):
                            add_square(fin_p, bass.ds(4 * i + m, 1), 4 * i + m, ("sq", "add"), freed(g + i, m))

        TAIL = CHUNKS[-1]

        def ring_slot(first, second, n, ring):
            n %= ring
            return first[:, n] if n < 4 else second[:, n - 4]

        def where(n, tail, tail_next):
            if tail:
                return n // TAIL // 4, n // TAIL % 4, n % TAIL
            if tail_next and n >= 16:
                dq, s, j = where(n - 16, True, False)
                return dq + 1, s, j
            return n // 16, n % 16 // 4, n % 4

        def split_hi(q, n, ring, tail=False, tail_next=False):
            if tail and n >= KT * TAIL:
                return
            dq, s, j = where(n, tail, tail_next)
            nc.scalar.wait_ge(landed[s], 16 * (q + dq + 1))
            nc.scalar.wait_ge(blocks, 16 * q + (n - ring + 1))
            nc.scalar.activation(ring_slot(whi, whi2, n, ring), raw[:, s, 4 * j:4 * j + 4], ACT.Copy).then_inc(hi_ready, 1)

        def split_lo(q, n, ring, tail=False, tail_next=False):
            if tail and n >= KT * TAIL:
                return
            dq, s, j = where(n, tail, tail_next)
            nc.vector.wait_ge(hi_ready, 16 * q + (n + 1))
            nc.vector.tensor_tensor(ring_slot(wlo, wlo2, n, ring), raw[:, s, 4 * j:4 * j + 4],
                                    ring_slot(whi, whi2, n, ring).bitcast(F32), ALU.subtract).then_inc(lo_ready, 1)

        def group(split, q, points=(), mixer=None, stages=0, ring=4, b0=0, n=16, **tail):
            for b in range(n):
                split(q, b0 + b + ring - 1, ring, **tail)
                for at, work in points:
                    if min(at + 1, n - 1) == b:
                        work()
                for _ in range((b + 1) * stages // n - b * stages // n):
                    next(mixer, None)
            for _ in mixer or ():
                pass

        def nothing(m, done):
            pass

        def repeat(eng, n, body, peel):
            with eng.Fori(0, n - 1 if peel else n) as i:
                body(i, False)
            if peel:
                body(n - 1, True)

        def column_tiles(*works, n=4):
            return [(n * m + n - 1 + k, lambda m=m, w=w: w(m, n * (m + 1))) for m in range(4) for k, w in enumerate(works)]

        @block.scalar
        def _(act):
            nc.scalar.preload_act_table_set(EXP_LN)
            act.dma_start(norm_rows[0:KT], a["norm_mix_w"][0].rearrange("(k p) -> k p", p=P)).then_inc(rows_in, 16)
            act.dma_start(norm_rows[KT:2 * KT], a["norm_ffn_w"][0].rearrange("(k p) -> k p", p=P)).then_inc(rows_in, 16)
            act.dma_start(norm_rows[2 * KT:3 * KT], a["norm_final_w"][0].rearrange("(k p) -> k p", p=P)).then_inc(rows_in, 16)
            act.dma_start(w_rows[:], a["gdn_conv_w"][0].rearrange("j (t p) -> (j t) p", p=P)).then_inc(rows_in, 16)
            act.dma_start(n_rows[:], a["state_ml_n"][0].rearrange("b h k -> (b h) k")).then_inc(rows_in, 16)
            act.dma_start(conv_rows[:], a["state_gdn_conv"][0].rearrange("b j n -> (b j) n")).then_inc(rows_in, 16)
            act.dma_start(wgn[:], a["gdn_norm_w"].rearrange("a p -> p a")).then_inc(rows_in, 16)

            act.wait_ge(x_in, 32)
            act.wait_ge(consts, 1)
            for c, (n, name) in enumerate(((P, "sq0"), (P, "sq1"), (TS, "sq2"))):
                squares = (h_hi, h_lo)[c // 2][0:n].rearrange("p k t -> p (k t)")
                nc.scalar.activation(squares[:, c % 2 * D:(c % 2 + 1) * D], x_rows[0:n, c], ACT.Square,
                                     accum_out=rstd[0:n, c:c + 1]).then_inc(*st_a.done(name))
            for name, src, n, cc in (("lnp", "sq1", P, slice(0, 2)), ("lns", "sq2", TS, slice(2, 3))):
                act.wait_ge(*st_a.after(src))
                nc.scalar.activation(rstd[0:n, cc], rstd[0:n, cc], ACT.Ln, bias=eps[0:n], scale=1.0 / D)\
                    .then_inc(*st_a.done(name))
            for name, src, n, cc in (("expp", "lnp", P, slice(0, 2)), ("exps", "lns", TS, slice(2, 3))):
                act.wait_ge(*st_a.after(src))
                nc.scalar.activation(rstd[0:n, cc], rstd[0:n, cc], ACT.Exp, scale=-0.5).then_inc(*st_a.done(name))
            act.wait_ge(small_in, 64)
            nc.scalar.activation(sm_hi[:], sm_raw[:], ACT.Copy).then_inc(*st_a.done("smhi"))
            act.wait_ge(*st_d.after("nw"))
            for f in range(KT):
                act.wait_ge(*st_t.after(f"x{f}"))
                nc.scalar.activation(h_hi[:, f], ps[:, f % 4, 0:T], ACT.Copy, scale=wn[:, 0, f:f + 1])\
                    .then_inc(*st_a.done(f"hi{f}"))

            for b in range(3):
                act.wait_ge(landed[0], 16)
                nc.scalar.activation(whi[:, b], raw[:, 0, 4 * b:4 * b + 4], ACT.Copy).then_inc(hi_ready, 1)

            act.wait_ge(*st_t.after("small"))
            act.dma_start(hcol[:, 0:1], a["gdn_A_log"].rearrange("a h -> h a")).then_inc(rows_in, 16)
            act.dma_start(hcol[:, 1:2], a["gdn_dt_bias"].rearrange("a h -> h a")).then_inc(rows_in, 16)
            act.dma_start(hcol[:, 2:3], a["ml_b_i"].rearrange("a h -> h a")).then_inc(rows_in, 16)
            act.dma_start(hcol[:, 3:4], a["ml_b_f"].rearrange("a h -> h a")).then_inc(rows_in, 16)
            act.dma_start(m_in[:, NCH:], a["state_ml_m"][0].rearrange("b h -> h b"), allow_slow_non_contiguous=True).then_inc(rows_in, 16)
            act.wait_ge(rows_in, 16 * 12)
            nc.scalar.activation(hcol[:, 4:5], hcol[:, 0:1], ACT.Exp).then_inc(*gate_a.done("expA"))
            act.wait_ge(*gate_d.after("mf"))
            nc.scalar.activation(sp_out[:], sp_in[:], ACT.Abs).then_inc(*gate_a.done("abs"))
            act.wait_ge(*gate_a.after("abs"))
            nc.scalar.activation(sp_out[:], sp_out[:], ACT.Exp, scale=-1.0).then_inc(*gate_a.done("exp"))
            act.wait_ge(*gate_a.after("exp"))
            nc.scalar.activation(sp_out[:], sp_out[:], ACT.Ln, bias=1.0).then_inc(*gate_a.done("ln"))
            act.wait_ge(*gate_d.after("sp"))
            nc.scalar.activation(g_row[:, 1], sp_out[:, 1], ACT.Exp, scale=-1.0).then_inc(*gate_a.done("beta"))
            act.wait_ge(*gate_d.after("gl2"))
            nc.scalar.activation(e_row[:], e_row[:], ACT.Exp).then_inc(*gate_a.done("er"))
            act.wait_ge(*gate_d.after("wi2"))
            nc.scalar.activation(m_row[:, T:2 * T], sw_row[:], ACT.Exp).then_inc(*gate_a.done("wi"))
            act.wait_ge(*gate_d.after("emt"))
            nc.scalar.activation(m_row[:, 2 * T:3 * T], ig[:], ACT.Exp, scale=-1.0).then_inc(*gate_a.done("emt"))
            act.wait_ge(*gate_d.after("fw2"))
            nc.scalar.activation(m_row[:, 3 * T:], f_row[:], ACT.Exp).then_inc(*gate_a.done("fw"))
            act.wait_ge(*gate_d.after("sw2"))
            nc.scalar.activation(cmx[0][:], cmx[0][:], ACT.Exp).then_inc(*gate_a.done("sw"))
            act.dma_start(o["p_m"].rearrange("a b h -> h (a b)"), m_new[:, NCH - 1:NCH]).then_inc(stored, 16)
            act.dma_start(o["s_m"][0].rearrange("b h -> h b"), m_new[:, NCH:], allow_slow_non_contiguous=True).then_inc(stored, 16)

            with act.Fori(0, 6) as i:
                def evacuate(m, done):
                    act.wait_ge(blocks, 16 * (i) + done)
                    t = one(gq, 4 * i + m)
                    nc.scalar.activation(t[:, GPAD:GPAD + TP], ps[:, m, 0:TP], ACT.Copy)
                    nc.scalar.activation(seqs(t[:, GPAD + TP:], GS, GPAD, GS),
                                         ps[:, m, TP:T].rearrange("p (b s) -> p b s", s=L), ACT.Copy).then_inc(bank_free, 1)
                group(split_hi, i, column_tiles(evacuate))

            def last_rows(i):
                act.wait_ge(*lst_t.after("tr", i))
                act.wait_ge(lrow_out, 32 * i)
                for b in range(3):
                    nc.scalar.activation(g_lrow[:, b], pm[0:GPAD * (1 + NB), b], ACT.Copy).then_inc(*lst_a.done(f"r{b}"))
                act.wait_ge(*lst_a.after("r2", i))
                n = 3 * NG
                act.dma_start(o["p_gconv"][0, 0][:, bass.ds(i * n, n)],
                              g_lrow[0:GPAD].rearrange("r b n -> r (b n)")).then_inc(lrow_out, 16)
                act.dma_start(o["s_gconv"][0].rearrange("b j n -> (b j) n")[:, bass.ds(i * n, n)],
                              g_lrow[GPAD:].rearrange("r b n -> r (b n)")).then_inc(lrow_out, 16)
                yield 0

            with act.Fori(0, 2) as i:
                def evacuate(m, done):
                    act.wait_ge(blocks, 16 * (i + q_z) + done)
                    nc.scalar.activation(one(zm, 4 * i + (m + 3 * H)), ps[:, m, 0:T], ACT.Copy).then_inc(bank_free, 1)
                group(split_hi, i + q_z, column_tiles(evacuate), last_rows(i), 0)

            def gdn(i):
                act.wait_ge(lrow_out, 64)
                act.wait_ge(ss_out, 32 * i)
                act.wait_ge(*gd.before(i))
                act.wait_ge(*gp.before(i))
                act.wait_ge(*gt.before(i))
                act.dma_start(ss[:], a["state_gdn_S"][0][:, bass.ds(i, 1)].rearrange("b a k v -> k (b a) v")).then_inc(ss_in, 16)
                for t in range(3):
                    nc.scalar.activation(cv[:, t * GV:(t + 1) * GV], one(gq, i + t * H)[:, 0:GV], ACT.Copy,
                                         scale=gcw[:, 0, bass.ds(i + t * H, 1)]).then_inc(*ga.done(f"c{t}"))
                yield 0
                act.wait_ge(*gd.after("clampz", i))
                act.wait_ge(*gp.after("clamp", i))
                nc.scalar.activation(sg[:], sg[:], ACT.Exp, scale=-1.0).then_inc(*ga.done("sg1"))
                act.wait_ge(*ga.after("sg1", i))
                nc.scalar.activation(sg[:], sg[:], ACT.Ln, bias=1.0).then_inc(*ga.done("sg2"))
                act.wait_ge(*ga.after("sg2", i))
                nc.scalar.activation(sg[:], sg[:], ACT.Exp, scale=-1.0).then_inc(*ga.done("sg3"))
                yield 1
                yield 2
                act.wait_ge(*gt.after("norm", i))
                act.wait_ge(*gp.after("sq", i))
                nc.scalar.activation(rn[:], pm[:, 0:2, 0:T], ACT.Ln, bias=eps[:]).then_inc(*ga.done("rn1"))
                act.wait_ge(*ga.after("rn1", i))
                nc.scalar.activation(rn[:], rn[:], ACT.Exp, scale=-0.5).then_inc(*ga.done("rn2"))
                nc.scalar.activation(eg[:], pm[:, 2, 0:T], ACT.Exp).then_inc(*ga.done("eg"))
                act.wait_ge(*gd.after("d2", i))
                nc.scalar.activation(dec[:, 0:TP], dec[:, 0:TP], ACT.Exp).then_inc(*ga.done("d1"))
                nc.scalar.activation(dec[0:TS, TP:T], dec[0:TS, TP:T], ACT.Exp).then_inc(*ga.done("d2"))
                yield 3
                act.wait_ge(*gt.after("tr", i))
                for n, _, c in PARTS:
                    nc.scalar.activation(kg[0:n, c], pm[0:n, 0, c * P:(c + 1) * P], ACT.Copy,
                                         scale=cols[0:n, 2, c, bass.ds(i, 1)]).then_inc(*ga.done(f"kg{c}"))
                yield 4
                yield 5
                act.wait_ge(*gt.after("x0", i))
                nc.scalar.activation(xx[:, 0, 0:TP], pm[:, 1, 0:TP], ACT.Copy).then_inc(*ga.done("x0a"))
                nc.scalar.activation(xx[0:TS, 0, TP:T], pm[0:TS, 1, TP:T], ACT.Copy).then_inc(*ga.done("x0b"))
                yield 6
                for l in LEVELS:
                    act.wait_ge(*gt.after(f"p{l}", i))
                    if l == 1:
                        nc.scalar.activation(psb[0:TS, TP:T], pm[0:TS, 3, TP:T], ACT.Copy).then_inc(*ga.done("psb1s"))
                    nc.scalar.activation(psb[:, 0:TP], pm[:, 3, 0:TP], ACT.Copy).then_inc(*ga.done(f"psb{l}"))
                    yield 2 * l + 5
                    yield 2 * l + 6

                def v_new(n):
                    lo = CH * (n % 2)
                    act.wait_ge(*gt.after(f"T{n}", i))
                    nc.scalar.activation(vn[lo:lo + CH], pm[lo:lo + CH, 2, 0:P], ACT.Copy).then_inc(*ga.done(f"vn{n}"))

                v_new(0)
                act.wait_ge(*gt.after("ksS", i))
                nc.scalar.activation(ks_s[:], pm[:, 1, 0:TS], ACT.Copy).then_inc(*ga.done("ks_s"))
                yield 17
                yield 18
                act.wait_ge(*gt.after("TS", i))
                nc.scalar.activation(vn_s[:], pm[0:TS, 1, 2 * P:3 * P], ACT.Copy).then_inc(*ga.done("vn_s"))
                yield 19
                v_new(1)
                yield 20
                yield 21
                yield 22
                v_new(2)
                yield 23
                yield 24
                yield 25
                v_new(3)
                yield 26
                act.wait_ge(*gt.after("u3", i))
                nc.scalar.activation(sqo[:], pm[:, 0, 0:T], ACT.Square).then_inc(*ga.done("sqo"))
                yield 27
                act.wait_ge(*gt.after("nrm", i))
                nc.scalar.activation(rso[:], pm[:, 1, 0:T], ACT.Ln, bias=eps[:], scale=1.0 / P).then_inc(*ga.done("rs1"))
                act.wait_ge(*ga.after("rs1", i))
                nc.scalar.activation(rso[:], rso[:], ACT.Exp, scale=-0.5).then_inc(*ga.done("rs2"))
                act.wait_ge(*gp.after("goz", i))
                nc.scalar.activation(one(go_hi, i), gout[:], ACT.Copy).then_inc(*ga.done("hi"))
                act.wait_ge(*gd.after("ss", i))
                act.dma_start(o["p_S"][0, 0][bass.ds(i, 1)].rearrange("a k v -> k (a v)"), S[:]).then_inc(ss_out, 16)
                act.dma_start(o["s_S"][0][:, bass.ds(i, 1)].rearrange("b a k v -> k (b a) v"), ss[:]).then_inc(ss_out, 16)

            with act.Fori(0, H) as i:
                def evacuate(m, done):
                    act.wait_ge(blocks, 16 * (i + q_heads) + done)
                    act.wait_ge(*gp.after("zz", i))
                    nc.scalar.activation(one(zm, 4 * i + m), ps[:, m, 0:T], ACT.Copy).then_inc(bank_free, 1)
                group(split_hi, i + q_heads, column_tiles(evacuate), gdn(i), GDN_STAGES)

            def mlstm(i):
                act.wait_ge(cs_out, 32 * i)
                act.wait_ge(ss_out, 32 * H)
                act.wait_ge(*md_.before(i))
                act.wait_ge(*mp.before(i))
                act.wait_ge(*mt.before(i))
                act.dma_start(cs[:], a["state_ml_C"][0][:, bass.ds(i, 1)].rearrange("b a v k -> v (b a) k")).then_inc(cs_in, 16)
                act.wait_ge(*md_.after("so", i))
                nc.scalar.activation(so[:], so[:], ACT.Exp, scale=-1.0).then_inc(*ma.done("so1"))
                act.wait_ge(*ma.after("so1", i))
                nc.scalar.activation(so[:], so[:], ACT.Ln, bias=1.0).then_inc(*ma.done("so2"))
                act.wait_ge(*ma.after("so2", i))
                nc.scalar.activation(so[:], so[:], ACT.Exp, scale=-1.0).then_inc(*ma.done("so3"))
                yield 0
                act.wait_ge(*mt.after("ktr", i))
                for n, _, c in PARTS:
                    nc.scalar.activation(kw[0:n, c], pm[0:n, 3, c * P:(c + 1) * P], ACT.Copy,
                                         scale=cols[0:n, 4, c, bass.ds(i, 1)]).then_inc(*ma.done(f"kw{c}"))
                act.wait_ge(*md_.after("D2", i))
                nc.scalar.activation(md[:, 0:TP], md[:, 0:TP], ACT.Exp).then_inc(*ma.done("d1"))
                nc.scalar.activation(md[0:TS, TP:T], md[0:TS, TP:T], ACT.Exp).then_inc(*ma.done("d2"))
                nc.scalar.activation(emt[:], pm[:, 2, 0:T + NC], ACT.Copy).then_inc(*ma.done("emt"))
                yield 1
                act.wait_ge(*mt.after("vtr", i))
                for n, _, c in PARTS:
                    nc.scalar.activation(vt[0:n, c, 0:P], pm[0:n, 3, c * P:(c + 1) * P], ACT.Copy).then_inc(*ma.done(f"v{c}"))
                yield 2
                for half in range(2):
                    act.wait_ge(*mt.after(f"c{half}", i))
                    nc.scalar.activation(cts[:, 4 * half:4 * half + 4].rearrange("p b k -> p (b k)"), pm[:, 0],
                                         ACT.Copy).then_inc(*ma.done(f"ct{half}"))
                    yield 3 + half
                yield 5
                yield 6
                act.wait_ge(*mt.after("so", i))
                nc.scalar.activation(dn[:], pm[:, 2, 0:T], ACT.Abs).then_inc(*ma.done("abs"))
                yield 7
                act.wait_ge(*md_.after("ho", i))
                nc.scalar.activation(one(mh_hi, i), mh[:], ACT.Copy).then_inc(*ma.done("hi"))
                act.wait_ge(*mt.after("cp", i))
                nc.scalar.activation(cout[:], pm[:, 1, 0:P], ACT.Copy).then_inc(*ma.done("cp"))
                act.wait_ge(*ma.after("cp", i))
                act.dma_start(o["p_C"][0, 0][bass.ds(i, 1)].rearrange("a v k -> v (a k)"), cout[:]).then_inc(cs_out, 16)
                act.wait_ge(*md_.after("cs2", i))
                act.dma_start(o["s_C"][0][:, bass.ds(i, 1)].rearrange("b a v k -> v (b a) k"), cs[:]).then_inc(cs_out, 16)

            with act.Fori(0, H) as i:
                def evacuate(m, done):
                    act.wait_ge(blocks, 16 * (i + q_gate) + done)
                    nc.scalar.activation(one(gates, 4 * i + m), ps[:, m, 0:T], ACT.Copy).then_inc(bank_free, 1)
                group(split_hi, i + q_gate, column_tiles(evacuate), mlstm(i), MLSTM_STAGES)

            act.wait_ge(*md_.before(H))
            act.wait_ge(*mp.before(H))
            act.wait_ge(cs_out, 32 * H)
            act.wait_ge(*no_t.after("tr"))
            nc.scalar.activation(n_out[0:NB * H, 0], pm[0:NB * H, 0, 0:P], ACT.Copy).then_inc(*no_a.done("s"))
            nc.scalar.activation(n_out[0:H, 1], pm[0:H, 1, 0:P], ACT.Copy).then_inc(*no_a.done("p"))
            act.wait_ge(*no_a.after("p"))
            act.dma_start(o["s_n"][0].rearrange("b h k -> (b h) k"), n_out[0:NB * H, 0]).then_inc(stored, 16)
            act.dma_start(o["p_n"][0, 0], n_out[0:H, 1]).then_inc(stored, 16)

            nc.scalar.preload_act_table(ACT.Sigmoid)
            with act.Fori(0, 4) as i:
                def sig(name, tile):
                    nc.scalar.activation(one(gates, tile), one(gates, tile), ACT.Sigmoid).then_inc(*br_a.done(name))

                def sigs(h):
                    for m in (2 * h, 2 * h + 1):
                        sig(f"sa{m}", 4 * i + m)
                    for m in (2 * h, 2 * h + 1):
                        sig(f"sb{m}", 4 * i + m + KT)

                def upper(h):
                    for m in (2 * h, 2 * h + 1):
                        act.wait_ge(*br_d.after(f"s{m}", i))
                        nc.scalar.activation(one(mix_hi, 4 * i + m), mix_b[:, m], ACT.Copy).then_inc(*br_a.done(f"hi{m}"))
                group(split_hi, i + q_branch, [(-1, lambda: sigs(0)), (9, lambda: upper(0)), (9, lambda: sigs(1)), (15, lambda: upper(1))])

            for n in range(3, 7):
                split_hi(q_out, n, 8)
            with act.Fori(0, 4) as i:
                def residual():
                    for k in range(4):
                        act.wait_ge(*ot_t.after(f"x{k}", i))
                        nc.scalar.activation(one(x2, 4 * i + k), pm[:, k, 0:T], ACT.Copy).then_inc(*ot_a.done(f"x{k}"))

                def evacuate(m, done):
                    act.wait_ge(*freed(i + g_out, m))
                    nc.scalar.activation(one(f_hi, 4 * i + m), one(x2, 4 * i + m), ACT.Copy,
                                         scale=wn[:, 1, bass.ds(4 * i + m, 1)]).then_inc(*ot_a.done(f"hi{m}"))
                group(split_hi, i + q_out, [(0, residual)] + column_tiles(evacuate), ring=8)
            nc.scalar.preload_act_table_set(EXP_LN)
            act.wait_ge(*n2_t.after("sum"))
            nc.scalar.activation(r2[:], pm[:, 0, 0:T], ACT.Ln, bias=eps[:], scale=1.0 / D).then_inc(*n2_a.done("ln"))
            act.wait_ge(*n2_a.after("ln"))
            nc.scalar.activation(r2[:], r2[:], ACT.Exp, scale=-0.5).then_inc(*n2_a.done("exp"))
            nc.scalar.preload_act_table(ACT.Silu)

            q, g, g0 = q_ffn, g_ffn, 0
            for c, n in enumerate(CHUNKS):
                def up(i, tail_next):
                    r = i + g0

                    def tap(dst, m, name, offset):
                        act.wait_ge(*freed(2 * i + (g + (offset > 0)), m))
                        nc.scalar.activation(dst[:, m], uu[:, m, 0:FV], ACT.Copy,
                                             scale=fcw[:, 0, bass.ds(4 * r + (m + offset), 1)]).then_inc(*up_a.done(f"{name}{m}"))

                    def gate_tap(m, done):
                        tap(ug, m, "g", 0)

                    def silu(m, done):
                        act.wait_ge(*up_d.after(f"gc{m}b", r))
                        nc.scalar.activation(ug[:, m], ug[:, m], ACT.Silu).then_inc(*up_a.done(f"sg{m}"))

                    def value_tap(m, done):
                        tap(uv, m, "v", FT)

                    def upper(m, done):
                        act.wait_ge(*up_d.after(f"ac{m}b", r))
                        nc.scalar.activation(one(u_hi, 4 * i + m), ac[:, m % 2], ACT.Copy).then_inc(*up_a.done(f"hi{m}"))
                    group(split_hi, 2 * i + q, column_tiles(gate_tap, silu), ring=8)
                    group(split_hi, 2 * i + (q + 1), column_tiles(value_tap, nothing, nothing, upper), ring=8, tail_next=tail_next)
                repeat(act, n, up, n == TAIL)
                q += 2 * n

                def last_rows_ffn(r, first):
                    act.wait_ge(*dn_t.after("tr", r))
                    act.wait_ge(lrow_out, 64 * r + 64)
                    for half in range(2):
                        nc.scalar.activation(u_lrow[:, half], pm[0:FPAD * (1 + NB), half], ACT.Copy).then_inc(*dn_a.done(f"r{half}"))
                    act.wait_ge(*dn_a.after("r1", r))
                    for half in range(2):
                        n0 = first * NG + half * FT * P
                        act.dma_start(o["p_fconv"][0, 0][:, bass.ds(n0, NG)], u_lrow[0:FPAD, half]).then_inc(lrow_out, 16)
                        act.dma_start(o["s_fconv"][0].rearrange("b j n -> (b j) n")[:, bass.ds(n0, NG)],
                                      u_lrow[FPAD:, half]).then_inc(lrow_out, 16)
                    yield 0

                if n == 4:
                    with act.Fori(0, 4) as i:
                        group(split_hi, i + q, (), last_rows_ffn(i + 4 * c, i + g0), 0, ring=8)
                else:
                    for i in range(4):
                        group(split_hi, q, (), last_rows_ffn(4 * c + i, g0 + i) if i < n else None, 0,
                              ring=8, b0=4 * n * i, n=4 * n, tail=True)
                q, g, g0 = q + n, g + 2 * n + 4, g0 + n

            nc.scalar.preload_act_table_set(EXP_LN)
            act.wait_ge(*y_t.after("sum"))
            nc.scalar.activation(r2[:], pm[:, 3, 0:T], ACT.Ln, bias=eps[:], scale=1.0 / D).then_inc(*y_a.done("ln"))
            act.wait_ge(*y_a.after("ln"))
            nc.scalar.activation(r2[:], r2[:], ACT.Exp, scale=-0.5).then_inc(*y_a.done("exp"))
            for g in range(4):
                act.wait_ge(*y_t.after(f"t{g}"))
                bank = (ps, pm)[g % 2]
                nc.scalar.activation(y_rows[:, 0:2, g * NG:(g + 1) * NG], bank[:, 0:2], ACT.Copy)
                nc.scalar.activation(y_rows[0:TS, 2, g * NG:(g + 1) * NG], bank[0:TS, 2], ACT.Copy).then_inc(*y_a.done(f"r{g}"))
                act.wait_ge(*y_a.after(f"r{g}"))
                act.dma_start(o["y_p"][0].rearrange("(c p) d -> p c d", p=P)[:, :, g * NG:(g + 1) * NG],
                              y_rows[:, 0:2, g * NG:(g + 1) * NG]).then_inc(y_out, 16)
                act.dma_start(o["y_s"].rearrange("b t d -> (b t) d")[:, g * NG:(g + 1) * NG],
                              y_rows[0:TS, 2, g * NG:(g + 1) * NG]).then_inc(y_out, 16)

        @block.vector
        def _(dve):
            def step(steps, name, r=0):
                dve.wait_ge(*steps.after(name, r))

            dve.wait_ge(consts, 1)
            for m in range(4):
                nc.vector.tensor_copy(n_p[:, m:m + 1], eps[:]).then_inc(bank_free, 1)

            dve.wait_ge(small_in, 64)
            dve.wait_ge(*st_a.after("expp"))
            for c in range(2):
                nc.vector.tensor_scalar(x_rows[:, c], x_rows[:, c], rstd[:, c:c + 1], None, ALU.mult).then_inc(*st_d.done(f"xs{c}"))
            dve.wait_ge(*st_a.after("exps"))
            nc.vector.tensor_scalar(x_rows[0:TS, 2], x_rows[0:TS, 2], rstd[0:TS, 2:3], None, ALU.mult).then_inc(*st_d.done("xs2"))
            dve.wait_ge(*st_a.after("smhi"))
            nc.vector.tensor_tensor(sm_lo[:], sm_raw[:], sm_hi[:].bitcast(F32), ALU.subtract).then_inc(*st_d.done("smlo"))
            dve.wait_ge(*st_t.after("consts"))
            nc.vector.tensor_copy(gcw[:].rearrange("p j t -> p (j t)"), pm[:, 0, 0:GC * 3 * H]).then_inc(*st_d.done("cw"))
            nc.vector.tensor_copy(wn[:].rearrange("p n k -> p (n k)"), pm[:, 0, 128:128 + 3 * KT]).then_inc(*st_d.done("nw"))
            nc.vector.tensor_copy(n_s[:].rearrange("p b h -> p (b h)"), pm[:, 0, 256:256 + NB * H]).then_inc(*st_d.done("ns"))
            dve.wait_ge(*st_t.after("old"))
            for b in range(3):
                nc.vector.tensor_copy(seqs3(gq[:, 8 * b:8 * b + 8, GPAD + TP:], GS, 0, GPAD),
                                      pm[:, b + 1, 0:8 * NB * GPAD].rearrange("p (t b s) -> p t b s", t=8, s=GPAD))\
                    .then_inc(*st_d.done(f"old{b}"))
            for f in range(KT):
                dve.wait_ge(*st_a.after(f"hi{f}"))
                nc.vector.scalar_tensor_tensor(h_lo[:, f], ps[:, f % 4, 0:T], wn[:, 0, f:f + 1], h_hi[:, f].bitcast(F32),
                                               ALU.mult, ALU.subtract).then_inc(*st_d.done(f"lo{f}"))

            for b in range(3):
                dve.wait_ge(hi_ready, b + 1)
                nc.vector.tensor_tensor(wlo[:, b], raw[:, 0, 4 * b:4 * b + 4], whi[:, b].bitcast(F32),
                                        ALU.subtract).then_inc(lo_ready, 1)

            def g(name, instruction):
                instruction.then_inc(*gate_d.done(name))
                step(gate_d, name)

            def chunked(ap):
                return ap[..., 0:TP].rearrange("h (n t) -> h n t", t=CH)

            def seqd(ap):
                return ap[..., TP:T].rearrange("h (b t) -> h b t", t=L)

            def chunked2(ap):
                return ap[:, :, 0:TP].rearrange("h r (n t) -> h r n t", t=CH)

            def seqd2(ap):
                return ap[:, :, TP:T].rearrange("h r (b t) -> h r b t", t=L)

            tt, tc, ts, stt = nc.vector.tensor_tensor, nc.vector.tensor_copy, nc.vector.tensor_scalar, nc.vector.scalar_tensor_tensor
            dve.wait_ge(rows_in, 16 * 12)
            dve.wait_ge(*st_t.after("small"))
            g("ga", ts(sp_in[:, 0], pm[0:H, 3, 0:T], hcol[:, 1:2], None, ALU.add))
            g("gb", ts(sp_in[:, 1], pm[32:32 + H, 3, 0:T], -1.0, None, ALU.mult))
            g("mf", ts(sp_in[:, 2], pm[96:96 + H, 3, 0:T], hcol[:, 3:4], -1.0, ALU.add, ALU.mult))
            g("mi", ts(ig[:], pm[64:64 + H, 3, 0:T], hcol[:, 2:3], None, ALU.add))
            dve.wait_ge(*gate_a.after("ln"))
            g("sp", stt(sp_out[:], sp_in[:], 0.0, sp_out[:], ALU.max, ALU.add))
            dve.wait_ge(*gate_a.after("expA"))
            g("g", ts(cum[0][:, 0], sp_out[:, 0], hcol[:, 4:5], -1.0, ALU.mult, ALU.mult))
            g("lf", ts(cum[0][:, 1], sp_out[:, 2], -1.0, None, ALU.mult))

            def doubling(tag, views, op):
                for k in range(NLEV):
                    (pa, sa), (pb, sb) = views(k)
                    s = 1 << k
                    g(f"{tag}{k}a", tt(pb[..., s:], pa[..., s:], pa[..., :-s], op))
                    g(f"{tag}{k}b", tc(pb[..., :s], pa[..., :s]))
                    if s < L:
                        g(f"{tag}{k}c", tt(sb[..., s:], sa[..., s:], sa[..., :-s], op))
                        g(f"{tag}{k}d", tc(sb[..., :s], sa[..., :s]))
                    else:
                        g(f"{tag}{k}c", tc(sb, sa))

            doubling("s", lambda k: [(chunked2(cum[j % 2][:]), seqd2(cum[j % 2][:])) for j in (k, k + 1)], ALU.add)
            G, b_ = cum[0][:, 0], cum[0][:, 1]
            g("G", tc(g_row[:, 0], G))
            g("gl1", tt(chunked(e_row[:]), chunked(G)[..., CH - 1:].to_broadcast([H, NCH, CH]), chunked(G), ALU.subtract))
            g("gl2", tt(seqd(e_row[:]), seqd(G)[..., L - 1:].to_broadcast([H, NB, L]), seqd(G), ALU.subtract))
            g("c", tt(c_row[:], ig[:], b_, ALU.subtract))
            doubling("x", lambda k: [(chunked(t[:]), seqd(t[:])) for t in
                                     ((c_row if k == 0 else cmx[(k + 1) % 2]), cmx[k % 2])], ALU.max)
            cm = cmx[1][:]
            one_col = lambda t: t.unsqueeze(2)
            g("bl1", tc(one_col(bl[:, 0:NCH]), chunked(b_)[..., CH - 1:]))
            g("bl2", tc(one_col(bl[:, NCH:]), seqd(b_)[..., L - 1:]))
            g("cl1", tc(one_col(cl[:, 0:NCH]), chunked(cm)[..., CH - 1:]))
            g("cl2", tc(one_col(cl[:, NCH:]), seqd(cm)[..., L - 1:]))
            g("emc", tt(cl[:], cl[:], bl[:], ALU.add))
            g("z0", nc.vector.memset(m_in[:, 0:1], 0.0))
            for n in range(NCH):
                g(f"m{n}", stt(m_new[:, n:n + 1], m_in[:, n:n + 1], bl[:, n:n + 1], cl[:, n:n + 1], ALU.add, ALU.max))
                if n + 1 < NCH:
                    g(f"n{n}", tc(m_in[:, n + 1:n + 2], m_new[:, n:n + 1]))
            g("ms1", tt(m_new[:, NCH:], m_in[:, NCH:], bl[:, NCH:], ALU.add))
            g("ms2", tt(m_new[:, NCH:], m_new[:, NCH:], cl[:, NCH:], ALU.max))
            at_chunk = lambda t: one_col(t[:, 0:NCH]).to_broadcast([H, NCH, CH])
            at_seq = lambda t: one_col(t[:, NCH:]).to_broadcast([H, NB, L])
            g("mm1", tt(chunked(mmx[:]), at_chunk(m_in), chunked(cm), ALU.max))
            g("mm2", tt(seqd(mmx[:]), at_seq(m_in), seqd(cm), ALU.max))
            g("negmx", ts(m_row[:, 0:T], mmx[:], -1.0, None, ALU.mult))
            g("wi1", tt(chunked(sw_row[:]), at_chunk(m_in), chunked(mmx[:]), ALU.subtract))
            g("wi2", tt(seqd(sw_row[:]), at_seq(m_in), seqd(mmx[:]), ALU.subtract))
            g("emt", tt(ig[:], b_, mmx[:], ALU.add))
            g("fw1", tt(f_row[:], bl[:], m_in[:], ALU.add))
            g("fw2", tt(f_row[:], f_row[:], m_new[:], ALU.subtract))
            g("sw0", tt(cl[:], bl[:], m_new[:], ALU.subtract))
            g("sw1", tt(chunked(cmx[0][:]), chunked(c_row[:]), at_chunk(cl), ALU.add))
            g("sw2", tt(seqd(cmx[0][:]), seqd(c_row[:]), at_seq(cl), ALU.add))
            dve.wait_ge(*gate_t.after("cols"))
            col_view = pm[:, 0, 0:15 * H].rearrange("p (q c h) -> p q c h", q=5, c=3)
            g("colsA", tc(cols[:, :, 0:2], col_view[:, :, 0:2]))
            g("colsB", tc(cols[0:TS, :, 2], col_view[0:TS, :, 2]))
            g("nbA", ts(nbeta[:, 0:2], cols[:, 1, 0:2], -1.0, None, ALU.mult))
            g("nbB", ts(nbeta[0:TS, 2], cols[0:TS, 1, 2], -1.0, None, ALU.mult))

            with dve.Fori(0, 8) as i:
                group(split_lo, i)

            def gdn(i):
                def d(name, instruction, then=True):
                    instruction.then_inc(*gd.done(name))
                    if then:
                        step(gd, name, i)
                hs = bass.ds(i, 1)
                dve.wait_ge(*ga.before(i))
                dve.wait_ge(*gt.before(i))
                dve.wait_ge(*gp.before(i))
                dve.wait_ge(*gate_a.after("sw"))
                dve.wait_ge(*freed(g_z + 1, 3))
                dve.wait_ge(lrow_out, 64)
                d("rsel", ts(rsel[:], g_row, ident[0:H, hs], None, ALU.mult), False)
                for j in range(1, GC):
                    for t in range(3):
                        if j == 1:
                            dve.wait_ge(*ga.after(f"c{t}", i))
                        else:
                            step(gd, f"cv{t}{j - 1}", i)
                        c = cv[:, t * GV:(t + 1) * GV]
                        d(f"cv{t}{j}", stt(c, one(gq, i + t * H)[:, j:j + GV], gcw[:, j, bass.ds(i + t * H, 1)], c,
                                           ALU.mult, ALU.add), False)
                yield 0
                d("clampz", ts(sg[:, 3 * GV:], one(zm, i + 3 * H), SIG_MIN, None, ALU.max), False)
                yield 1
                dve.wait_ge(*ga.after("sg3", i))
                step(gd, f"cv2{GC - 1}", i)
                cv3, sg3 = cv[:].rearrange("p (t g) -> p t g", t=3), sg[:, 0:3 * GV].rearrange("p (t g) -> p t g", t=3)
                d("qkv1", tt(qkv[:, :, 0:TP], cv3[:, :, 0:TP], sg3[:, :, 0:TP], ALU.mult), False)
                d("qkv2", tt(qkv[:, :, TP:T].rearrange("p t (b s) -> p t b s", s=L), spaced(cv3[:, :, GPAD + TP:], GS),
                             spaced(sg3[:, :, GPAD + TP:], GS), ALU.mult), False)
                yield 2
                dve.wait_ge(*ga.after("rn2", i))
                step(gd, "qkv2", i)
                q_, k_, v_ = (qkv[:, t] for t in range(3))
                d("k", tt(k_, k_, rn[:, 1], ALU.mult), False)
                d("q", stt(q_, q_, QSCALE, rn[:, 0], ALU.mult, ALU.mult), False)
                dve.wait_ge(*ga.after("eg", i))
                step(gd, "q", i)
                d("ke", tt(ke[:], k_, eg[:], ALU.mult), False)
                d("qe", tt(qe[:], q_, eg[:], ALU.mult), False)
                for n, t0, c in PARTS:
                    d(f"d{c}", stt(dec[0:n, t0:t0 + n], pm[0:n, 2, t0:t0 + n], cols[0:n, 0, c, hs],
                                   (incl if n == P else incl_s)[:], ALU.subtract, ALU.min), False)
                yield 3
                dve.wait_ge(*gt.after("tr", i))
                for n, _, c in PARTS:
                    d(f"bv{c}", ts(bv[0:n, c], pm[0:n, 1, c * P:(c + 1) * P], cols[0:n, 1, c, hs], None, ALU.mult), False)
                dve.wait_ge(*ga.after("d2", i))
                d("bd1", tt(bd[:, 0:TP], dec[:, 0:TP], pm[:, 3, 0:TP], ALU.mult), False)
                d("bd2", tt(bd[0:TS, TP:T], dec[0:TS, TP:T], pm[0:TS, 3, TP:T], ALU.mult), False)
                yield 4
                halves = [(P, slice(0, TP)), (TS, slice(TP, T))]

                def level(l, n):
                    return lev[:, l].unsqueeze(1).to_broadcast([P, 2, P]) if n == P else lev[0:TS, l, 0:TS]

                def part(t, n, cc):
                    return t[:, cc].rearrange("p (c t) -> p c t", c=2) if n == P else t[0:n, cc]

                dve.wait_ge(*gt.after("kk", i))
                step(gd, "bd2", i)
                for (n, cc), name in zip(halves, ("at1", "at2")):
                    d(name, tt(at_[0:n, cc], pm[0:n, 2, cc], bd[0:n, cc], ALU.mult), False)
                dve.wait_ge(*gt.after("kq", i))
                for (n, cc), name in zip(halves, ("pt1", "pt2")):
                    d(name, tt(pt[0:n, cc], pm[0:n, 0, cc], dec[0:n, cc], ALU.mult), False)
                step(gd, "at2", i)
                for (n, cc), name in zip(halves, ("n0a", "n0b")):
                    d(name, tt(part(nt0, n, cc), part(at_, n, cc), level(0, n), ALU.mult))
                eye = lambda n: ident[:].unsqueeze(1).to_broadcast([P, 2, P]) if n == P else ident[0:TS, 0:TS]
                for (n, cc), name in zip(halves, ("xt1", "xt2")):
                    d(name, tt(part(xx[:, 1], n, cc), eye(n), part(nt0, n, cc), ALU.subtract), False)
                yield 5
                for (n, cc), name in zip(halves, ("n1a", "n1b")):
                    d(name, tt(part(nt1, n, cc), part(at_, n, cc), level(1, n), ALU.mult), False)
                yield 6
                yield 7
                for l in LEVELS:
                    dve.wait_ge(*gt.after(f"xx{l}", i))
                    if l == 1:
                        d("xx1s", tt(xx[0:TS, :, TP:T], xx[0:TS, :, TP:T], pm[0:TS, 0:2, TP:T], ALU.subtract), False)
                    d(f"xx{l}", tt(xx[:, :, 0:TP], xx[:, :, 0:TP], pm[:, 0:2, 0:TP], ALU.subtract), False)
                    if l < NLEV - 1:
                        nt = (nt0, nt1)[(l + 1) % 2]
                        d(f"n{l + 1}", tt(part(nt, P, slice(0, TP)), part(at_, P, slice(0, TP)), level(l + 1, P), ALU.mult), False)
                        yield 2 * l + 6
                        yield 2 * l + 7
                yield 16
                yield 17

                def state(n):
                    dve.wait_ge(*gt.after(f"u{n}", i))
                    if n == 0:
                        dve.wait_ge(ss_out, 32 * i)
                        d("S0", tc(S[:], pm[:, 3, 0:P]), False)
                    else:
                        d(f"S{n}", stt(S[:], S[:], eg[:, CH * n + CH - 1:CH * n + CH], pm[:, 3, 0:P], ALU.mult, ALU.add), False)

                def resid(n):
                    lo, c = CH * (n % 2), n // 2
                    dve.wait_ge(*gt.after(f"k{n}", i))
                    d(f"R{n}", stt(rr[lo:lo + CH], pm[lo:lo + CH, 2, P:2 * P], nbeta[lo:lo + CH, c, hs], bv[lo:lo + CH, c],
                                   ALU.mult, ALU.add), False)

                state(0)
                dve.wait_ge(*gt.after("trS", i))
                d("rs", stt(r_s[:], pm[0:TS, 1, P:2 * P], nbeta[0:TS, 2, hs], bv[0:TS, 2], ALU.mult, ALU.add), False)
                yield 18
                resid(1)
                yield 19
                yield 20
                state(1)
                yield 21
                resid(2)
                yield 22
                yield 23
                state(2)
                yield 24
                resid(3)
                yield 25
                yield 26
                state(3)
                yield 27
                dve.wait_ge(*ga.after("rs2", i))
                dve.wait_ge(*gp.after("sse", i))
                d("go", stt(gout[:], pm[:, 0, 0:T], wgn[:], rso[:], ALU.mult, ALU.mult), False)
                dve.wait_ge(*gt.after("Ss", i))
                d("ss", tt(ss[:], ss[:], pm[:, 2:4].rearrange("p a (b v) -> p (a b) v", v=P), ALU.add), False)
                dve.wait_ge(*ga.after("hi", i))
                d("lo", tt(one(go_lo, i), gout[:], one(go_hi, i).bitcast(F32), ALU.subtract), False)

            with dve.Fori(0, H) as i:
                group(split_lo, i + q_heads, (), gdn(i), GDN_STAGES)

            dve.wait_ge(ss_out, 32 * H)
            nc.vector.memset(vt[:, :, P:], 1.0).then_inc(vt_ones, 1)

            def mlstm(i):
                def d(name, instruction):
                    instruction.then_inc(*md_.done(name))
                hs = bass.ds(i, 1)
                dve.wait_ge(cs_out, 32 * i)
                dve.wait_ge(*ma.before(i))
                dve.wait_ge(*mt.before(i))
                q_t = one(zm, i)
                d("so", ts(so[:], one(zm, i + 3 * H), SIG_MIN, None, ALU.max))
                d("sel", ts(mrsel[32:32 + H], m_row, ident[32:32 + H, bass.ds(i + 32, 1)], None, ALU.mult))
                d("k", ts(mk[:], one(zm, i + H), QSCALE, None, ALU.mult))
                d("v", tc(mv[:], one(zm, i + 2 * H)))
                yield 0
                dve.wait_ge(*mt.after("rows", i))
                for n, t0, c in PARTS:
                    d(f"D{c}", stt(md[0:n, t0:t0 + n], pm[0:n, 0, t0:t0 + n], cols[0:n, 3, c, hs],
                                   (incl if n == P else incl_s)[:], ALU.add, ALU.min))
                d("qw", tt(qw[:], q_t, pm[:, 1, 0:T], ALU.mult))
                yield 1
                step(md_, "qw", i)
                d("prs", tt(prd[:, TP:T].rearrange("p (b s) -> p b s", s=L), qw[:, TP:T].rearrange("p (b s) -> p b s", s=L),
                            n_s[:, :, hs].to_broadcast([P, NB, L]), ALU.mult))
                dve.wait_ge(*mt.after("kq", i))
                dve.wait_ge(*ma.after("d2", i))
                d("pt1", tt(mpt[:, 0:TP], pm[:, 0, 0:TP], md[:, 0:TP], ALU.mult))
                d("pt2", tt(mpt[0:TS, TP:T], pm[0:TS, 0, TP:T], md[0:TS, TP:T], ALU.mult))
                yield 2

                def state(n):
                    dve.wait_ge(*mt.after(f"u{n}", i))
                    if n == 0:
                        d("C0", tc(ctn[:], pm[:, 3, 0:P + 1]))
                    else:
                        d(f"C{n}", stt(ctn[:], ctn[:], emt[:, T + n:T + n + 1], pm[:, 3, 0:P + 1], ALU.mult, ALU.add))
                    step(md_, f"C{n}", i)
                    if n + 1 < NCH:
                        cc = slice(CH * (n + 1), CH * (n + 2))
                        d(f"pr{n + 1}", ts(prd[:, cc], qw[:, cc], ctn[:, P:], None, ALU.mult))

                for n in range(3):
                    state(n)
                    yield 3 + n
                state(3)
                d("np", tc(n_p[:, hs], ctn[:, P:]))
                dve.wait_ge(*mt.after("ns", i))
                n_h = n_s[:, :, hs].rearrange("p b a -> p (b a)")
                d("ns", tt(n_h, n_h, emt[:, T + NCH:], ALU.mult))
                step(md_, "ns", i)
                d("ns2", tt(n_h, n_h, pm[:, 0, 0:NB], ALU.add))
                yield 6
                dve.wait_ge(*ma.after("abs", i))
                d("mx", tt(dn[:], dn[:], emt[:, 0:T], ALU.max))
                step(md_, "mx", i)
                d("rc", nc.vector.reciprocal(dn[:], dn[:]))
                step(md_, "rc", i)
                d("h", tt(mh[:], pm[:, 1, 0:T], dn[:], ALU.mult))
                step(md_, "h", i)
                d("ho", tt(mh[:], mh[:], so[:], ALU.mult))
                dve.wait_ge(*mt.after("C", i))
                dve.wait_ge(*mp.after("cs", i))
                for k, bank in enumerate((0, 3)):
                    half = cs[:, 4 * k:4 * k + 4].rearrange("p b v -> p (b v)")
                    d(f"cs{k + 1}", tt(half, half, pm[:, bank], ALU.add))
                dve.wait_ge(*ma.after("hi", i))
                d("lo", tt(one(mh_lo, i), mh[:], one(mh_hi, i).bitcast(F32), ALU.subtract))

            with dve.Fori(0, H) as i:
                group(split_lo, i + q_gate, (), mlstm(i), MLSTM_STAGES)

            with dve.Fori(0, 4) as i:
                def first(h, c):
                    m = 2 * h + c
                    dve.wait_ge(blocks, 16 * (i + q_branch) + (8 * h + 4))
                    dve.wait_ge(*br_a.after(f"sa{m}", i))
                    tt(mix_a[:, m], one(gates, 4 * i + m), ps[:, c, 0:T], ALU.mult).then_inc(bank_free, 1)

                def second(h, c):
                    m = 2 * h + c
                    dve.wait_ge(blocks, 16 * (i + q_branch) + (8 * h + 8))
                    dve.wait_ge(*br_a.after(f"sb{m}", i))
                    tt(mix_b[:, m], one(gates, 4 * i + m + KT), ps[:, 2 + c, 0:T], ALU.mult).then_inc(bank_free, 1)
                    dve.wait_ge(*freed(2 * i + (g_branch + h), 2 + c))
                    tt(mix_b[:, m], mix_b[:, m], mix_a[:, m], ALU.add).then_inc(*br_d.done(f"s{m}"))

                def rest(h):
                    for m in (2 * h, 2 * h + 1):
                        dve.wait_ge(*br_a.after(f"hi{m}", i))
                        tt(one(mix_lo, 4 * i + m), mix_b[:, m], one(mix_hi, 4 * i + m).bitcast(F32), ALU.subtract)\
                            .then_inc(*br_d.done(f"lo{m}"))
                points = []
                for h in range(2):
                    points += [(8 * h + 3 + k % 2 + 4 * (k // 2), lambda h=h, k=k: (first, second)[k // 2](h, k % 2)) for k in range(4)]
                    points += [(8 * h + 10, lambda h=h: rest(h))]
                group(split_lo, i + q_branch, points)

            for n in range(3, 7):
                split_lo(q_out, n, 8)
            with dve.Fori(0, 4) as i:
                def evacuate(m, done):
                    dve.wait_ge(blocks, 16 * (i + q_out) + done)
                    dve.wait_ge(*ot_a.after(f"x{m}", i))
                    t = one(x2, 4 * i + m)
                    tt(t, t, ps[:, m, 0:T], ALU.add).then_inc(bank_free, 1)

                def rest(m, done):
                    dve.wait_ge(*ot_a.after(f"hi{m}", i))
                    stt(one(f_lo, 4 * i + m), one(x2, 4 * i + m), wn[:, 1, bass.ds(4 * i + m, 1)],
                        one(f_hi, 4 * i + m).bitcast(F32), ALU.mult, ALU.subtract).then_inc(*ot_d.done(f"lo{m}"))
                group(split_lo, i + q_out, column_tiles(evacuate, rest), ring=8)
            dve.wait_ge(*n2_t.after("w"))
            for j in range(FC):
                last = tc(fcw[:, j], pm[:, 1, j * 2 * FT:(j + 1) * 2 * FT])
            last.then_inc(*n2_d.done("w"))
            dve.wait_ge(*n2_d.after("w"))
            last = nc.vector.memset(uu[:, :, 0:FPAD], 0.0)
            last.then_inc(uu_zero, 1)
            dve.wait_ge(*n2_a.after("exp"))

            q, g0 = q_ffn, 0
            for c, n in enumerate(CHUNKS):
                def up(i, tail_next):
                    r = i + g0

                    def old_rows(half, name):
                        dve.wait_ge(*up_t.after(f"old{half}", r))
                        if half:
                            dve.wait_ge(*up_p.after("g2", r))
                        else:
                            dve.wait_ge(*up_p.before(r))
                        tc(seqs3(uu[:, :, FPAD + TP:], FS, 0, FPAD),
                           pm[:, 2 + half, 0:4 * NB * FPAD].rearrange("p (t b s) -> p t b s", t=4, s=FPAD))\
                            .then_inc(*up_d.done(name))

                    def turned(m, n_, q_, done):
                        dve.wait_ge(blocks, 16 * (2 * i + q_) + done)
                        tt(seqs(uu[:, m, FPAD + TP:], FS, FPAD, FS), ps[:, m, TP:T].rearrange("p (b s) -> p b s", s=L),
                           r2[:, TP:T].rearrange("p (b s) -> p b s", s=L), ALU.mult).then_inc(*up_d.done(f"{n_}{m}"))
                        tt(uu[:, m, FPAD:FPAD + TP], ps[:, m, 0:TP], r2[:, 0:TP], ALU.mult).then_inc(bank_free, 1)

                    def taps(dst, m, n_, offset):
                        tile = bass.ds(4 * r + (m + offset), 1)
                        for j, k in ((1, "a"), (2, "b")):
                            if j == 1:
                                dve.wait_ge(*up_a.after(f"{n_}{m}", r))
                            else:
                                dve.wait_ge(*up_d.after(f"{n_}c{m}a", r))
                            stt(dst[:, m], uu[:, m, j:j + FV], fcw[:, j, tile], dst[:, m], ALU.mult, ALU.add)\
                                .then_inc(*up_d.done(f"{n_}c{m}{k}"))

                    def gate(m, done):
                        if m == 0:
                            old_rows(0, "og")
                        turned(m, "g", q, done)

                    def gate_taps(m, done):
                        taps(ug, m, "g", 0)

                    def value(m, done):
                        if m == 0:
                            old_rows(1, "ov")
                        turned(m, "v", q + 1, done)

                    def value_taps(m, done):
                        taps(uv, m, "v", FT)

                    def gated(m, done):
                        dve.wait_ge(*up_a.after(f"sg{m}", r))
                        dve.wait_ge(*up_d.after(f"vc{m}b", r))
                        a_t = ac[:, m % 2]
                        tt(a_t[:, 0:TP], ug[:, m, 0:TP], uv[:, m, 0:TP], ALU.mult).then_inc(*up_d.done(f"ac{m}a"))
                        tt(a_t[:, TP:T].rearrange("p (b s) -> p b s", s=L), spaced(ug[:, m, FPAD + TP:], FS),
                           spaced(uv[:, m, FPAD + TP:], FS), ALU.mult).then_inc(*up_d.done(f"ac{m}b"))

                    def rest(m, done):
                        dve.wait_ge(*up_a.after(f"hi{m}", r))
                        tt(one(u_lo, 4 * i + m), ac[:, m % 2], one(u_hi, 4 * i + m).bitcast(F32), ALU.subtract).then_inc(*up_d.done(f"lo{m}"))
                    group(split_lo, 2 * i + q, column_tiles(gate, gate_taps), ring=8)
                    group(split_lo, 2 * i + (q + 1), column_tiles(value, value_taps, gated, rest), ring=8, tail_next=tail_next)
                repeat(dve, n, up, n == TAIL)
                q += 2 * n
                g0 += n

                def down(q_, tile, at=0, n=4):
                    def evacuate(m, done):
                        dve.wait_ge(blocks, 16 * q_ + (at + done))
                        t = one(x2, tile + m)
                        tt(t, t, ps[:, m, 0:T], ALU.add).then_inc(bank_free, 1)
                    return column_tiles(evacuate, n=n)

                if n == 4:
                    with dve.Fori(0, 4) as i:
                        group(split_lo, i + q, down(i + q, 4 * i), ring=8)
                else:
                    for i in range(4):
                        at = 4 * n * i
                        group(split_lo, q, down(q, 4 * i, at, n), ring=8, b0=at, n=4 * n, tail=True)
                q += n
            dve.wait_ge(*y_a.after("exp"))
            for f in range(KT):
                if f >= 8:
                    dve.wait_ge(*y_t.after(f"t{f // 4 - 2}"))
                stt(yt[:, f % 8], x2[:, f], wn[:, 2, f:f + 1], r2[:], ALU.mult, ALU.mult).then_inc(*y_d.done(f"y{f}"))

        @block.tensor
        def _(pe):
            mm = nc.tensor.matmul

            def turn(out, in_, n):
                return nc.tensor.transpose(out, in_, ident[0:n, 0:n])

            pe.wait_ge(rows_in, 16 * 7)
            pe.wait_ge(consts, N_CONST)
            turn(pm[:, 0, 0:GC * 3 * H], w_rows[:], GC * 3 * H)
            turn(pm[:, 0, 128:128 + 3 * KT], norm_rows[:], 3 * KT)
            turn(pm[:, 0, 256:256 + NB * H], n_rows[:], NB * H).then_inc(*st_t.done("consts"))
            for t in range(3 * H):
                n = NB * GPAD
                last = turn(pm[:, t // 8 + 1, t % 8 * n:(t % 8 + 1) * n], conv_rows[:, t * P:(t + 1) * P], n)
            last.then_inc(*st_t.done("old"))
            pe.wait_ge(*st_d.after("xs2"))
            for f in range(KT):
                if f >= 4:
                    pe.wait_ge(*st_d.after(f"lo{f - 4}"))
                for n, t0, c in PARTS:
                    last = turn(ps[:, f % 4, t0:t0 + n], x_rows[0:n, c, f * P:(f + 1) * P], n)
                last.then_inc(*st_t.done(f"x{f}"))

            def product(out, w_hi, w_lo, x_hi, x_lo, start, stop):
                mm(out, w_hi, x_hi, start=start, stop=False)
                mm(out, w_hi, x_lo, start=False, stop=False)
                return mm(out, w_lo, x_hi, start=False, stop=stop)

            pe.wait_ge(*st_d.after(f"lo{KT - 1}"))
            pe.wait_ge(*st_d.after("old2"))
            for k in range(KT):
                last = product(pm[:, 3, 0:T], sm_hi[:, k], sm_lo[:, k], h_hi[:, k], h_lo[:, k], k == 0, k == KT - 1)
            last.then_inc(*st_t.done("small"))
            pe.wait_ge(*gate_d.after("sw2"))
            pe.wait_ge(*gate_a.after("sw"))
            for n_, t in enumerate((g_row[:, 0], g_row[:, 1], e_row[:], c_row[:], cmx[0][:])):
                for n, t0, c in PARTS:
                    at0 = (3 * n_ + c) * H
                    last = turn(pm[0:n, 0, at0:at0 + H], t[:, t0:t0 + n], H)
            last.then_inc(*gate_t.done("cols"))

            def column_tile(q, b0, n, bank, free, x_hi, x_lo, ring, mixer=None, stages=0, b_all=0, n_all=16, x_last=None):
                pe.wait_ge(bank_free, free)
                for j in range(n):
                    if x_last and j == n - 1:
                        pe.wait_ge(*x_last)
                    pe.wait_ge(lo_ready, 16 * q + (b0 + j + 1))
                    hi, lo = ring_slot(whi, whi2, b0 + j, ring), ring_slot(wlo, wlo2, b0 + j, ring)
                    for k in range(4):
                        kk = 4 * j + k
                        last = product(ps[:, bank, 0:T], hi[:, k], lo[:, k], x_hi[:, kk], x_lo[:, kk],
                                       kk == 0, kk == 4 * n - 1)
                    last.then_inc(blocks, 1)
                    b = b_all + j
                    for _ in range((b + 1) * stages // n_all - b * stages // n_all):
                        next(mixer, None)

            def pe_group(q, g, x_hi, x_lo, mixer=None, stages=0, ring=4, b0=0, n=4, x_last=None):
                for m in range(4):
                    column_tile(q, b0 + n * m, n, m, 4 * g + (m + 1), x_hi, x_lo, ring, mixer, stages, n * m, 4 * n, x_last)
                for _ in mixer or ():
                    pass

            with pe.Fori(0, 6) as i:
                pe_group(i, i, h_hi, h_lo)

            def last_rows(i):
                pe.wait_ge(*lst_p.after("b", i))
                pe.wait_ge(*lst_a.before(i))
                for t in range(12):
                    last = turn(pm[0:GPAD * (1 + NB), t // 4, t % 4 * P:(t % 4 + 1) * P], g_last[:, t], P)
                last.then_inc(*lst_t.done("tr"))
                yield 0

            with pe.Fori(0, 2) as i:
                pe_group(i + q_z, i + g_z, h_hi, h_lo, last_rows(i), 16)

            def gdn(i):
                q_, k_, v_ = (qkv[:, t] for t in range(3))
                yield 0
                yield 1
                pe.wait_ge(*gp.after("sq", i))
                pe.wait_ge(*gd.before(i))
                for t in range(2):
                    mm(pm[:, t, 0:T], ones[:], sq[:, t], start=True, stop=True)
                pe.wait_ge(*gd.after("rsel", i))
                for t in range(2):
                    last = mm(pm[:, 2 + t, 0:T], ones[0:H], rsel[:, t], start=True, stop=True)
                last.then_inc(*gt.done("norm"))
                yield 2
                pe.wait_ge(*gd.after("q", i))
                for t, src in ((0, k_), (1, v_)):
                    for n, t0, c in PARTS:
                        last = turn(pm[0:n, t, c * P:(c + 1) * P], src[:, t0:t0 + n], P)
                last.then_inc(*gt.done("tr"))
                pe.wait_ge(*gd.after("d2", i))
                pe.wait_ge(*ga.after("eg", i))
                for n, t0, c in PARTS:
                    cc = slice(t0, t0 + n)
                    last = mm(pm[0:n, 2, cc], k_[:, cc], k_[:, cc], start=True, stop=True)
                last.then_inc(*gt.done("kk"))
                yield 3
                pe.wait_ge(*ga.after("kg2", i))
                for n, t0, c in PARTS:
                    cc = slice(t0, t0 + n)
                    last = mm(pm[0:n, 0, cc], k_[:, cc], q_[:, cc], start=True, stop=True)
                last.then_inc(*gt.done("kq"))
                yield 4
                pe.wait_ge(*gd.after("xt2", i))
                for n, t0, c in PARTS:
                    cc = slice(t0, t0 + n)
                    last = turn(pm[0:n, 1, cc], xx[0:n, 1, cc], n)
                last.then_inc(*gt.done("x0"))
                yield 5
                for l in LEVELS:
                    nt = (nt0, nt1)[l % 2]
                    parts = PARTS if l == 1 else PARTS[:2]
                    if l == 1:
                        pe.wait_ge(*gd.after("n1b", i))
                        pe.wait_ge(*ga.after("x0b", i))
                    else:
                        pe.wait_ge(*gd.after(f"n{l}", i))
                    for n, t0, c in parts:
                        cc = slice(t0, t0 + n)
                        last = mm(pm[0:n, 3, cc], nt[0:n, cc], xx[0:n, 0, cc], start=True, stop=True)
                    last.then_inc(*gt.done(f"p{l}"))
                    yield 2 * l + 4
                    pe.wait_ge(*ga.after(f"psb{l}", i))
                    for n, t0, c in parts:
                        cc = slice(t0, t0 + n)
                        mm(pm[0:n, 0, cc], xx[0:n, 1, cc], psb[0:n, cc], start=True, stop=True)
                        last = mm(pm[0:n, 1, cc], psb[0:n, cc], xx[0:n, 1, cc], start=True, stop=True)
                    last.then_inc(*gt.done(f"xx{l}"))
                    yield 2 * l + 5

                def k_s(n):
                    lo, cc = CH * (n % 2), slice(CH * n, CH * n + CH)
                    pe.wait_ge(*gd.after(f"S{n - 1}", i))
                    mm(pm[lo:lo + CH, 2, P:2 * P], ke[:, cc], S[:], start=True, stop=True).then_inc(*gt.done(f"k{n}"))

                def t_r(n):
                    lo, cc, c = CH * (n % 2), slice(CH * n, CH * n + CH), n // 2
                    rhs = bv[lo:lo + CH, c] if n == 0 else rr[lo:lo + CH]
                    pe.wait_ge(*gd.after("xx5" if n == 0 else f"R{n}", i))
                    apart(pe)
                    mm(pm[lo:lo + CH, 2, 0:P], xx[lo:lo + CH, 1, cc], rhs, start=True, stop=True).then_inc(*gt.done(f"T{n}"))

                def update(n):
                    lo, cc, c = CH * (n % 2), slice(CH * n, CH * n + CH), n // 2
                    pe.wait_ge(*ga.after(f"vn{n}", i))
                    if n:
                        mm(pm[:, 0, cc], S[:], qe[:, cc], start=True, stop=False)
                    mm(pm[:, 0, cc], vn[lo:lo + CH], pt[lo:lo + CH, cc], start=n == 0, stop=True)
                    mm(pm[:, 3, 0:P], kg[lo:lo + CH, c], vn[lo:lo + CH], start=True, stop=True).then_inc(*gt.done(f"u{n}"))

                t_r(0)
                pe.wait_ge(ss_in, 16 * i + 16)
                for b in range(NB):
                    cc = slice(TP + b * L, TP + b * L + L)
                    last = mm(pm[:, 1, b * L:(b + 1) * L], ss[:, b], ke[:, cc], start=True, stop=True)
                last.then_inc(*gt.done("ksS"))
                yield 16
                update(0)
                pe.wait_ge(*ga.after("ks_s", i))
                turn(pm[0:TS, 1, P:2 * P], ks_s[:], P).then_inc(*gt.done("trS"))
                yield 17
                k_s(1)
                pe.wait_ge(*gd.after("rs", i))
                apart(pe)
                mm(pm[0:TS, 1, 2 * P:3 * P], xx[0:TS, 1, TP:T], r_s[:], start=True, stop=True).then_inc(*gt.done("TS"))
                yield 18
                t_r(1)
                pe.wait_ge(*ga.after("vn_s", i))
                mm(pm[:, 0, TP:T], vn_s[:], pt[0:TS, TP:T], start=True, stop=False)
                for b in range(NB):
                    cc = slice(TP + b * L, TP + b * L + L)
                    last = mm(pm[:, 0, cc], ss[:, b], qe[:, cc], start=False, stop=b == NB - 1)
                last.then_inc(*gt.done("oS"))
                yield 19
                update(1)
                yield 20
                k_s(2)
                yield 21
                t_r(2)
                yield 22
                update(2)
                yield 23
                k_s(3)
                yield 24
                t_r(3)
                yield 25
                update(3)
                yield 26
                pe.wait_ge(*gd.after("S3", i))
                pe.wait_ge(*gp.after("vnm", i))
                for half in range(2):
                    last = mm(pm[:, 2 + half], kg[0:TS, 2], vnm[:, 4 * half:4 * half + 4].rearrange("p b v -> p (b v)"),
                              start=True, stop=True)
                last.then_inc(*gt.done("Ss"))
                pe.wait_ge(*ga.after("sqo", i))
                mm(pm[:, 1, 0:T], ones[:], sqo[:], start=True, stop=True).then_inc(*gt.done("nrm"))

            with pe.Fori(0, H) as i:
                pe_group(i + q_heads, i + g_heads, h_hi, h_lo, gdn(i), GDN_STAGES)

            def mlstm(i):
                q_t = one(zm, i)
                pe.wait_ge(*md_.after("v", i))
                pe.wait_ge(*ma.before(i))
                if 1:
                    sel = mrsel[32:32 + H]
                    for bank, cc in ((0, slice(0, T)), (1, slice(T, 2 * T)), (2, slice(2 * T, 3 * T + NC))):
                        last = mm(pm[:, bank, 0:cc.stop - cc.start], ones[32:32 + H], sel[:, cc], start=True, stop=True)
                    last.then_inc(*mt.done("rows"))
                for n, t0, c in PARTS:
                    last = turn(pm[0:n, 3, c * P:(c + 1) * P], mk[:, t0:t0 + n], P)
                last.then_inc(*mt.done("ktr"))
                yield 0
                pe.wait_ge(*ma.after("kw2", i))
                for n, t0, c in PARTS:
                    last = turn(pm[0:n, 3, c * P:(c + 1) * P], mv[:, t0:t0 + n], P)
                last.then_inc(*mt.done("vtr"))
                pe.wait_ge(*md_.after("D2", i))
                for n, t0, c in PARTS:
                    cc = slice(t0, t0 + n)
                    last = mm(pm[0:n, 0, cc], mk[:, cc], q_t[:, cc], start=True, stop=True)
                last.then_inc(*mt.done("kq"))
                yield 1

                def turn_states(half):
                    for b in range(4):
                        last = turn(pm[:, 0, b * P:(b + 1) * P], cs[:, 4 * half + b], P)
                    last.then_inc(*mt.done(f"c{half}"))

                def chunk(n):
                    lo, cc, c = CH * (n % 2), slice(CH * n, CH * n + CH), n // 2
                    if n:
                        pe.wait_ge(*md_.after(f"pr{n}", i))
                        mm(pm[:, 1, cc], ctn[:, 0:P], qw[:, cc], start=True, stop=False)
                    mm(pm[:, 1, cc], vt[lo:lo + CH, c, 0:P], mpt[lo:lo + CH, cc], start=n == 0, stop=True)
                    if n:
                        mm(pm[:, 2, cc], ones[:], prd[:, cc], start=True, stop=False)
                    mm(pm[:, 2, cc], ones[lo:lo + CH], mpt[lo:lo + CH, cc], start=n == 0, stop=True)
                    mm(pm[:, 3, 0:P + 1], kw[lo:lo + CH, c], vt[lo:lo + CH, c], start=True, stop=True).then_inc(*mt.done(f"u{n}"))

                pe.wait_ge(cs_in, 16 * i + 16)
                pe.wait_ge(*md_.after("pt2", i))
                pe.wait_ge(*ma.after("v2", i))
                turn_states(0)
                chunk(0)
                yield 2
                pe.wait_ge(*ma.after("ct0", i))
                turn_states(1)
                chunk(1)
                yield 3
                chunk(2)
                yield 4
                chunk(3)
                pe.wait_ge(*ma.after("ct1", i))
                mm(pm[:, 0, 0:NB], kw[0:TS, 2], seq[:], start=True, stop=True).then_inc(*mt.done("ns"))
                mm(pm[:, 1, TP:T], vt[0:TS, 2, 0:P], mpt[0:TS, TP:T], start=True, stop=False)
                for b in range(NB):
                    cc = slice(TP + b * L, TP + b * L + L)
                    mm(pm[:, 1, cc], cts[:, b], qw[:, cc], start=False, stop=b == NB - 1)
                mm(pm[:, 2, TP:T], ones[:], prd[:, TP:T], start=True, stop=False)
                mm(pm[:, 2, TP:T], ones[0:TS], mpt[0:TS, TP:T], start=False, stop=True).then_inc(*mt.done("so"))
                yield 5
                pe.wait_ge(*md_.after("ns2", i))
                pe.wait_ge(*mp.after("km", i))
                for half, bank in enumerate((0, 3)):
                    last = mm(pm[:, bank], vt[0:TS, 2, 0:P], km[:, 4 * half:4 * half + 4].rearrange("p b k -> p (b k)"),
                              start=True, stop=True)
                last.then_inc(*mt.done("C"))
                yield 6
                pe.wait_ge(*md_.after("h", i))
                turn(pm[:, 1, 0:P], ctn[:, 0:P], P).then_inc(*mt.done("cp"))

            with pe.Fori(0, H) as i:
                pe_group(i + q_gate, i + g_gate, h_hi, h_lo, mlstm(i), MLSTM_STAGES)

            pe.wait_ge(*md_.before(H))
            pe.wait_ge(*ma.before(H))
            turn(pm[0:NB * H, 0, 0:P], n_s[:].rearrange("p b h -> p (b h)"), P)
            turn(pm[0:H, 1, 0:P], n_p[:], P).then_inc(*no_t.done("tr"))

            with pe.Fori(0, 4) as i:
                for u in range(4):
                    x_hi, x_lo = ((go_hi, go_lo), (mh_hi, mh_lo))[u % 2]
                    pe.wait_ge(bank_free, 8 * i + (4 * g_branch + 2 * u + 2))
                    for j in range(4):
                        pe.wait_ge(lo_ready, 16 * (i + q_branch) + (4 * u + j + 1))
                        for k in range(4):
                            kk = 2 * j + k // 2
                            last = product(ps[:, 2 * (u % 2) + k % 2, 0:T], whi[:, j, k], wlo[:, j, k], x_hi[:, kk], x_lo[:, kk],
                                           kk == 0, kk == 7)
                        last.then_inc(blocks, 1)

            pe.wait_ge(*br_d.before(4))
            pe.wait_ge(*no_a.after("p"))

            def turn_input(i):
                pe.wait_ge(x_in2, 32 * i + 32)
                pe.wait_ge(*ot_a.before(i))
                for m in range(4):
                    for n, t0, c in PARTS:
                        last = turn(pm[:, m, t0:t0 + n], xg[0:n, c, m * P:(m + 1) * P], n)
                    last.then_inc(*ot_t.done(f"x{m}"))
                yield 0

            with pe.Fori(0, 4) as i:
                pe_group(i + q_out, i + g_out, mix_hi, mix_lo, turn_input(i), 16, ring=8)
            pe.wait_ge(fw_in, 16)
            pe.wait_ge(*ot_a.before(4))
            for j in range(FC):
                last = turn(pm[:, 1, j * 2 * FT:(j + 1) * 2 * FT], fw_rows[:, j], 2 * FT)
            last.then_inc(*n2_t.done("w"))
            pe.wait_ge(*ot_p.before(4))
            mm(pm[:, 0, 0:T], ones[:], ssq[:], start=True, stop=True).then_inc(*n2_t.done("sum"))
            pe.wait_ge(*ot_d.before(4))
            pe.wait_ge(*n2_d.after("w"))
            pe.wait_ge(*n2_a.after("ln"))

            q, g, g0, k0 = q_ffn, g_ffn, 0, 0
            for c, n in enumerate(CHUNKS):
                with pe.Fori(0, n) as i:
                    r = i + g0

                    def old_rows(half):
                        yield from range(3)
                        pe.wait_ge(old_in, 32 * r + 16 * (half + 1))
                        if half == 0:
                            pe.wait_ge(*up_d.before(r))
                        apart(pe)
                        for m in range(4):
                            n_ = NB * FPAD
                            last = turn(pm[:, 2 + half, m * n_:(m + 1) * n_], st_rows[:, half, m * P:(m + 1) * P], n_)
                        last.then_inc(*up_t.done(f"old{half}"))
                        yield 0
                    pe_group(2 * i + q, 2 * i + g, f_hi, f_lo, old_rows(0), 16, ring=8)
                    pe_group(2 * i + (q + 1), 2 * i + (g + 1), f_hi, f_lo, old_rows(1), 16, ring=8)
                q, g, g0 = q + 2 * n, g + 2 * n, g0 + n

                def last_rows(r):
                    pe.wait_ge(*dn_p.after("sel", r))
                    pe.wait_ge(*dn_a.before(r))
                    for t in range(8):
                        last = turn(pm[0:FPAD * (1 + NB), t // 4, t % 4 * P:(t % 4 + 1) * P], u_out[:, t], P)
                    last.then_inc(*dn_t.done("tr"))
                    yield 0
                pe.wait_ge(*up_d.before(g0 - 1))
                x_last = up_d.before(g0)
                if n == 4:
                    with pe.Fori(0, 4) as i:
                        pe_group(i + q, i + g, u_hi, u_lo, last_rows(i + 4 * c), 16, ring=8, x_last=x_last)
                else:
                    for i in range(4):
                        pe_group(q, g + i, u_hi, u_lo, last_rows(4 * c + i) if i < n else None, 16 if i < n else 0,
                                 ring=8, b0=4 * n * i, n=n, x_last=x_last)
                q, g = q + n, g + 4
            pe.wait_ge(*fin_p.before(KT))
            mm(pm[:, 3, 0:T], ones[:], ssq[:], start=True, stop=True).then_inc(*y_t.done("sum"))
            pe.wait_ge(*dn_a.before(11))
            for k in range(4):
                if k >= 2:
                    pe.wait_ge(*y_a.after(f"r{k - 2}"))
                bank = (ps, pm)[k % 2]
                pe.wait_ge(*y_d.after(f"y{4 * k + 3}"))
                for m in range(4):
                    f = 4 * k + m
                    for n, t0, c in PARTS:
                        last = turn(bank[0:n, c, m * P:(m + 1) * P], yt[:, f % 8, t0:t0 + n], P)
                last.then_inc(*y_t.done(f"t{k}"))


_OUTS = ["y_p", "y_s", "p_gconv", "p_S", "p_C", "p_n", "p_m", "p_fconv", "s_gconv", "s_S", "s_C", "s_n", "s_m", "s_fconv"]


def kernel(**inputs):
    import numpy as np
    import concourse.bacc as bacc
    from concourse.bass_utils import run_bass_kernel_spmd

    nc = bacc.Bacc("TRN2", target_bir_lowering=False, num_devices=1)
    arrays = {n: np.ascontiguousarray(x) for n, x in inputs.items()}
    arrays["norm_final_w"] = arrays["norm_final_w"].reshape(1, -1)
    a = {n: nc.dram_tensor(f"in_{n}", x.shape, F32, kind="ExternalInput").ap() for n, x in arrays.items()}
    x, s = arrays["x_prompt"].shape, arrays["x_sample"].shape
    one = lambda n: (1, x[0]) + arrays[n].shape[2:]
    states = ["state_gdn_conv", "state_gdn_S", "state_ml_C", "state_ml_n", "state_ml_m", "state_ffn_conv"]
    shapes = [x, s] + [one(n) for n in states] + [arrays[n].shape for n in states]
    o = {n: nc.dram_tensor(f"out_{n}", shape, F32, kind="ExternalOutput").ap() for n, shape in zip(_OUTS, shapes)}
    build(nc, a, o)
    r = run_bass_kernel_spmd(nc, [{f"in_{n}": x for n, x in arrays.items()}], core_ids=[0])
    return tuple(r.results[0][f"out_{n}"] for n in _OUTS)
```

```python
import concourse.bass as bass
from concourse import mybir
from concourse.alu_op_type import AluOpType as ALU
from contextlib import ExitStack
from itertools import islice

P = 128
F32 = mybir.dt.float32
F32R = mybir.dt.float32r
ACT = mybir.ActivationFunctionType
EPS = 1e-6
NEG = -1e30
SIG_MIN = -40.0
GATE_STAGES, MLSTM_STAGES = 24, 12
GDN_PACE = ["sp"] * 13 + ["spp", "ppp", "pppp"]
GDN_FIRST_PACE = ["p"] * 8 + ["p", "pp"] * 4
EXP_LN = "natural_log_exp_and_others"


class Steps:

    def __init__(self, sem, names):
        self.sem, self.names, self.at = sem, names.split(), 0
        assert len(set(self.names)) == len(self.names)

    def done(self, name):
        assert self.names[self.at % len(self.names)] == name, (name, self.names[self.at % len(self.names)])
        self.at += 1
        return self.sem, 1

    def after(self, name, r=0):
        return self.sem, r * len(self.names) + self.names.index(name) + 1

    def before(self, r):
        return self.sem, r * len(self.names)


def build(nc, a, o):
    D = a["w_in"].shape[1]
    KT = D // P
    TP = a["x_prompt"].shape[1]
    NB, L = a["x_sample"].shape[0], a["x_sample"].shape[1]
    TS = NB * L
    T = TP + TS
    CH = 64
    NCH = TP // CH
    H = a["state_gdn_S"].shape[2]
    FT = a["w_down"].shape[1] // P
    GC, QKV = a["gdn_conv_w"].shape[1:]
    FC = a["ffn_conv_w"].shape[1]
    GPAD, FPAD = GC - 1, FC - 1
    GS, FS = GPAD + L, FPAD + L
    GW, FW = GPAD + TP + NB * GS, FPAD + TP + NB * FS
    GV, FV = GW - GPAD, FW - FPAD
    c_z = QKV
    c_ga = c_z + H * P
    c_gb = c_ga + H
    c_mqkv = c_gb + H
    c_mi = c_mqkv + 3 * H * P
    c_mf = c_mi + H
    c_mo = c_mf + H
    c_gate = c_mo + H * P
    assert (D, T, H, NCH, FT, GC, FC) == (2048, 288, 8, 4, 44, 4, 3) and c_gate + 2 * D == a["w_in"].shape[2]
    QSCALE = float(P) ** -0.5
    PARTS = [(P, 0, 0), (P, P, 1), (TS, TP, 2)]
    TB = T * 4
    NG = 512
    NLEV = 6

    def row_tiles(w):
        return w[0].rearrange("(k p) n -> p k n", p=P)

    w_in, w_ba, w_bb, w_out, w_up, w_down = (
        row_tiles(a[n]) for n in ("w_in", "w_branch_a", "w_branch_b", "w_out", "w_up", "w_down"))
    xp_rows = a["x_prompt"][0].rearrange("(c p) d -> p c d", p=P)
    xs_rows = a["x_sample"].rearrange("b t d -> (b t) d")

    q_z, q_heads, q_gate, q_branch, q_out, q_ffn = 6, 8, 16, 24, 28, 32
    g_z, g_heads, g_gate, g_branch, g_out, g_ffn = 6, 8, 16, 24, 32, 36
    CHUNKS = [4, 4, 3]
    N_CONST = 5 + 4 * 2 - 2 + 4 * 6 + 3 + 1
    N_STORED, N_LROW = 4, 4 + 4 * sum(CHUNKS)

    ctx = ExitStack()
    with ctx:
        end = nc.sbuf_usable_end
        top = (nc.sbuf_base + 31) // 32 * 32

        def size_of(shape):
            n = 4
            for s in shape[1:]:
                n *= s
            return (n + 31) // 32 * 32

        class Region:

            def __init__(self, at, nbytes):
                self.at, self.end = at, at + nbytes
                assert self.end <= end, (self.end, end)

            def put(self, name, shape, dt=F32):
                n = size_of(shape)
                assert self.at + n <= self.end, (name, self.at + n - self.end)
                t = nc.alloc_sbuf_tensor_at(name, shape, dt, offset=self.at)
                self.at += n
                return t

        b_raw = top
        b_hi = b_raw + 4 * 4 * NG * 4
        b_lo = b_hi + 4 * 4 * P * 4
        b_gq = b_lo + 4 * 4 * P * 4
        b_x1 = b_gq + 3 * H * GW * 4
        b_zm = b_x1 + 6 * TB
        b_e = b_zm + 4 * H * TB
        b_h = b_e + 2 * H * TB
        b_mx = b_h + 2 * KT * TB
        raw = nc.alloc_sbuf_tensor_at("w_raw", [P, 4, KT, P], F32, offset=b_raw)
        whi = nc.alloc_sbuf_tensor_at("w_hi", [P, 4, 4, P], F32R, offset=b_hi)
        wlo = nc.alloc_sbuf_tensor_at("w_lo", [P, 4, 4, P], F32R, offset=b_lo)
        whi2 = nc.alloc_sbuf_tensor_at("w_hi_2", [P, 4, 4, P], F32R, offset=b_zm)
        wlo2 = nc.alloc_sbuf_tensor_at("w_lo_2", [P, 4, 4, P], F32R, offset=b_zm + 4 * 4 * P * 4)

        def tiles(name, at, n, dt=F32):
            return nc.alloc_sbuf_tensor_at(name, [P, n, T], dt, offset=at)

        gq = nc.alloc_sbuf_tensor_at("gdn_qkv", [P, 3 * H, GW], F32, offset=b_gq)
        zm = tiles("mqkv_z", b_zm, 4 * H)
        h_hi, h_lo = tiles("h_hi", b_h, KT, F32R), tiles("h_lo", b_h + KT * TB, KT, F32R)
        go_hi, go_lo = tiles("go_hi", b_e, H, F32R), tiles("go_lo", b_e + H * TB, H, F32R)
        mh_hi, mh_lo = tiles("mh_hi", b_zm, H, F32R), tiles("mh_lo", b_zm + H * TB, H, F32R)
        gates = tiles("gates", b_gq, 2 * KT)
        mix_hi, mix_lo = tiles("mix_hi", b_h, KT, F32R), tiles("mix_lo", b_h + KT * TB, KT, F32R)
        mix_a, mix_b = tiles("mix_a", b_zm + 3 * H * TB, 4), tiles("mix_b", b_zm + (3 * H + 4) * TB, 4)
        x2 = tiles("x2", b_zm + 2 * H * TB, KT)
        f_hi, f_lo = tiles("f_hi", b_gq, KT, F32R), tiles("f_lo", b_gq + KT * TB, KT, F32R)
        u_hi, u_lo = tiles("u_hi", b_h, KT, F32R), tiles("u_lo", b_h + KT * TB, KT, F32R)
        x_rows = nc.alloc_sbuf_tensor_at("x_rows", [P, 3, D], F32, offset=b_zm)
        e0 = Region(b_e, 2 * H * TB)
        conv_rows = e0.put("conv_rows", [NB * GPAD, QKV])
        w_rows = e0.put("w_rows", [GC * 3 * H, P])
        norm_rows = e0.put("norm_rows", [3 * KT, P])
        n_rows = e0.put("n_rows", [NB * H, P])
        y_rows = nc.alloc_sbuf_tensor_at("y_rows", [P, 3, D], F32, offset=b_h)
        yt = tiles("y_tiles", b_gq, 8)

        mx = Region(b_mx, end - b_mx)
        ident = mx.put("ident", [P, P])
        ones = mx.put("ones", [P, P])
        incl = mx.put("mask_chunk", [P, P])
        incl_s = mx.put("mask_seq", [TS, TS])
        lev = mx.put("mask_level", [P, NLEV, P])
        seq = mx.put("seq_of", [TS, NB])
        gcw = mx.put("gdn_conv_w_t", [P, GC, 3 * H])
        cols = mx.put("token_cols", [P, 5, 3, H])
        nbeta = mx.put("minus_beta", [P, 3, H])
        rows = mx.put("token_rows", [32 + H, 3 * T + NCH + NB])
        wn = mx.put("norm_w", [P, 3, KT])
        wgn = mx.put("gdn_norm_w_t", [P, 1])
        eps = mx.put("eps_col", [P, 1])
        rstd = mx.put("rstd", [P, 3])
        n_s = mx.put("n_sample", [P, NB, H])
        n_p = mx.put("n_prompt", [P, H])
        b_scr, n_scr = mx.at, mx.end - mx.at
        g_row = rows[0:H, 0:2 * T].rearrange("h (r t) -> h r t", r=2)
        m_row = rows[32:32 + H, :]

        s0 = Region(b_scr, n_scr)
        sm_raw = nc.alloc_sbuf_tensor_at("small_w", [P, KT, P], F32, offset=b_zm + size_of([P, 3, D]))
        sm_hi, sm_lo = s0.put("small_w_hi", [P, KT, P], F32R), s0.put("small_w_lo", [P, KT, P], F32R)
        s1 = Region(b_scr, n_scr)
        sp_in, sp_out = s1.put("sp_in", [H, 3, T]), s1.put("sp_out", [H, 3, T])
        cum = [s1.put(f"cum{i}", [H, 2, T]) for i in range(2)]
        cmx = [s1.put(f"cum_max{i}", [H, T]) for i in range(2)]
        c_row, e_row = s1.put("c_row", [H, T]), s1.put("e_row", [H, T])
        sw_row = s1.put("sw_row", [H, T])
        ig, mmx = s1.put("ig", [H, T]), s1.put("m_max", [H, T])
        NC = NCH + NB
        bl, cl = s1.put("b_last", [H, NC]), s1.put("c_last", [H, NC])
        m_in, m_new, f_row = s1.put("m_in", [H, NC]), s1.put("m_new", [H, NC]), s1.put("fw_row", [H, NC])
        hcol = s1.put("head_cols", [H, 8])
        s2, s3 = Region(b_x1, 6 * TB), Region(b_x1, 6 * TB)
        cv = s2.put("conv_out", [P, 3 * GV])
        dec, bd, nt0, psb = (s3.put(n, [P, T]) for n in ("decay", "beta_decay", "nt0", "p_sb"))
        at_, nt1 = bd, dec
        s5 = Region(b_scr, n_scr)
        sgz_at = s5.at
        sg = s5.put("sig", [P, 3 * GV + T])
        s6 = Region(sgz_at, size_of([P, 3 * GV + T]))
        rn = s6.put("rn", [P, 2, T])
        sq = s6.put("sq", [P, 2, T])
        qkv = s5.put("qkv", [P, 3, T])
        eg = s5.put("eg", [P, T])
        rsel = s5.put("row_sel", [H, T])
        s7 = Region(b_raw + 2 * KT * P * 4, 2 * KT * P * 4)
        handed = []
        for par, reg in enumerate((s5, s7)):
            qe, ke, pt = (reg.put(f"{n}_{par}", [P, T]) for n in ("qe", "ke", "pt"))
            kg, bv = (reg.put(f"{n}_{par}", [P, 3, P]) for n in ("kg", "bv"))
            xx = (s3, s7)[par].put(f"x_xt_{par}", [P, 2, T])
            ec = s5.put(f"eg_last_{par}", [P, NC])
            handed.append((qe, ke, pt, kg, bv, xx, ec))
        vnm = s7.put("v_new_by_seq", [TS, NB, P])
        gout, rso = s7.put("gdn_out", [P, T]), s7.put("rs_o", [P, T])
        sqo = rso
        S = s5.put("S", [P, P])
        rr, vn = s5.put("resid", [P, P]), s5.put("v_new", [P, P])
        ks_s, r_s, vn_s = s5.put("ks_sample", [P, TS]), s5.put("resid_s", [TS, P]), s5.put("v_new_s", [TS, P])
        ss = s5.put("S_sample", [P, NB, P])
        s8 = Region(b_scr, n_scr)
        mk, mv = s8.put("mk", [P, T]), s8.put("mv", [P, T])
        qw, prd = s8.put("qw", [P, T]), s8.put("qw_n", [P, T])
        kw, vt = s8.put("kw", [P, 3, P]), s8.put("vt", [P, 3, P + 1])
        md, mpt = s8.put("m_decay", [P, T]), s8.put("m_pt", [P, T])
        emt = s8.put("emt_fw", [P, T + NC])
        ctn = s8.put("ct_n", [P, P + 1])
        so = s8.put("sig_o", [P, T])
        dn, mh = s8.put("den", [P, T]), s8.put("mh", [P, T])
        cs = s8.put("C_sample", [P, NB, P])
        cts_at = s8.at
        cts = s8.put("Ct_sample", [P, NB, P])
        km = nc.alloc_sbuf_tensor_at("kw_by_seq", [TS, NB, P], F32, offset=cts_at)
        cout = s8.put("C_prompt", [P, P])
        mrsel = nc.alloc_sbuf_tensor_at("m_row_sel", [32 + H, 3 * T + NC], F32, offset=cts_at)
        s9 = Region(b_scr, n_scr)
        g_last = s9.put("gdn_last_cols", [P, 12, GPAD * (1 + NB)])
        g_lrow = s9.put("gdn_last_rows", [GPAD * (1 + NB), 3, NG])
        s10 = Region(b_scr, n_scr)
        xg = s10.put("x_group", [P, 3, NG])
        st_rows = s10.put("ffn_old_rows", [NB * FPAD, 2, NG])
        u_out = s10.put("ffn_last_sel", [P, 8, FPAD * (1 + NB)])
        u_lrow = s10.put("ffn_last_rows", [FPAD * (1 + NB), 2, NG])
        ssq, sqt, r2 = s10.put("ssq", [P, T]), s10.put("sq_t", [P, T]), s10.put("r2", [P, T])
        ac = s10.put("act", [P, 2, T])
        fw_rows = s10.put("ffn_w_rows", [2 * FT, FC, P])
        n_out = s10.put("n_rows_out", [NB * H, 2, P])
        e1 = Region(b_e, 2 * H * TB)
        uu = e1.put("u_padded", [P, 4, FW])
        ug, uv = e1.put("u_gate", [P, 4, FV]), e1.put("u_val", [P, 4, FV])
        u_last = e1.put("u_last", [P, 4 * 2 * 4, FPAD * (1 + NB)])
        fcw = e1.put("ffn_conv_w_t", [P, FC, 2 * FT])

        ps = ctx.enter_context(nc.psum_tensor("products", [P, 4, NG], F32))
        pm = ctx.enter_context(nc.psum_tensor("mixer", [P, 4, NG], F32))
        bo, bw, bu = pm[:, 3], ps[:, 2], ps[:, 3]

        def sem(name):
            return ctx.enter_context(nc.semaphore(name))

        landed = [sem(f"unit_landed_{s}") for s in range(4)]
        hi_ready, lo_ready = sem("block_hi_ready"), sem("block_lo_ready")
        blocks, bank_free = sem("blocks_multiplied"), sem("bank_free")
        x_in, rows_in, small_in = sem("x_rows_in"), sem("const_rows_in"), sem("small_w_in")
        consts = sem("constants_made")
        x_in2, old_in, ss_in, cs_in = sem("x_group_in"), sem("ffn_old_rows_in"), sem("S_in"), sem("C_in")
        fw_in = sem("ffn_w_rows_in")
        stored, ss_out, cs_out = sem("outputs_stored"), sem("S_stored"), sem("C_stored")
        lrow_out, y_out = sem("last_rows_stored"), sem("y_stored")

        st_a = Steps(sem("start_act"), "sq0 sq1 sq2 lnp lns expp exps " + " ".join(f"hi{f}" for f in range(KT)) + " smhi")
        st_d = Steps(sem("start_dve"), "xs0 xs1 xs2 cw nw ns old0 old1 old2 " + " ".join(f"lo{f}" for f in range(KT)) + " smlo")
        st_t = Steps(sem("start_pe"), "consts old " + " ".join(f"x{f}" for f in range(KT)) + " small")

        LEVELS = range(1, NLEV)
        prep_a = Steps(sem("prep_act"), "c0 c1 c2 sg1 sg2 sg3 rn1 rn2 eg egp egs d1 d2 kg0 kg1 kg2 x0a x0b psb1s "
                       + " ".join(f"psb{l}" for l in LEVELS))
        prep_d = Steps(sem("prep_dve"), "rsel " + " ".join(f"cv{t}{j}" for j in range(1, GC) for t in range(3))
                       + " clampz qkv1 qkv2 k q rselb ke qe d0 d1 d2 bv0 bv1 bv2 bd1 bd2 at1 at2 pt1 pt2 n0a n0b xt1 xt2 n1a n1b xx1s "
                       + " ".join(f"xx{l} n{l + 1}" for l in LEVELS[:-1]) + " xx5")
        prep_p = Steps(sem("prep_pool"), "clamp zz sq")
        prep_t = Steps(sem("prep_pe"), "norm tr kk kq beta x0 " + " ".join(f"p{l} xx{l}" for l in LEVELS))
        scan_a = Steps(sem("scan_act"), "vn0 vn1 ks_s vn_s vn2 vn3 sqo rs1 rs2 hi")
        scan_d = Steps(sem("scan_dve"), "S0 R1 S1 rs R2 S2 R3 S3 go ss1 ss2 lo")
        scan_p = Steps(sem("scan_pool"), "vnm sse goz")
        scan_t = Steps(sem("scan_pe"), "T0 u0 k1 T1 ksS u1 trS k2 TS T2 oS u2 k3 T3 u3 Ss1 nrm Ss2")
        ma = Steps(sem("mlstm_act"), "so1 so2 so3 kw0 kw1 kw2 d1 d2 emt v0 v1 v2 ct0 ct1 abs hi cp")
        md_ = Steps(sem("mlstm_dve"), "so sel k v D0 D1 D2 qw prs pt1 pt2 C0 pr1 C1 pr2 C2 pr3 C3 np ns ns2 mx rc h ho cs1 cs2 lo")
        mp = Steps(sem("mlstm_pool"), "km cs")
        mt = Steps(sem("mlstm_pe"), "rows ktr vtr kq c0 u0 c1 u1 u2 u3 ns so C cp")
        gate_a = Steps(sem("gates_act"), "expA abs exp ln beta er wi emt fw sw")
        gate_d = Steps(sem("gates_dve"), "ga gb mf mi sp g lf "
                       + " ".join(f"s{k}a s{k}b s{k}c" + (f" s{k}d" if k < 2 else "") for k in range(6)) + " G gl1 gl2 c "
                       + " ".join(f"x{k}a x{k}b x{k}c" + (f" x{k}d" if k < 2 else "") for k in range(6))
                       + " bl1 bl2 cl1 cl2 emc z0 m0 n0 m1 n1 m2 n2 m3 ms1 ms2 mm1 mm2 negmx wi1 wi2 emt fw1 fw2"
                       " sw0 sw1 sw2 colsA colsB nbA nbB")
        gate_t = Steps(sem("gates_pe"), "cols")
        lst_p = Steps(sem("last_pool"), "a b")
        lst_t = Steps(sem("last_pe"), "tr")
        lst_a = Steps(sem("last_act"), "r0 r1 r2")
        no_t, no_a = Steps(sem("n_pe"), "tr"), Steps(sem("n_act"), "s p")
        br_a = Steps(sem("branch_act"), "sa0 sa1 sb0 sb1 hi0 hi1 sa2 sa3 sb2 sb3 hi2 hi3")
        vt_ones, uu_zero = sem("vt_ones_set"), sem("u_pads_zero")
        br_d = Steps(sem("branch_dve"), "s0 s1 lo0 lo1 s2 s3 lo2 lo3")
        ot_t = Steps(sem("out_pe"), "x0 x1 x2 x3")
        ot_a = Steps(sem("out_act"), "x0 x1 x2 x3 hi0 hi1 hi2 hi3")
        ot_d = Steps(sem("out_dve"), "lo0 lo1 lo2 lo3")
        ot_p = Steps(sem("out_pool"), "s0 a0 s1 a1 s2 a2 s3 a3")
        n2_t, n2_a = Steps(sem("norm2_pe"), "w sum"), Steps(sem("norm2_act"), "ln exp")
        n2_d = Steps(sem("norm2_dve"), "w")
        up_t = Steps(sem("up_pe"), "old0 old1")
        up_d = Steps(sem("up_dve"), "og " + " ".join(f"g{m} gc{m}a gc{m}b" for m in range(4)) + " ov "
                     + " ".join(f"v{m} vc{m}a vc{m}b ac{m}a ac{m}b lo{m}" for m in range(4)))
        up_a = Steps(sem("up_act"), " ".join(f"g{m} sg{m}" for m in range(4)) + " "
                     + " ".join(f"v{m} hi{m}" for m in range(4)))
        up_p = Steps(sem("up_pool"), "g1 g2 v1 v2")
        dn_p = Steps(sem("down_pool"), "sel")
        dn_t = Steps(sem("down_pe"), "tr")
        dn_a = Steps(sem("down_act"), "r0 r1")
        fin_p = Steps(sem("final_pool"), "sq add")
        y_t, y_a = Steps(sem("y_pe"), "sum t0 t1 t2 t3"), Steps(sem("y_act"), "ln exp r0 r1 r2 r3")
        y_d = Steps(sem("y_dve"), " ".join(f"y{f}" for f in range(KT)))

        def seqs(ap, step, lo, hi):
            return ap.rearrange("p (b s) -> p b s", s=step)[:, :, lo:hi]

        def seqs3(ap, step, lo, hi):
            return ap.rearrange("p t (b s) -> p t b s", s=step)[:, :, :, lo:hi]

        def spaced(ap, step):
            return bass.AP(tensor=ap.tensor, offset=ap.offset, ap=list(ap.ap)[:-1] + [[step, NB], [1, L]])

        def one(t, i):
            return t[:, bass.ds(i, 1)].rearrange("p a t -> p (a t)")

        def apart(eng):
            eng.nop(nofuse=True)

        def freed(g, m):
            return bank_free, 4 * g + (m + 5)

        block = ctx.enter_context(nc.Block())

        @block.sync
        def _(sp):
            def unit(src, k, nk, n, q, s, first=False):
                if not first:
                    sp.wait_ge(lo_ready, 16 * q + 4 * s - 12)
                sp.dma_start(raw[:, s, 0:nk], src[:, k:k + nk, bass.ds(n, P)]).then_inc(landed[s], 16)

            def quad(src, n, q, k=0, first=False):
                for s in range(4):
                    unit(src, k, KT, n + s * P, q, s, first)

            sp.dma_start(x_rows[:, 0:2], xp_rows).then_inc(x_in, 16)
            sp.dma_start(x_rows[0:TS, 2], xs_rows).then_inc(x_in, 16)
            quad(w_in, 0, 0, first=True)
            with sp.Fori(1, 8) as i:
                quad(w_in, NG * i, i)
            def half_slots(n, q, units=range(4)):
                for s in units:
                    sp.wait_ge(lo_ready, 16 * q + (4 * s - 4))
                    sp.dma_start(raw[:, s % 2], w_in[:, :, bass.ds(n + s * P, P)]).then_inc(landed[s], 16)

            with sp.Fori(0, 6) as i:
                half_slots(NG * i + c_mqkv, i + q_heads)
            with sp.Fori(0, 2) as i:
                half_slots(NG * i + c_mo, i + (q_heads + 6))
            half_slots(c_gate, q_gate, range(2))
            for steps in (scan_a, scan_d, scan_p, scan_t):
                sp.wait_ge(*steps.before(H))
            for s in range(2, 4):
                unit(w_in, 0, KT, c_gate + s * P, q_gate, s)
            with sp.Fori(1, 8) as i:
                quad(w_in, NG * i + c_gate, i + q_gate)
            with sp.Fori(0, 4) as i:
                for s in range(4):
                    sp.wait_ge(lo_ready, 16 * (i + q_branch) + (4 * s - 12))
                    sp.dma_start(raw[:, s].rearrange("p (k c) n -> p k (c n)", c=2),
                                 (w_ba, w_bb)[s % 2][:, :, bass.ds(NG * i + 2 * P * (s // 2), 2 * P)]).then_inc(landed[s], 16)

            def x_group(i):
                sp.dma_start(xg[:, 0:2], xp_rows[:, :, bass.ds(i * NG, NG)]).then_inc(x_in2, 16)
                sp.dma_start(xg[0:TS, 2], xs_rows[:, bass.ds(i * NG, NG)]).then_inc(x_in2, 16)

            sp.wait_ge(*md_.before(H))
            sp.wait_ge(cs_out, 32 * H)
            sp.wait_ge(*mt.before(H))
            sp.wait_ge(*ma.before(H))
            sp.dma_start(fw_rows[:], a["ffn_conv_w"][0].rearrange("j (t p) -> t j p", p=P)).then_inc(fw_in, 16)
            with sp.Fori(0, 4) as i:
                sp.wait_ge(*ot_t.before(i))
                x_group(i)
                quad(w_out, NG * i, i + q_out)
            q, first_group = q_ffn, 0
            old = a["state_ffn_conv"][0].rearrange("b j n -> (b j) n")
            for c, n in enumerate(CHUNKS):
                with sp.Fori(0, n) as i:
                    for half in range(2):
                        n0 = (i + first_group) * NG + half * FT * P
                        sp.wait_ge(*up_t.before(i + first_group))
                        sp.dma_start(st_rows[:, half], old[:, bass.ds(n0, NG)]).then_inc(old_in, 16)
                        quad(w_up, n0, 2 * i + q + half)
                q += 2 * n
                if n == 4:
                    with sp.Fori(0, 4) as i:
                        quad(w_down, NG * i, i + q, 4 * first_group)
                else:
                    for u in range(KT):
                        sp.wait_ge(lo_ready, 16 * q + (4 * u - 12 if u < 4 else n * (u - 3)))
                        sp.dma_start(raw[:, u % 4, 0:4 * n], w_down[:, 4 * first_group:4 * (first_group + n), u * P:(u + 1) * P])\
                            .then_inc(landed[u % 4], 16)
                q += n
                first_group += n
            sp.wait_ge(stored, 16 * N_STORED)
            sp.wait_ge(ss_out, 32 * H)
            sp.wait_ge(cs_out, 32 * H)
            sp.wait_ge(lrow_out, 16 * N_LROW)
            sp.wait_ge(y_out, 16 * 8)

        TAIL = CHUNKS[-1]

        def ring_slot(first, second, n, ring):
            n %= ring
            return first[:, n] if n < 4 else second[:, n - 4]

        def where(n, tail, tail_next):
            if tail:
                return n // TAIL // 4, n // TAIL % 4, n % TAIL
            if tail_next and n >= 16:
                dq, s, j = where(n - 16, True, False)
                return dq + 1, s, j
            return n // 16, n % 16 // 4, n % 4

        def split_hi(q, n, ring, tail=False, tail_next=False, slots=4):
            if tail and n >= KT * TAIL:
                return
            dq, s, j = where(n, tail, tail_next)
            nc.scalar.wait_ge(landed[s], 16 * (q + dq + 1))
            nc.scalar.wait_ge(blocks, 16 * q + (n - ring + 1))
            nc.scalar.activation(ring_slot(whi, whi2, n, ring), raw[:, s % slots, 4 * j:4 * j + 4], ACT.Copy).then_inc(hi_ready, 1)

        def split_lo(q, n, ring, tail=False, tail_next=False, slots=4):
            if tail and n >= KT * TAIL:
                return
            dq, s, j = where(n, tail, tail_next)
            nc.vector.wait_ge(hi_ready, 16 * q + (n + 1))
            nc.vector.tensor_tensor(ring_slot(wlo, wlo2, n, ring), raw[:, s % slots, 4 * j:4 * j + 4],
                                    ring_slot(whi, whi2, n, ring).bitcast(F32), ALU.subtract).then_inc(lo_ready, 1)

        def group(split, q, points=(), mixer=None, stages=0, ring=4, b0=0, n=16, **tail):
            for b in range(n):
                split(q, b0 + b + ring - 1, ring, **tail)
                for at, work in points:
                    if min(at + 1, n - 1) == b:
                        work()
                for _ in range((b + 1) * stages // n - b * stages // n):
                    next(mixer, None)
            for _ in mixer or ():
                pass

        def nothing(m, done):
            pass

        def repeat(eng, n, body, peel):
            with eng.Fori(0, n - 1 if peel else n) as i:
                body(i, False)
            if peel:
                body(n - 1, True)

        def beside(scan=iter(()), prep=iter(()), pace=GDN_PACE):
            for order in pace:
                for c in order:
                    next(scan if c == "s" else prep, None)
                yield 0
            for rest in (scan, prep):
                for _ in rest:
                    pass

        def two_before(eng, h):
            if isinstance(h, int) and h == 0:
                return
            for steps in (scan_a, scan_d, scan_p, scan_t):
                eng.wait_ge(*steps.before(h - 1))
            eng.wait_ge(lo_ready, 16 * q_heads)

        def heads(eng, body):
            with eng.Fori(0, H // 2 - 1) as i:
                for k in range(2):
                    body(2 * i + k, k)
            for k in range(2):
                body(H - 2 + k, k)

        def column_tiles(*works, n=4):
            return [(n * m + n - 1 + k, lambda m=m, w=w: w(m, n * (m + 1))) for m in range(4) for k, w in enumerate(works)]

        @block.gpsimd
        def _(pool):
            made = [0]

            def done(instruction):
                made[0] += 1
                instruction.then_inc(consts, 1)
                pool.wait_ge(consts, made[0])

            def keep(t, pattern, base, channel, fill=0.0, op=ALU.is_ge):
                done(pool.affine_select(out=t, in_=t, compare_op=op, fill=fill, base=base,
                                        pattern=pattern, channel_multiplier=channel))

            done(pool.memset(eps[:], EPS))
            done(pool.memset(ident[:], 0.0))
            keep(ident[:], [[-1, P]], 0, 1, 1.0, ALU.not_equal)
            done(pool.memset(ones[:], 1.0))
            done(pool.memset(sm_raw[:], 0.0))
            pool.dma_start(sm_raw[:, :, 0:H], w_in[:, :, c_ga:c_ga + H]).then_inc(small_in, 16)
            pool.dma_start(sm_raw[:, :, 32:32 + H], w_in[:, :, c_gb:c_gb + H]).then_inc(small_in, 16)
            pool.dma_start(sm_raw[:, :, 64:64 + H], w_in[:, :, c_mi:c_mi + H]).then_inc(small_in, 16)
            pool.dma_start(sm_raw[:, :, 96:96 + H], w_in[:, :, c_mf:c_mf + H]).then_inc(small_in, 16)
            done(pool.memset(gq[:, :, 0:GPAD], 0.0))
            for m, n, b in ((incl, P, CH), (incl_s, TS, L)):
                done(pool.memset(m[:], 0.0))
                keep(m[:], [[1, n]], 0, -1, NEG)
                view = m[:].rearrange("j (b t) -> j b t", t=b)
                keep(view, [[-b, n // b], [0, b]], 0, 1, NEG)
            for k in range(NLEV):
                s = 1 << k
                done(pool.memset(lev[:, k], 0.0))
                half = lev[:, k].rearrange("j (b h t) -> j b h t", h=2, t=s)[:, :, 1]
                done(pool.memset(half, 1.0))
                keep(half, [[-2 * s, P // (2 * s)], [0, s]], 0, 1)
                keep(half, [[2 * s, P // (2 * s)], [0, s]], s - 1, -1)
            done(pool.memset(seq[:], 1.0))
            keep(seq[:], [[-L, NB]], 0, 1)
            keep(seq[:], [[L, NB]], L - 1, -1)
            assert made[0] == N_CONST

            pool.wait_ge(*freed(5, 3))
            pool.wait_ge(*gate_d.after("nbB"))
            pool.wait_ge(stored, 32)
            with pool.Fori(0, 2) as i:
                pool.wait_ge(*lst_t.before(i))
                pool.tensor_copy(g_last[:, :, 0:GPAD], gq[:, bass.ds(i * 12, 12), TP:TP + GPAD]).then_inc(*lst_p.done("a"))
                pool.tensor_copy(g_last[:, :, GPAD:].rearrange("p t (b s) -> p t b s", s=GPAD),
                                 seqs3(gq[:, bass.ds(i * 12, 12), GPAD + TP:], GS, L, GS)).then_inc(*lst_p.done("b"))

            def prepare(h):
                pool.wait_ge(*prep_d.after(f"cv2{GC - 1}", h))
                pool.wait_ge(*prep_a.before(h))
                apart(pool)
                pool.tensor_scalar(sg[:, 0:3 * GV], cv[:], SIG_MIN, None, ALU.max).then_inc(*prep_p.done("clamp"))
                z_t = one(zm, h + 3 * H)
                pool.wait_ge(*prep_a.after("sg3", h))
                apart(pool)
                pool.tensor_tensor(z_t, z_t, sg[:, 3 * GV:], ALU.mult).then_inc(*prep_p.done("zz"))
                pool.wait_ge(*prep_d.after("qkv2", h))
                pool.wait_ge(*prep_p.after("zz", h))
                pool.tensor_tensor(sq[:], qkv[:, 0:2], qkv[:, 0:2], ALU.mult).then_inc(*prep_p.done("sq"))

            def scan(h, par):
                ec = handed[par][-1]
                pool.wait_ge(*scan_a.after("vn_s", h))
                pool.wait_ge(lo_ready, 16 * q_heads)
                pool.tensor_tensor(vnm[:], vn_s[:].unsqueeze(1).to_broadcast([TS, NB, P]),
                                   seq[:].unsqueeze(2).to_broadcast([TS, NB, P]), ALU.mult).then_inc(*scan_p.done("vnm"))
                pool.wait_ge(*scan_t.after("oS", h))
                pool.tensor_tensor(ss[:], ss[:], ec[:, NCH:].unsqueeze(2).to_broadcast([P, NB, P]), ALU.mult)\
                    .then_inc(*scan_p.done("sse"))
                pool.wait_ge(*scan_d.after("go", h))
                apart(pool)
                pool.tensor_tensor(gout[:], gout[:], one(zm, h + 3 * H), ALU.mult).then_inc(*scan_p.done("goz"))

            prepare(0)

            def head(j, par):
                if not (isinstance(j, int) and j == H - 1):
                    prepare(j + 1)
                scan(j, par)
            heads(pool, head)

            with pool.Fori(0, H) as i:
                pool.wait_ge(*mt.after("so", i))
                pool.tensor_tensor(km[:], kw[0:TS, 2].unsqueeze(1).to_broadcast([TS, NB, P]),
                                   seq[:].unsqueeze(2).to_broadcast([TS, NB, P]), ALU.mult).then_inc(*mp.done("km"))
                pool.tensor_tensor(cs[:], cs[:], emt[:, T + NCH:].unsqueeze(2).to_broadcast([P, NB, P]),
                                   ALU.mult).then_inc(*mp.done("cs"))

            pool.wait_ge(*md_.before(H))
            pool.wait_ge(*mt.before(H))
            pool.wait_ge(cs_out, 32 * H)
            pool.memset(ssq[:], 0.0).then_inc(consts, 1)
            pool.wait_ge(consts, N_CONST + 1)

            def add_square(steps, tile, r, names, y_done):
                pool.wait_ge(*y_done)
                t = x2[:, tile].rearrange("p a t -> p (a t)")
                pool.tensor_tensor(sqt[:], t, t, ALU.mult).then_inc(*steps.done(names[0]))
                pool.wait_ge(*steps.after(names[0], r))
                pool.tensor_tensor(ssq[:], ssq[:], sqt[:], ALU.add).then_inc(*steps.done(names[1]))
                pool.wait_ge(*steps.after(names[1], r))

            with pool.Fori(0, 4) as i:
                for m in range(4):
                    add_square(ot_p, bass.ds(4 * i + m, 1), i, (f"s{m}", f"a{m}"), freed(i + g_out, m))
            g, g0 = g_ffn, 0
            for c, n in enumerate(CHUNKS):
                with pool.Fori(0, n) as i:
                    r = i + g0
                    pool.wait_ge(*dn_t.before(4 * c))
                    for half, name in enumerate("gv"):
                        pool.wait_ge(*freed(2 * i + (g + half), 3))
                        u_t = u_last[:, bass.ds(8 * i + 4 * half, 4)]
                        pool.tensor_copy(u_t[:, :, 0:FPAD], uu[:, :, TP:TP + FPAD]).then_inc(*up_p.done(f"{name}1"))
                        pool.tensor_copy(u_t[:, :, FPAD:].rearrange("p t (b s) -> p t b s", s=FPAD),
                                         seqs3(uu[:, :, FPAD + TP:], FS, L, FS)).then_inc(*up_p.done(f"{name}2"))
                g, g0 = g + 2 * n, g0 + n
                if c == 0:
                    pool.wait_ge(*n2_t.after("sum"))
                    pool.memset(ssq[:], 0.0).then_inc(consts, 1)
                    pool.wait_ge(consts, N_CONST + 2)
                if n == 4:
                    with pool.Fori(0, 4) as i:
                        pool.wait_ge(*up_p.before(g0))
                        pool.wait_ge(*dn_t.before(i + 4 * c))
                        pool.tensor_copy(u_out[:], u_last[:, bass.ds(8 * i, 8)]).then_inc(*dn_p.done("sel"))
                    g += 4
                else:
                    for i in range(4):
                        if i < n:
                            pool.wait_ge(*up_p.before(g0))
                            pool.wait_ge(*dn_t.before(i + 4 * c))
                            pool.tensor_copy(u_out[:], u_last[:, 8 * i:8 * i + 8]).then_inc(*dn_p.done("sel"))
                        for m in range(4):
                            add_square(fin_p, bass.ds(4 * i + m, 1), 4 * i + m, ("sq", "add"), freed(g + i, m))

        @block.scalar
        def _(act):
            nc.scalar.preload_act_table_set(EXP_LN)
            act.dma_start(norm_rows[0:KT], a["norm_mix_w"][0].rearrange("(k p) -> k p", p=P)).then_inc(rows_in, 16)
            act.dma_start(norm_rows[KT:2 * KT], a["norm_ffn_w"][0].rearrange("(k p) -> k p", p=P)).then_inc(rows_in, 16)
            act.dma_start(norm_rows[2 * KT:3 * KT], a["norm_final_w"][0].rearrange("(k p) -> k p", p=P)).then_inc(rows_in, 16)
            act.dma_start(w_rows[:], a["gdn_conv_w"][0].rearrange("j (t p) -> (j t) p", p=P)).then_inc(rows_in, 16)
            act.dma_start(n_rows[:], a["state_ml_n"][0].rearrange("b h k -> (b h) k")).then_inc(rows_in, 16)
            act.dma_start(conv_rows[:], a["state_gdn_conv"][0].rearrange("b j n -> (b j) n")).then_inc(rows_in, 16)
            act.dma_start(wgn[:], a["gdn_norm_w"].rearrange("a p -> p a")).then_inc(rows_in, 16)

            act.wait_ge(x_in, 32)
            act.wait_ge(consts, 1)
            for c, (n, name) in enumerate(((P, "sq0"), (P, "sq1"), (TS, "sq2"))):
                squares = (h_hi, h_lo)[c // 2][0:n].rearrange("p k t -> p (k t)")
                nc.scalar.activation(squares[:, c % 2 * D:(c % 2 + 1) * D], x_rows[0:n, c], ACT.Square,
                                     accum_out=rstd[0:n, c:c + 1]).then_inc(*st_a.done(name))
            for name, src, n, cc in (("lnp", "sq1", P, slice(0, 2)), ("lns", "sq2", TS, slice(2, 3))):
                act.wait_ge(*st_a.after(src))
                nc.scalar.activation(rstd[0:n, cc], rstd[0:n, cc], ACT.Ln, bias=eps[0:n], scale=1.0 / D)\
                    .then_inc(*st_a.done(name))
            for name, src, n, cc in (("expp", "lnp", P, slice(0, 2)), ("exps", "lns", TS, slice(2, 3))):
                act.wait_ge(*st_a.after(src))
                nc.scalar.activation(rstd[0:n, cc], rstd[0:n, cc], ACT.Exp, scale=-0.5).then_inc(*st_a.done(name))
            act.wait_ge(*st_d.after("nw"))
            for f in range(KT):
                act.wait_ge(*st_t.after(f"x{f}"))
                nc.scalar.activation(h_hi[:, f], ps[:, f % 4, 0:T], ACT.Copy, scale=wn[:, 0, f:f + 1])\
                    .then_inc(*st_a.done(f"hi{f}"))

            for b in range(3):
                act.wait_ge(landed[0], 16)
                nc.scalar.activation(whi[:, b], raw[:, 0, 4 * b:4 * b + 4], ACT.Copy).then_inc(hi_ready, 1)

            def gates_rows():
                act.wait_ge(small_in, 64)
                nc.scalar.activation(sm_hi[:], sm_raw[:], ACT.Copy).then_inc(*st_a.done("smhi"))
                yield 0
                act.wait_ge(*st_t.after("small"))
                act.dma_start(hcol[:, 0:1], a["gdn_A_log"].rearrange("a h -> h a")).then_inc(rows_in, 16)
                act.dma_start(hcol[:, 1:2], a["gdn_dt_bias"].rearrange("a h -> h a")).then_inc(rows_in, 16)
                act.dma_start(hcol[:, 2:3], a["ml_b_i"].rearrange("a h -> h a")).then_inc(rows_in, 16)
                act.dma_start(hcol[:, 3:4], a["ml_b_f"].rearrange("a h -> h a")).then_inc(rows_in, 16)
                act.dma_start(m_in[:, NCH:], a["state_ml_m"][0].rearrange("b h -> h b"), allow_slow_non_contiguous=True).then_inc(rows_in, 16)
                yield from range(1, 3)
                act.wait_ge(consts, N_CONST)
                act.wait_ge(rows_in, 16 * 12)
                nc.scalar.activation(hcol[:, 4:5], hcol[:, 0:1], ACT.Exp).then_inc(*gate_a.done("expA"))
                act.wait_ge(*gate_d.after("mf"))
                nc.scalar.activation(sp_out[:], sp_in[:], ACT.Abs).then_inc(*gate_a.done("abs"))
                act.wait_ge(*gate_a.after("abs"))
                nc.scalar.activation(sp_out[:], sp_out[:], ACT.Exp, scale=-1.0).then_inc(*gate_a.done("exp"))
                act.wait_ge(*gate_a.after("exp"))
                nc.scalar.activation(sp_out[:], sp_out[:], ACT.Ln, bias=1.0).then_inc(*gate_a.done("ln"))
                yield from range(2)
                act.wait_ge(*gate_d.after("sp"))
                nc.scalar.activation(g_row[:, 1], sp_out[:, 1], ACT.Exp, scale=-1.0).then_inc(*gate_a.done("beta"))
                yield from range(2, 9)
                act.wait_ge(*gate_d.after("gl2"))
                nc.scalar.activation(e_row[:], e_row[:], ACT.Exp).then_inc(*gate_a.done("er"))
                yield from range(9, 18)
                act.wait_ge(*gate_d.after("wi2"))
                nc.scalar.activation(m_row[:, T:2 * T], sw_row[:], ACT.Exp).then_inc(*gate_a.done("wi"))
                yield 18
                act.wait_ge(*gate_d.after("emt"))
                nc.scalar.activation(m_row[:, 2 * T:3 * T], ig[:], ACT.Exp, scale=-1.0).then_inc(*gate_a.done("emt"))
                act.wait_ge(*gate_d.after("fw2"))
                nc.scalar.activation(m_row[:, 3 * T:], f_row[:], ACT.Exp).then_inc(*gate_a.done("fw"))
                act.wait_ge(*gate_d.after("sw2"))
                nc.scalar.activation(cmx[0][:], cmx[0][:], ACT.Exp).then_inc(*gate_a.done("sw"))
                act.dma_start(o["p_m"].rearrange("a b h -> h (a b)"), m_new[:, NCH - 1:NCH]).then_inc(stored, 16)
                act.dma_start(o["s_m"][0].rearrange("b h -> h b"), m_new[:, NCH:], allow_slow_non_contiguous=True).then_inc(stored, 16)


            def quad(i, mixer=None):
                def evacuate(m, done):
                    act.wait_ge(blocks, 16 * (i) + done)
                    t = one(gq, 4 * i + m)
                    nc.scalar.activation(t[:, GPAD:GPAD + TP], ps[:, m, 0:TP], ACT.Copy)
                    nc.scalar.activation(seqs(t[:, GPAD + TP:], GS, GPAD, GS),
                                         ps[:, m, TP:T].rearrange("p (b s) -> p b s", s=L), ACT.Copy).then_inc(bank_free, 1)
                group(split_hi, i, column_tiles(evacuate), mixer, GATE_STAGES // 2 if mixer else 0)

            gates_mixer = gates_rows()
            quad(0, islice(gates_mixer, GATE_STAGES // 2))
            quad(1, gates_mixer)
            with act.Fori(2, 6) as i:
                quad(i)

            def last_rows():
                for i in range(2):
                    yield 0
                    act.wait_ge(*lst_t.after("tr", i))
                    act.wait_ge(lrow_out, 32 * i)
                    for b in range(3):
                        nc.scalar.activation(g_lrow[:, b], pm[0:GPAD * (1 + NB), b], ACT.Copy).then_inc(*lst_a.done(f"r{b}"))
                    act.wait_ge(*lst_a.after("r2", i))
                    n = 3 * NG
                    act.dma_start(o["p_gconv"][0, 0][:, i * n:i * n + n],
                                  g_lrow[0:GPAD].rearrange("r b n -> r (b n)")).then_inc(lrow_out, 16)
                    act.dma_start(o["s_gconv"][0].rearrange("b j n -> (b j) n")[:, i * n:i * n + n],
                                  g_lrow[GPAD:].rearrange("r b n -> r (b n)")).then_inc(lrow_out, 16)
                    yield 1

            def prepare(h, par):
                qe, ke, pt, kg, bv, xx, ec = handed[par]
                act.wait_ge(lrow_out, 64)
                act.wait_ge(*prep_d.before(h))
                act.wait_ge(*prep_p.before(h))
                act.wait_ge(*prep_t.before(h))
                for t in range(3):
                    nc.scalar.activation(cv[:, t * GV:(t + 1) * GV], one(gq, h + t * H)[:, 0:GV], ACT.Copy,
                                         scale=gcw[:, 0, bass.ds(h + t * H, 1)]).then_inc(*prep_a.done(f"c{t}"))
                yield 0
                yield from range(2)
                act.wait_ge(*prep_d.after("clampz", h))
                act.wait_ge(*prep_p.after("clamp", h))
                nc.scalar.activation(sg[:], sg[:], ACT.Exp, scale=-1.0).then_inc(*prep_a.done("sg1"))
                yield 3
                act.wait_ge(*prep_a.after("sg1", h))
                nc.scalar.activation(sg[:], sg[:], ACT.Ln, bias=1.0).then_inc(*prep_a.done("sg2"))
                yield 4
                act.wait_ge(*prep_a.after("sg2", h))
                nc.scalar.activation(sg[:], sg[:], ACT.Exp, scale=-1.0).then_inc(*prep_a.done("sg3"))
                yield 1
                yield 2
                act.wait_ge(*prep_t.after("norm", h))
                act.wait_ge(*prep_p.after("sq", h))
                nc.scalar.activation(rn[:], pm[:, 0:2, 0:T], ACT.Ln, bias=eps[:]).then_inc(*prep_a.done("rn1"))
                act.wait_ge(*prep_a.after("rn1", h))
                nc.scalar.activation(rn[:], rn[:], ACT.Exp, scale=-0.5).then_inc(*prep_a.done("rn2"))
                nc.scalar.activation(eg[:], pm[:, 2, 0:T], ACT.Exp).then_inc(*prep_a.done("eg"))
                two_before(act, h)
                nc.scalar.activation(ec[:, 0:NCH].unsqueeze(2), pm[:, 2, 0:TP].rearrange("p (n t) -> p n t", t=CH)[:, :, CH - 1:],
                                     ACT.Exp).then_inc(*prep_a.done("egp"))
                nc.scalar.activation(ec[:, NCH:].unsqueeze(2), seqs(pm[:, 2, TP:T], L, L - 1, L), ACT.Exp)\
                    .then_inc(*prep_a.done("egs"))
                act.wait_ge(*prep_d.after("d2", h))
                nc.scalar.activation(dec[:, 0:TP], dec[:, 0:TP], ACT.Exp).then_inc(*prep_a.done("d1"))
                nc.scalar.activation(dec[0:TS, TP:T], dec[0:TS, TP:T], ACT.Exp).then_inc(*prep_a.done("d2"))
                yield 3
                act.wait_ge(*prep_t.after("tr", h))
                for n, _, c in PARTS:
                    nc.scalar.activation(kg[0:n, c], pm[0:n, 0, c * P:(c + 1) * P], ACT.Copy,
                                         scale=cols[0:n, 2, c, bass.ds(h, 1)]).then_inc(*prep_a.done(f"kg{c}"))
                yield 4
                yield 5
                act.wait_ge(*prep_t.after("x0", h))
                nc.scalar.activation(xx[:, 0, 0:TP], pm[:, 1, 0:TP], ACT.Copy).then_inc(*prep_a.done("x0a"))
                nc.scalar.activation(xx[0:TS, 0, TP:T], pm[0:TS, 1, TP:T], ACT.Copy).then_inc(*prep_a.done("x0b"))
                yield 6
                for l in LEVELS:
                    act.wait_ge(*prep_t.after(f"p{l}", h))
                    if l == 1:
                        nc.scalar.activation(psb[0:TS, TP:T], pm[0:TS, 2, TP:T], ACT.Copy).then_inc(*prep_a.done("psb1s"))
                    nc.scalar.activation(psb[:, 0:TP], pm[:, 2, 0:TP], ACT.Copy).then_inc(*prep_a.done(f"psb{l}"))
                    yield 2 * l + 5
                    yield 2 * l + 6

            def scan(h, par):
                act.wait_ge(lo_ready, 16 * q_heads)
                act.wait_ge(*scan_d.before(h))
                act.wait_ge(*scan_t.before(h))
                yield 0

                def v_new(n):
                    lo = CH * (n % 2)
                    act.wait_ge(*scan_t.after(f"T{n}", h))
                    nc.scalar.activation(vn[lo:lo + CH], bw[lo:lo + CH, 0:P], ACT.Copy).then_inc(*scan_a.done(f"vn{n}"))

                v_new(0)
                yield 1
                act.wait_ge(ss_out, 32 * h)
                act.wait_ge(*scan_p.before(h))
                act.dma_start(ss[:], a["state_gdn_S"][0][:, bass.ds(h, 1)].rearrange("b a k v -> k (b a) v")).then_inc(ss_in, 16)
                yield from range(2, 4)
                v_new(1)
                act.wait_ge(*scan_t.after("ksS", h))
                nc.scalar.activation(ks_s[:], bu[:, 2 * P:2 * P + TS], ACT.Copy).then_inc(*scan_a.done("ks_s"))
                yield 4
                yield 5
                act.wait_ge(*scan_t.after("TS", h))
                nc.scalar.activation(vn_s[:], bu[0:TS, P:2 * P], ACT.Copy).then_inc(*scan_a.done("vn_s"))
                yield 6
                v_new(2)
                yield from range(7, 10)
                v_new(3)
                yield 10
                act.wait_ge(*scan_t.after("u3", h))
                nc.scalar.activation(sqo[:], bo[:, 0:T], ACT.Square).then_inc(*scan_a.done("sqo"))
                yield 11
                act.wait_ge(*scan_t.after("nrm", h))
                nc.scalar.activation(rso[:], bu[:, 0:T], ACT.Ln, bias=eps[:], scale=1.0 / P).then_inc(*scan_a.done("rs1"))
                act.wait_ge(*scan_a.after("rs1", h))
                nc.scalar.activation(rso[:], rso[:], ACT.Exp, scale=-0.5).then_inc(*scan_a.done("rs2"))
                yield 12
                yield 13
                act.wait_ge(*scan_p.after("goz", h))
                nc.scalar.activation(one(go_hi, h), gout[:], ACT.Copy).then_inc(*scan_a.done("hi"))
                act.wait_ge(*scan_d.after("ss2", h))
                act.dma_start(o["p_S"][0, 0][bass.ds(h, 1)].rearrange("a k v -> k (a v)"), S[:]).then_inc(ss_out, 16)
                act.dma_start(o["s_S"][0][:, bass.ds(h, 1)].rearrange("b a k v -> k (b a) v"), ss[:]).then_inc(ss_out, 16)

            for i, mixer, stages in ((0, last_rows(), 4), (1, beside(prep=prepare(0, 0), pace=GDN_FIRST_PACE), 16)):
                def evacuate(m, done):
                    act.wait_ge(blocks, 16 * (i + q_z) + done)
                    nc.scalar.activation(one(zm, 4 * i + (m + 3 * H)), ps[:, m, 0:T], ACT.Copy).then_inc(bank_free, 1)
                group(split_hi, i + q_z, column_tiles(evacuate), mixer, stages)

            def head(j, par):
                def evacuate(m, done):
                    act.wait_ge(blocks, 16 * (j + q_heads) + done)
                    if isinstance(j, int):
                        act.wait_ge(*scan_p.after("goz", 4 * (j - H + 2) + m))
                    nc.scalar.activation(one(zm, 4 * j + m), ps[:, m % 2, 0:T], ACT.Copy).then_inc(bank_free, 1)
                points, late, last = column_tiles(evacuate), (), isinstance(j, int) and j == H - 1
                if last:
                    points, late = points[:-1], points[-1:]
                mixer = beside(scan(j, par), iter(()) if last else prepare(j + 1, 1 - par))
                group(split_hi, j + q_heads, points, mixer, 16, slots=2)
                for _, work in late:
                    work()
            heads(act, head)

            def mlstm(i):
                act.wait_ge(ss_out, 32 * H)
                act.wait_ge(*md_.before(i))
                act.wait_ge(*mp.before(i))
                act.wait_ge(*mt.before(i))
                act.wait_ge(*md_.after("so", i))
                nc.scalar.activation(so[:], so[:], ACT.Exp, scale=-1.0).then_inc(*ma.done("so1"))
                act.wait_ge(*ma.after("so1", i))
                nc.scalar.activation(so[:], so[:], ACT.Ln, bias=1.0).then_inc(*ma.done("so2"))
                act.wait_ge(*ma.after("so2", i))
                nc.scalar.activation(so[:], so[:], ACT.Exp, scale=-1.0).then_inc(*ma.done("so3"))
                yield 0
                act.wait_ge(cs_out, 32 * i)
                act.dma_start(cs[:], a["state_ml_C"][0][:, bass.ds(i, 1)].rearrange("b a v k -> v (b a) k")).then_inc(cs_in, 16)
                act.wait_ge(*mt.after("ktr", i))
                for n, _, c in PARTS:
                    nc.scalar.activation(kw[0:n, c], pm[0:n, 3, c * P:(c + 1) * P], ACT.Copy,
                                         scale=cols[0:n, 4, c, bass.ds(i, 1)]).then_inc(*ma.done(f"kw{c}"))
                act.wait_ge(*md_.after("D2", i))
                nc.scalar.activation(md[:, 0:TP], md[:, 0:TP], ACT.Exp).then_inc(*ma.done("d1"))
                nc.scalar.activation(md[0:TS, TP:T], md[0:TS, TP:T], ACT.Exp).then_inc(*ma.done("d2"))
                nc.scalar.activation(emt[:], pm[:, 2, 0:T + NC], ACT.Copy).then_inc(*ma.done("emt"))
                yield 1
                act.wait_ge(*mt.after("vtr", i))
                for n, _, c in PARTS:
                    nc.scalar.activation(vt[0:n, c, 0:P], pm[0:n, 3, c * P:(c + 1) * P], ACT.Copy).then_inc(*ma.done(f"v{c}"))
                yield 2
                for half in range(2):
                    act.wait_ge(*mt.after(f"c{half}", i))
                    nc.scalar.activation(cts[:, 4 * half:4 * half + 4].rearrange("p b k -> p (b k)"), pm[:, 0],
                                         ACT.Copy).then_inc(*ma.done(f"ct{half}"))
                    yield 3 + half
                yield 5
                act.wait_ge(*mt.after("so", i))
                nc.scalar.activation(dn[:], pm[:, 2, 0:T], ACT.Abs).then_inc(*ma.done("abs"))
                yield 6
                yield 7
                yield 8
                act.wait_ge(*md_.after("ho", i))
                nc.scalar.activation(one(mh_hi, i), mh[:], ACT.Copy).then_inc(*ma.done("hi"))
                act.wait_ge(*mt.after("cp", i))
                nc.scalar.activation(cout[:], pm[:, 2, 0:P], ACT.Copy).then_inc(*ma.done("cp"))
                yield 9
                act.wait_ge(*ma.after("cp", i))
                act.dma_start(o["p_C"][0, 0][bass.ds(i, 1)].rearrange("a v k -> v (a k)"), cout[:]).then_inc(cs_out, 16)
                act.wait_ge(*md_.after("cs2", i))
                act.dma_start(o["s_C"][0][:, bass.ds(i, 1)].rearrange("b a v k -> v (b a) k"), cs[:]).then_inc(cs_out, 16)

            with act.Fori(0, H) as i:
                def evacuate(m, done):
                    act.wait_ge(blocks, 16 * (i + q_gate) + done)
                    nc.scalar.activation(one(gates, 4 * i + m), ps[:, m, 0:T], ACT.Copy).then_inc(bank_free, 1)
                group(split_hi, i + q_gate, column_tiles(evacuate), mlstm(i), MLSTM_STAGES)

            act.wait_ge(*md_.before(H))
            act.wait_ge(*mp.before(H))
            act.wait_ge(cs_out, 32 * H)
            act.wait_ge(*no_t.after("tr"))
            nc.scalar.activation(n_out[0:NB * H, 0], pm[0:NB * H, 0, 0:P], ACT.Copy).then_inc(*no_a.done("s"))
            nc.scalar.activation(n_out[0:H, 1], pm[0:H, 1, 0:P], ACT.Copy).then_inc(*no_a.done("p"))
            act.wait_ge(*no_a.after("p"))
            act.dma_start(o["s_n"][0].rearrange("b h k -> (b h) k"), n_out[0:NB * H, 0]).then_inc(stored, 16)
            act.dma_start(o["p_n"][0, 0], n_out[0:H, 1]).then_inc(stored, 16)

            nc.scalar.preload_act_table(ACT.Sigmoid)
            with act.Fori(0, 4) as i:
                def sig(name, tile):
                    nc.scalar.activation(one(gates, tile), one(gates, tile), ACT.Sigmoid).then_inc(*br_a.done(name))

                def sigs(h):
                    for m in (2 * h, 2 * h + 1):
                        sig(f"sa{m}", 4 * i + m)
                    for m in (2 * h, 2 * h + 1):
                        sig(f"sb{m}", 4 * i + m + KT)

                def upper(h):
                    for m in (2 * h, 2 * h + 1):
                        act.wait_ge(*br_d.after(f"s{m}", i))
                        nc.scalar.activation(one(mix_hi, 4 * i + m), mix_b[:, m], ACT.Copy).then_inc(*br_a.done(f"hi{m}"))
                group(split_hi, i + q_branch, [(-1, lambda: sigs(0)), (9, lambda: upper(0)), (9, lambda: sigs(1)), (15, lambda: upper(1))])

            for n in range(3, 7):
                split_hi(q_out, n, 8)
            with act.Fori(0, 4) as i:
                def residual():
                    for k in range(4):
                        act.wait_ge(*ot_t.after(f"x{k}", i))
                        nc.scalar.activation(one(x2, 4 * i + k), pm[:, k, 0:T], ACT.Copy).then_inc(*ot_a.done(f"x{k}"))

                def evacuate(m, done):
                    act.wait_ge(*freed(i + g_out, m))
                    nc.scalar.activation(one(f_hi, 4 * i + m), one(x2, 4 * i + m), ACT.Copy,
                                         scale=wn[:, 1, bass.ds(4 * i + m, 1)]).then_inc(*ot_a.done(f"hi{m}"))
                group(split_hi, i + q_out, [(0, residual)] + column_tiles(evacuate), ring=8)
            nc.scalar.preload_act_table_set(EXP_LN)
            act.wait_ge(*n2_t.after("sum"))
            nc.scalar.activation(r2[:], pm[:, 0, 0:T], ACT.Ln, bias=eps[:], scale=1.0 / D).then_inc(*n2_a.done("ln"))
            act.wait_ge(*n2_a.after("ln"))
            nc.scalar.activation(r2[:], r2[:], ACT.Exp, scale=-0.5).then_inc(*n2_a.done("exp"))
            nc.scalar.preload_act_table(ACT.Silu)

            q, g, g0 = q_ffn, g_ffn, 0
            for c, n in enumerate(CHUNKS):
                def up(i, tail_next):
                    r = i + g0

                    def tap(dst, m, name, offset):
                        act.wait_ge(*freed(2 * i + (g + (offset > 0)), m))
                        nc.scalar.activation(dst[:, m], uu[:, m, 0:FV], ACT.Copy,
                                             scale=fcw[:, 0, bass.ds(4 * r + (m + offset), 1)]).then_inc(*up_a.done(f"{name}{m}"))

                    def gate_tap(m, done):
                        tap(ug, m, "g", 0)

                    def silu(m, done):
                        act.wait_ge(*up_d.after(f"gc{m}b", r))
                        nc.scalar.activation(ug[:, m], ug[:, m], ACT.Silu).then_inc(*up_a.done(f"sg{m}"))

                    def value_tap(m, done):
                        tap(uv, m, "v", FT)

                    def upper(m, done):
                        act.wait_ge(*up_d.after(f"ac{m}b", r))
                        nc.scalar.activation(one(u_hi, 4 * i + m), ac[:, m % 2], ACT.Copy).then_inc(*up_a.done(f"hi{m}"))
                    group(split_hi, 2 * i + q, column_tiles(gate_tap, silu), ring=8)
                    group(split_hi, 2 * i + (q + 1), column_tiles(value_tap, nothing, nothing, upper), ring=8, tail_next=tail_next)
                repeat(act, n, up, n == TAIL)
                q += 2 * n

                def last_rows_ffn(r, first):
                    act.wait_ge(*dn_t.after("tr", r))
                    act.wait_ge(lrow_out, 64 * r + 64)
                    for half in range(2):
                        nc.scalar.activation(u_lrow[:, half], pm[0:FPAD * (1 + NB), half], ACT.Copy).then_inc(*dn_a.done(f"r{half}"))
                    act.wait_ge(*dn_a.after("r1", r))
                    for half in range(2):
                        n0 = first * NG + half * FT * P
                        act.dma_start(o["p_fconv"][0, 0][:, bass.ds(n0, NG)], u_lrow[0:FPAD, half]).then_inc(lrow_out, 16)
                        act.dma_start(o["s_fconv"][0].rearrange("b j n -> (b j) n")[:, bass.ds(n0, NG)],
                                      u_lrow[FPAD:, half]).then_inc(lrow_out, 16)
                    yield 0

                if n == 4:
                    with act.Fori(0, 4) as i:
                        group(split_hi, i + q, (), last_rows_ffn(i + 4 * c, i + g0), 0, ring=8)
                else:
                    for i in range(4):
                        group(split_hi, q, (), last_rows_ffn(4 * c + i, g0 + i) if i < n else None, 0,
                              ring=8, b0=4 * n * i, n=4 * n, tail=True)
                q, g, g0 = q + n, g + 2 * n + 4, g0 + n

            nc.scalar.preload_act_table_set(EXP_LN)
            act.wait_ge(*y_t.after("sum"))
            nc.scalar.activation(r2[:], pm[:, 3, 0:T], ACT.Ln, bias=eps[:], scale=1.0 / D).then_inc(*y_a.done("ln"))
            act.wait_ge(*y_a.after("ln"))
            nc.scalar.activation(r2[:], r2[:], ACT.Exp, scale=-0.5).then_inc(*y_a.done("exp"))
            for g in range(4):
                act.wait_ge(*y_t.after(f"t{g}"))
                bank = (ps, pm)[g % 2]
                nc.scalar.activation(y_rows[:, 0:2, g * NG:(g + 1) * NG], bank[:, 0:2], ACT.Copy)
                nc.scalar.activation(y_rows[0:TS, 2, g * NG:(g + 1) * NG], bank[0:TS, 2], ACT.Copy).then_inc(*y_a.done(f"r{g}"))
                act.wait_ge(*y_a.after(f"r{g}"))
                act.dma_start(o["y_p"][0].rearrange("(c p) d -> p c d", p=P)[:, :, g * NG:(g + 1) * NG],
                              y_rows[:, 0:2, g * NG:(g + 1) * NG]).then_inc(y_out, 16)
                act.dma_start(o["y_s"].rearrange("b t d -> (b t) d")[:, g * NG:(g + 1) * NG],
                              y_rows[0:TS, 2, g * NG:(g + 1) * NG]).then_inc(y_out, 16)

        @block.vector
        def _(dve):
            def step(steps, name, r=0):
                dve.wait_ge(*steps.after(name, r))

            dve.wait_ge(consts, 1)
            for m in range(4):
                nc.vector.tensor_copy(n_p[:, m:m + 1], eps[:]).then_inc(bank_free, 1)

            dve.wait_ge(*st_a.after("expp"))
            for c in range(2):
                nc.vector.tensor_scalar(x_rows[:, c], x_rows[:, c], rstd[:, c:c + 1], None, ALU.mult).then_inc(*st_d.done(f"xs{c}"))
            dve.wait_ge(*st_a.after("exps"))
            nc.vector.tensor_scalar(x_rows[0:TS, 2], x_rows[0:TS, 2], rstd[0:TS, 2:3], None, ALU.mult).then_inc(*st_d.done("xs2"))
            dve.wait_ge(*st_t.after("consts"))
            nc.vector.tensor_copy(gcw[:].rearrange("p j t -> p (j t)"), pm[:, 0, 0:GC * 3 * H]).then_inc(*st_d.done("cw"))
            nc.vector.tensor_copy(wn[:].rearrange("p n k -> p (n k)"), pm[:, 0, 128:128 + 3 * KT]).then_inc(*st_d.done("nw"))
            nc.vector.tensor_copy(n_s[:].rearrange("p b h -> p (b h)"), pm[:, 0, 256:256 + NB * H]).then_inc(*st_d.done("ns"))
            dve.wait_ge(*st_t.after("old"))
            for b in range(3):
                nc.vector.tensor_copy(seqs3(gq[:, 8 * b:8 * b + 8, GPAD + TP:], GS, 0, GPAD),
                                      pm[:, b + 1, 0:8 * NB * GPAD].rearrange("p (t b s) -> p t b s", t=8, s=GPAD))\
                    .then_inc(*st_d.done(f"old{b}"))
            for f in range(KT):
                dve.wait_ge(*st_a.after(f"hi{f}"))
                nc.vector.scalar_tensor_tensor(h_lo[:, f], ps[:, f % 4, 0:T], wn[:, 0, f:f + 1], h_hi[:, f].bitcast(F32),
                                               ALU.mult, ALU.subtract).then_inc(*st_d.done(f"lo{f}"))

            for b in range(3):
                dve.wait_ge(hi_ready, b + 1)
                nc.vector.tensor_tensor(wlo[:, b], raw[:, 0, 4 * b:4 * b + 4], whi[:, b].bitcast(F32),
                                        ALU.subtract).then_inc(lo_ready, 1)

            def g(name, instruction):
                instruction.then_inc(*gate_d.done(name))
                step(gate_d, name)

            def chunked(ap):
                return ap[..., 0:TP].rearrange("h (n t) -> h n t", t=CH)

            def seqd(ap):
                return ap[..., TP:T].rearrange("h (b t) -> h b t", t=L)

            def chunked2(ap):
                return ap[:, :, 0:TP].rearrange("h r (n t) -> h r n t", t=CH)

            def seqd2(ap):
                return ap[:, :, TP:T].rearrange("h r (b t) -> h r b t", t=L)

            tt, tc, ts, stt = nc.vector.tensor_tensor, nc.vector.tensor_copy, nc.vector.tensor_scalar, nc.vector.scalar_tensor_tensor
            def gates_rows():
                dve.wait_ge(small_in, 64)
                dve.wait_ge(*st_a.after("smhi"))
                nc.vector.tensor_tensor(sm_lo[:], sm_raw[:], sm_hi[:].bitcast(F32), ALU.subtract).then_inc(*st_d.done("smlo"))
                yield from range(3)
                dve.wait_ge(consts, N_CONST)
                dve.wait_ge(rows_in, 16 * 12)
                dve.wait_ge(*st_t.after("small"))
                g("ga", ts(sp_in[:, 0], pm[0:H, 3, 0:T], hcol[:, 1:2], None, ALU.add))
                g("gb", ts(sp_in[:, 1], pm[32:32 + H, 3, 0:T], -1.0, None, ALU.mult))
                g("mf", ts(sp_in[:, 2], pm[96:96 + H, 3, 0:T], hcol[:, 3:4], -1.0, ALU.add, ALU.mult))
                g("mi", ts(ig[:], pm[64:64 + H, 3, 0:T], hcol[:, 2:3], None, ALU.add))
                yield 0
                dve.wait_ge(*gate_a.after("ln"))
                g("sp", stt(sp_out[:], sp_in[:], 0.0, sp_out[:], ALU.max, ALU.add))
                dve.wait_ge(*gate_a.after("expA"))
                g("g", ts(cum[0][:, 0], sp_out[:, 0], hcol[:, 4:5], -1.0, ALU.mult, ALU.mult))
                g("lf", ts(cum[0][:, 1], sp_out[:, 2], -1.0, None, ALU.mult))
                yield 1

                def doubling(tag, views, op):
                    for k in range(NLEV):
                        (pa, sa), (pb, sb) = views(k)
                        s = 1 << k
                        g(f"{tag}{k}a", tt(pb[..., s:], pa[..., s:], pa[..., :-s], op))
                        g(f"{tag}{k}b", tc(pb[..., :s], pa[..., :s]))
                        if s < L:
                            g(f"{tag}{k}c", tt(sb[..., s:], sa[..., s:], sa[..., :-s], op))
                            g(f"{tag}{k}d", tc(sb[..., :s], sa[..., :s]))
                        else:
                            g(f"{tag}{k}c", tc(sb, sa))
                        yield k

                yield from doubling("s", lambda k: [(chunked2(cum[j % 2][:]), seqd2(cum[j % 2][:])) for j in (k, k + 1)], ALU.add)
                G, b_ = cum[0][:, 0], cum[0][:, 1]
                g("G", tc(g_row[:, 0], G))
                g("gl1", tt(chunked(e_row[:]), chunked(G)[..., CH - 1:].to_broadcast([H, NCH, CH]), chunked(G), ALU.subtract))
                g("gl2", tt(seqd(e_row[:]), seqd(G)[..., L - 1:].to_broadcast([H, NB, L]), seqd(G), ALU.subtract))
                g("c", tt(c_row[:], ig[:], b_, ALU.subtract))
                yield 8
                yield from doubling("x", lambda k: [(chunked(t[:]), seqd(t[:])) for t in
                                         ((c_row if k == 0 else cmx[(k + 1) % 2]), cmx[k % 2])], ALU.max)
                cm = cmx[1][:]
                one_col = lambda t: t.unsqueeze(2)
                g("bl1", tc(one_col(bl[:, 0:NCH]), chunked(b_)[..., CH - 1:]))
                g("bl2", tc(one_col(bl[:, NCH:]), seqd(b_)[..., L - 1:]))
                g("cl1", tc(one_col(cl[:, 0:NCH]), chunked(cm)[..., CH - 1:]))
                g("cl2", tc(one_col(cl[:, NCH:]), seqd(cm)[..., L - 1:]))
                g("emc", tt(cl[:], cl[:], bl[:], ALU.add))
                g("z0", nc.vector.memset(m_in[:, 0:1], 0.0))
                yield 15
                for n in range(NCH):
                    g(f"m{n}", stt(m_new[:, n:n + 1], m_in[:, n:n + 1], bl[:, n:n + 1], cl[:, n:n + 1], ALU.add, ALU.max))
                    if n + 1 < NCH:
                        g(f"n{n}", tc(m_in[:, n + 1:n + 2], m_new[:, n:n + 1]))
                yield 16
                g("ms1", tt(m_new[:, NCH:], m_in[:, NCH:], bl[:, NCH:], ALU.add))
                g("ms2", tt(m_new[:, NCH:], m_new[:, NCH:], cl[:, NCH:], ALU.max))
                at_chunk = lambda t: one_col(t[:, 0:NCH]).to_broadcast([H, NCH, CH])
                at_seq = lambda t: one_col(t[:, NCH:]).to_broadcast([H, NB, L])
                g("mm1", tt(chunked(mmx[:]), at_chunk(m_in), chunked(cm), ALU.max))
                g("mm2", tt(seqd(mmx[:]), at_seq(m_in), seqd(cm), ALU.max))
                g("negmx", ts(m_row[:, 0:T], mmx[:], -1.0, None, ALU.mult))
                g("wi1", tt(chunked(sw_row[:]), at_chunk(m_in), chunked(mmx[:]), ALU.subtract))
                g("wi2", tt(seqd(sw_row[:]), at_seq(m_in), seqd(mmx[:]), ALU.subtract))
                yield 17
                g("emt", tt(ig[:], b_, mmx[:], ALU.add))
                g("fw1", tt(f_row[:], bl[:], m_in[:], ALU.add))
                g("fw2", tt(f_row[:], f_row[:], m_new[:], ALU.subtract))
                g("sw0", tt(cl[:], bl[:], m_new[:], ALU.subtract))
                g("sw1", tt(chunked(cmx[0][:]), chunked(c_row[:]), at_chunk(cl), ALU.add))
                g("sw2", tt(seqd(cmx[0][:]), seqd(c_row[:]), at_seq(cl), ALU.add))
                yield 18
                dve.wait_ge(*gate_t.after("cols"))
                col_view = pm[:, 0, 0:15 * H].rearrange("p (q c h) -> p q c h", q=5, c=3)
                g("colsA", tc(cols[:, :, 0:2], col_view[:, :, 0:2]))
                g("colsB", tc(cols[0:TS, :, 2], col_view[0:TS, :, 2]))
                g("nbA", ts(nbeta[:, 0:2], cols[:, 1, 0:2], -1.0, None, ALU.mult))
                g("nbB", ts(nbeta[0:TS, 2], cols[0:TS, 1, 2], -1.0, None, ALU.mult))

            gates_mixer = gates_rows()
            group(split_lo, 0, (), islice(gates_mixer, GATE_STAGES // 2), GATE_STAGES // 2)
            group(split_lo, 1, (), gates_mixer, GATE_STAGES // 2)
            with dve.Fori(2, 7) as i:
                group(split_lo, i)

            def prepare(i, par):
                qe, ke, pt, kg, bv, xx, ec = handed[par]
                def d(name, instruction, then=True):
                    instruction.then_inc(*prep_d.done(name))
                    if then:
                        step(prep_d, name, i)
                hs = bass.ds(i, 1)
                dve.wait_ge(*prep_a.before(i))
                dve.wait_ge(*prep_t.before(i))
                dve.wait_ge(*prep_p.before(i))
                dve.wait_ge(*gate_a.after("sw"))
                dve.wait_ge(*freed(g_z if isinstance(i, int) and i == 0 else g_z + 1, 3))
                dve.wait_ge(lrow_out, 64)
                d("rsel", ts(rsel[:], g_row[:, 0], ident[0:H, hs], None, ALU.mult), False)
                for j in range(1, GC):
                    for t in range(3):
                        if j == 1:
                            dve.wait_ge(*prep_a.after(f"c{t}", i))
                        else:
                            step(prep_d, f"cv{t}{j - 1}", i)
                        c = cv[:, t * GV:(t + 1) * GV]
                        d(f"cv{t}{j}", stt(c, one(gq, i + t * H)[:, j:j + GV], gcw[:, j, bass.ds(i + t * H, 1)], c,
                                           ALU.mult, ALU.add), False)
                    yield j - 1
                d("clampz", ts(sg[:, 3 * GV:], one(zm, i + 3 * H), SIG_MIN, None, ALU.max), False)
                yield from range(3)
                dve.wait_ge(*prep_a.after("sg3", i))
                step(prep_d, f"cv2{GC - 1}", i)
                cv3, sg3 = cv[:].rearrange("p (t g) -> p t g", t=3), sg[:, 0:3 * GV].rearrange("p (t g) -> p t g", t=3)
                d("qkv1", tt(qkv[:, :, 0:TP], cv3[:, :, 0:TP], sg3[:, :, 0:TP], ALU.mult), False)
                d("qkv2", tt(qkv[:, :, TP:T].rearrange("p t (b s) -> p t b s", s=L), spaced(cv3[:, :, GPAD + TP:], GS),
                             spaced(sg3[:, :, GPAD + TP:], GS), ALU.mult), False)
                yield 2
                dve.wait_ge(*prep_a.after("rn2", i))
                step(prep_d, "qkv2", i)
                q_, k_, v_ = (qkv[:, t] for t in range(3))
                d("k", tt(k_, k_, rn[:, 1], ALU.mult), False)
                d("q", stt(q_, q_, QSCALE, rn[:, 0], ALU.mult, ALU.mult), False)
                dve.wait_ge(*prep_a.after("egs", i))
                step(prep_d, "q", i)
                dve.wait_ge(*prep_t.after("norm", i))
                d("rselb", ts(rsel[:], g_row[:, 1], ident[0:H, hs], None, ALU.mult), False)
                two_before(dve, i)
                d("ke", tt(ke[:], k_, eg[:], ALU.mult), False)
                d("qe", tt(qe[:], q_, eg[:], ALU.mult), False)
                for n, t0, c in PARTS:
                    d(f"d{c}", stt(dec[0:n, t0:t0 + n], pm[0:n, 2, t0:t0 + n], cols[0:n, 0, c, hs],
                                   (incl if n == P else incl_s)[:], ALU.subtract, ALU.min), False)
                yield 3
                dve.wait_ge(*prep_t.after("tr", i))
                for n, _, c in PARTS:
                    d(f"bv{c}", ts(bv[0:n, c], pm[0:n, 1, c * P:(c + 1) * P], cols[0:n, 1, c, hs], None, ALU.mult), False)
                dve.wait_ge(*prep_a.after("d2", i))
                dve.wait_ge(*prep_t.after("beta", i))
                d("bd1", tt(bd[:, 0:TP], dec[:, 0:TP], pm[:, 1, 0:TP], ALU.mult), False)
                d("bd2", tt(bd[0:TS, TP:T], dec[0:TS, TP:T], pm[0:TS, 1, TP:T], ALU.mult), False)
                yield 4
                halves = [(P, slice(0, TP)), (TS, slice(TP, T))]

                def level(l, n):
                    return lev[:, l].unsqueeze(1).to_broadcast([P, 2, P]) if n == P else lev[0:TS, l, 0:TS]

                def part(t, n, cc):
                    return t[:, cc].rearrange("p (c t) -> p c t", c=2) if n == P else t[0:n, cc]

                dve.wait_ge(*prep_t.after("kk", i))
                step(prep_d, "bd2", i)
                for (n, cc), name in zip(halves, ("at1", "at2")):
                    d(name, tt(at_[0:n, cc], pm[0:n, 2, cc], bd[0:n, cc], ALU.mult), False)
                dve.wait_ge(*prep_t.after("kq", i))
                for (n, cc), name in zip(halves, ("pt1", "pt2")):
                    d(name, tt(pt[0:n, cc], pm[0:n, 0, cc], dec[0:n, cc], ALU.mult), False)
                step(prep_d, "at2", i)
                for (n, cc), name in zip(halves, ("n0a", "n0b")):
                    d(name, tt(part(nt0, n, cc), part(at_, n, cc), level(0, n), ALU.mult))
                eye = lambda n: ident[:].unsqueeze(1).to_broadcast([P, 2, P]) if n == P else ident[0:TS, 0:TS]
                for (n, cc), name in zip(halves, ("xt1", "xt2")):
                    d(name, tt(part(xx[:, 1], n, cc), eye(n), part(nt0, n, cc), ALU.subtract), False)
                yield 5
                for (n, cc), name in zip(halves, ("n1a", "n1b")):
                    d(name, tt(part(nt1, n, cc), part(at_, n, cc), level(1, n), ALU.mult), False)
                yield 6
                yield 7
                for l in LEVELS:
                    dve.wait_ge(*prep_t.after(f"xx{l}", i))
                    if l == 1:
                        d("xx1s", tt(xx[0:TS, :, TP:T], xx[0:TS, :, TP:T], pm[0:TS, 0:2, TP:T], ALU.subtract), False)
                    d(f"xx{l}", tt(xx[:, :, 0:TP], xx[:, :, 0:TP], pm[:, 0:2, 0:TP], ALU.subtract), False)
                    if l < NLEV - 1:
                        nt = (nt0, nt1)[(l + 1) % 2]
                        d(f"n{l + 1}", tt(part(nt, P, slice(0, TP)), part(at_, P, slice(0, TP)), level(l + 1, P), ALU.mult), False)
                        yield 2 * l + 6
                        yield 2 * l + 7

            def scan(i, par):
                qe, ke, pt, kg, bv, xx, ec = handed[par]
                hs = bass.ds(i, 1)

                def d(name, instruction):
                    instruction.then_inc(*scan_d.done(name))

                def state(n):
                    dve.wait_ge(*scan_t.after(f"u{n}", i))
                    if n == 0:
                        dve.wait_ge(ss_out, 32 * i)
                        dve.wait_ge(*scan_t.before(i))
                        d("S0", tc(S[:], bu[:, 0:P]))
                    else:
                        step(scan_d, f"S{n - 1}", i)
                        d(f"S{n}", stt(S[:], S[:], ec[:, n:n + 1], bu[:, 0:P], ALU.mult, ALU.add))

                def resid(n):
                    lo, c = CH * (n % 2), n // 2
                    dve.wait_ge(*scan_t.after(f"k{n}", i))
                    d(f"R{n}", stt(rr[lo:lo + CH], bw[lo:lo + CH, P:2 * P], nbeta[lo:lo + CH, c, hs], bv[lo:lo + CH, c],
                                   ALU.mult, ALU.add))

                yield 0
                yield 1
                state(0)
                yield 2
                resid(1)
                yield 3
                yield 4
                state(1)
                dve.wait_ge(*scan_t.after("trS", i))
                d("rs", stt(r_s[:], bw[0:TS, 2 * P:3 * P], nbeta[0:TS, 2, hs], bv[0:TS, 2], ALU.mult, ALU.add))
                yield 5
                resid(2)
                yield 6
                yield 7
                state(2)
                yield 8
                resid(3)
                yield 9
                yield 10
                state(3)
                yield 11
                yield 12
                dve.wait_ge(*scan_a.after("rs2", i))
                dve.wait_ge(*scan_p.after("sse", i))
                d("go", stt(gout[:], bo[:, 0:T], wgn[:], rso[:], ALU.mult, ALU.mult))
                for k, bank in enumerate((bw, bu)):
                    dve.wait_ge(*scan_t.after(f"Ss{k + 1}", i))
                    half = ss[:, 4 * k:4 * k + 4].rearrange("p b v -> p (b v)")
                    d(f"ss{k + 1}", tt(half, half, bank, ALU.add))
                yield 13
                dve.wait_ge(*scan_a.after("hi", i))
                d("lo", tt(one(go_lo, i), gout[:], one(go_hi, i).bitcast(F32), ALU.subtract))

            group(split_lo, q_z + 1, (), beside(prep=prepare(0, 0), pace=GDN_FIRST_PACE), 16)

            def head(j, par):
                last = isinstance(j, int) and j == H - 1
                mixer = beside(scan(j, par), iter(()) if last else prepare(j + 1, 1 - par))
                group(split_lo, j + q_heads, (), mixer, 16, slots=2)
            heads(dve, head)

            dve.wait_ge(ss_out, 32 * H)
            nc.vector.memset(vt[:, :, P:], 1.0).then_inc(vt_ones, 1)

            def mlstm(i):
                def d(name, instruction):
                    instruction.then_inc(*md_.done(name))
                hs = bass.ds(i, 1)
                dve.wait_ge(*ma.before(i))
                dve.wait_ge(*mt.before(i))
                q_t = one(zm, i)
                d("so", ts(so[:], one(zm, i + 3 * H), SIG_MIN, None, ALU.max))
                d("sel", ts(mrsel[32:32 + H], m_row, ident[32:32 + H, bass.ds(i + 32, 1)], None, ALU.mult))
                d("k", ts(mk[:], one(zm, i + H), QSCALE, None, ALU.mult))
                d("v", tc(mv[:], one(zm, i + 2 * H)))
                yield 0
                dve.wait_ge(*mt.after("rows", i))
                for n, t0, c in PARTS:
                    d(f"D{c}", stt(md[0:n, t0:t0 + n], pm[0:n, 0, t0:t0 + n], cols[0:n, 3, c, hs],
                                   (incl if n == P else incl_s)[:], ALU.add, ALU.min))
                d("qw", tt(qw[:], q_t, pm[:, 1, 0:T], ALU.mult))
                yield 1
                step(md_, "qw", i)
                d("prs", tt(prd[:, TP:T].rearrange("p (b s) -> p b s", s=L), qw[:, TP:T].rearrange("p (b s) -> p b s", s=L),
                            n_s[:, :, hs].to_broadcast([P, NB, L]), ALU.mult))
                dve.wait_ge(*mt.after("kq", i))
                dve.wait_ge(*ma.after("d2", i))
                d("pt1", tt(mpt[:, 0:TP], pm[:, 0, 0:TP], md[:, 0:TP], ALU.mult))
                d("pt2", tt(mpt[0:TS, TP:T], pm[0:TS, 0, TP:T], md[0:TS, TP:T], ALU.mult))
                yield 2

                def state(n):
                    dve.wait_ge(*mt.after(f"u{n}", i))
                    if n == 0:
                        d("C0", tc(ctn[:], pm[:, 3, 0:P + 1]))
                    else:
                        d(f"C{n}", stt(ctn[:], ctn[:], emt[:, T + n:T + n + 1], pm[:, 3, 0:P + 1], ALU.mult, ALU.add))
                    step(md_, f"C{n}", i)
                    if n + 1 < NCH:
                        cc = slice(CH * (n + 1), CH * (n + 2))
                        d(f"pr{n + 1}", ts(prd[:, cc], qw[:, cc], ctn[:, P:], None, ALU.mult))

                for n in range(3):
                    state(n)
                    if n < 2:
                        yield 3 + n
                state(3)
                d("np", tc(n_p[:, hs], ctn[:, P:]))
                dve.wait_ge(*mt.after("ns", i))
                n_h = n_s[:, :, hs].rearrange("p b a -> p (b a)")
                d("ns", tt(n_h, n_h, emt[:, T + NCH:], ALU.mult))
                step(md_, "ns", i)
                d("ns2", tt(n_h, n_h, pm[:, 0, 0:NB], ALU.add))
                yield 6
                dve.wait_ge(*ma.after("abs", i))
                d("mx", tt(dn[:], dn[:], emt[:, 0:T], ALU.max))
                step(md_, "mx", i)
                d("rc", nc.vector.reciprocal(dn[:], dn[:]))
                yield 7
                step(md_, "rc", i)
                d("h", tt(mh[:], pm[:, 1, 0:T], dn[:], ALU.mult))
                step(md_, "h", i)
                d("ho", tt(mh[:], mh[:], so[:], ALU.mult))
                yield 8
                dve.wait_ge(*mt.after("C", i))
                dve.wait_ge(*mp.after("cs", i))
                for k, bank in enumerate((0, 3)):
                    half = cs[:, 4 * k:4 * k + 4].rearrange("p b v -> p (b v)")
                    d(f"cs{k + 1}", tt(half, half, pm[:, bank], ALU.add))
                yield 9
                dve.wait_ge(*ma.after("hi", i))
                d("lo", tt(one(mh_lo, i), mh[:], one(mh_hi, i).bitcast(F32), ALU.subtract))

            with dve.Fori(0, H) as i:
                group(split_lo, i + q_gate, (), mlstm(i), MLSTM_STAGES)

            with dve.Fori(0, 4) as i:
                def first(h, c):
                    m = 2 * h + c
                    dve.wait_ge(blocks, 16 * (i + q_branch) + (8 * h + 4))
                    dve.wait_ge(*br_a.after(f"sa{m}", i))
                    tt(mix_a[:, m], one(gates, 4 * i + m), ps[:, c, 0:T], ALU.mult).then_inc(bank_free, 1)

                def second(h, c):
                    m = 2 * h + c
                    dve.wait_ge(blocks, 16 * (i + q_branch) + (8 * h + 8))
                    dve.wait_ge(*br_a.after(f"sb{m}", i))
                    tt(mix_b[:, m], one(gates, 4 * i + m + KT), ps[:, 2 + c, 0:T], ALU.mult).then_inc(bank_free, 1)
                    dve.wait_ge(*freed(2 * i + (g_branch + h), 2 + c))
                    tt(mix_b[:, m], mix_b[:, m], mix_a[:, m], ALU.add).then_inc(*br_d.done(f"s{m}"))

                def rest(h):
                    for m in (2 * h, 2 * h + 1):
                        dve.wait_ge(*br_a.after(f"hi{m}", i))
                        tt(one(mix_lo, 4 * i + m), mix_b[:, m], one(mix_hi, 4 * i + m).bitcast(F32), ALU.subtract)\
                            .then_inc(*br_d.done(f"lo{m}"))
                points = []
                for h in range(2):
                    points += [(8 * h + 3 + k % 2 + 4 * (k // 2), lambda h=h, k=k: (first, second)[k // 2](h, k % 2)) for k in range(4)]
                    points += [(8 * h + 10, lambda h=h: rest(h))]
                group(split_lo, i + q_branch, points)

            for n in range(3, 7):
                split_lo(q_out, n, 8)
            with dve.Fori(0, 4) as i:
                def evacuate(m, done):
                    dve.wait_ge(blocks, 16 * (i + q_out) + done)
                    dve.wait_ge(*ot_a.after(f"x{m}", i))
                    t = one(x2, 4 * i + m)
                    tt(t, t, ps[:, m, 0:T], ALU.add).then_inc(bank_free, 1)

                def rest(m, done):
                    dve.wait_ge(*ot_a.after(f"hi{m}", i))
                    stt(one(f_lo, 4 * i + m), one(x2, 4 * i + m), wn[:, 1, bass.ds(4 * i + m, 1)],
                        one(f_hi, 4 * i + m).bitcast(F32), ALU.mult, ALU.subtract).then_inc(*ot_d.done(f"lo{m}"))
                group(split_lo, i + q_out, column_tiles(evacuate, rest), ring=8)
            dve.wait_ge(*n2_t.after("w"))
            for j in range(FC):
                last = tc(fcw[:, j], pm[:, 1, j * 2 * FT:(j + 1) * 2 * FT])
            last.then_inc(*n2_d.done("w"))
            dve.wait_ge(*n2_d.after("w"))
            last = nc.vector.memset(uu[:, :, 0:FPAD], 0.0)
            last.then_inc(uu_zero, 1)
            dve.wait_ge(*n2_a.after("exp"))

            q, g0 = q_ffn, 0
            for c, n in enumerate(CHUNKS):
                def up(i, tail_next):
                    r = i + g0

                    def old_rows(half, name):
                        dve.wait_ge(*up_t.after(f"old{half}", r))
                        if half:
                            dve.wait_ge(*up_p.after("g2", r))
                        else:
                            dve.wait_ge(*up_p.before(r))
                        tc(seqs3(uu[:, :, FPAD + TP:], FS, 0, FPAD),
                           pm[:, 2 + half, 0:4 * NB * FPAD].rearrange("p (t b s) -> p t b s", t=4, s=FPAD))\
                            .then_inc(*up_d.done(name))

                    def turned(m, n_, q_, done):
                        dve.wait_ge(blocks, 16 * (2 * i + q_) + done)
                        tt(seqs(uu[:, m, FPAD + TP:], FS, FPAD, FS), ps[:, m, TP:T].rearrange("p (b s) -> p b s", s=L),
                           r2[:, TP:T].rearrange("p (b s) -> p b s", s=L), ALU.mult).then_inc(*up_d.done(f"{n_}{m}"))
                        tt(uu[:, m, FPAD:FPAD + TP], ps[:, m, 0:TP], r2[:, 0:TP], ALU.mult).then_inc(bank_free, 1)

                    def taps(dst, m, n_, offset):
                        tile = bass.ds(4 * r + (m + offset), 1)
                        for j, k in ((1, "a"), (2, "b")):
                            if j == 1:
                                dve.wait_ge(*up_a.after(f"{n_}{m}", r))
                            else:
                                dve.wait_ge(*up_d.after(f"{n_}c{m}a", r))
                            stt(dst[:, m], uu[:, m, j:j + FV], fcw[:, j, tile], dst[:, m], ALU.mult, ALU.add)\
                                .then_inc(*up_d.done(f"{n_}c{m}{k}"))

                    def gate(m, done):
                        if m == 0:
                            old_rows(0, "og")
                        turned(m, "g", q, done)

                    def gate_taps(m, done):
                        taps(ug, m, "g", 0)

                    def value(m, done):
                        if m == 0:
                            old_rows(1, "ov")
                        turned(m, "v", q + 1, done)

                    def value_taps(m, done):
                        taps(uv, m, "v", FT)

                    def gated(m, done):
                        dve.wait_ge(*up_a.after(f"sg{m}", r))
                        dve.wait_ge(*up_d.after(f"vc{m}b", r))
                        a_t = ac[:, m % 2]
                        tt(a_t[:, 0:TP], ug[:, m, 0:TP], uv[:, m, 0:TP], ALU.mult).then_inc(*up_d.done(f"ac{m}a"))
                        tt(a_t[:, TP:T].rearrange("p (b s) -> p b s", s=L), spaced(ug[:, m, FPAD + TP:], FS),
                           spaced(uv[:, m, FPAD + TP:], FS), ALU.mult).then_inc(*up_d.done(f"ac{m}b"))

                    def rest(m, done):
                        dve.wait_ge(*up_a.after(f"hi{m}", r))
                        tt(one(u_lo, 4 * i + m), ac[:, m % 2], one(u_hi, 4 * i + m).bitcast(F32), ALU.subtract).then_inc(*up_d.done(f"lo{m}"))
                    group(split_lo, 2 * i + q, column_tiles(gate, gate_taps), ring=8)
                    group(split_lo, 2 * i + (q + 1), column_tiles(value, value_taps, gated, rest), ring=8, tail_next=tail_next)
                repeat(dve, n, up, n == TAIL)
                q += 2 * n
                g0 += n

                def down(q_, tile, at=0, n=4):
                    def evacuate(m, done):
                        dve.wait_ge(blocks, 16 * q_ + (at + done))
                        t = one(x2, tile + m)
                        tt(t, t, ps[:, m, 0:T], ALU.add).then_inc(bank_free, 1)
                    return column_tiles(evacuate, n=n)

                if n == 4:
                    with dve.Fori(0, 4) as i:
                        group(split_lo, i + q, down(i + q, 4 * i), ring=8)
                else:
                    for i in range(4):
                        at = 4 * n * i
                        group(split_lo, q, down(q, 4 * i, at, n), ring=8, b0=at, n=4 * n, tail=True)
                q += n
            dve.wait_ge(*y_a.after("exp"))
            for f in range(KT):
                if f >= 8:
                    dve.wait_ge(*y_t.after(f"t{f // 4 - 2}"))
                stt(yt[:, f % 8], x2[:, f], wn[:, 2, f:f + 1], r2[:], ALU.mult, ALU.mult).then_inc(*y_d.done(f"y{f}"))

        @block.tensor
        def _(pe):
            mm = nc.tensor.matmul

            def turn(out, in_, n):
                return nc.tensor.transpose(out, in_, ident[0:n, 0:n])

            pe.wait_ge(rows_in, 16 * 7)
            pe.wait_ge(consts, 4)
            turn(pm[:, 0, 0:GC * 3 * H], w_rows[:], GC * 3 * H)
            turn(pm[:, 0, 128:128 + 3 * KT], norm_rows[:], 3 * KT)
            turn(pm[:, 0, 256:256 + NB * H], n_rows[:], NB * H).then_inc(*st_t.done("consts"))
            for t in range(3 * H):
                n = NB * GPAD
                last = turn(pm[:, t // 8 + 1, t % 8 * n:(t % 8 + 1) * n], conv_rows[:, t * P:(t + 1) * P], n)
            last.then_inc(*st_t.done("old"))
            pe.wait_ge(*st_d.after("xs2"))
            for f in range(KT):
                if f >= 4:
                    pe.wait_ge(*st_d.after(f"lo{f - 4}"))
                for n, t0, c in PARTS:
                    last = turn(ps[:, f % 4, t0:t0 + n], x_rows[0:n, c, f * P:(f + 1) * P], n)
                last.then_inc(*st_t.done(f"x{f}"))

            def product(out, w_hi, w_lo, x_hi, x_lo, start, stop):
                mm(out, w_hi, x_hi, start=start, stop=False)
                mm(out, w_hi, x_lo, start=False, stop=False)
                return mm(out, w_lo, x_hi, start=False, stop=stop)

            pe.wait_ge(*st_d.after(f"lo{KT - 1}"))
            pe.wait_ge(*st_d.after("old2"))
            def column_tile(q, b0, n, bank, free, x_hi, x_lo, ring, mixer=None, stages=0, b_all=0, n_all=16, x_last=None):
                pe.wait_ge(bank_free, free)
                for j in range(n):
                    if x_last and j == n - 1:
                        pe.wait_ge(*x_last)
                    pe.wait_ge(lo_ready, 16 * q + (b0 + j + 1))
                    hi, lo = ring_slot(whi, whi2, b0 + j, ring), ring_slot(wlo, wlo2, b0 + j, ring)
                    for k in range(4):
                        kk = 4 * j + k
                        last = product(ps[:, bank, 0:T], hi[:, k], lo[:, k], x_hi[:, kk], x_lo[:, kk],
                                       kk == 0, kk == 4 * n - 1)
                    last.then_inc(blocks, 1)
                    b = b_all + j
                    for _ in range((b + 1) * stages // n_all - b * stages // n_all):
                        next(mixer, None)

            def pe_group(q, g, x_hi, x_lo, mixer=None, stages=0, ring=4, b0=0, n=4, x_last=None, banks=4):
                for m in range(4):
                    column_tile(q, b0 + n * m, n, m % banks, 4 * g + (m + 5 - banks), x_hi, x_lo, ring, mixer, stages, n * m, 4 * n, x_last)
                for _ in mixer or ():
                    pass

            def gates_rows():
                pe.wait_ge(*st_d.after("smlo"))
                for k in range(KT):
                    last = product(pm[:, 3, 0:T], sm_hi[:, k], sm_lo[:, k], h_hi[:, k], h_lo[:, k], k == 0, k == KT - 1)
                last.then_inc(*st_t.done("small"))
                yield from range(22)
                pe.wait_ge(consts, N_CONST)
                pe.wait_ge(*gate_d.after("sw2"))
                pe.wait_ge(*gate_a.after("sw"))
                for n_, t in enumerate((g_row[:, 0], g_row[:, 1], e_row[:], c_row[:], cmx[0][:])):
                    for n, t0, c in PARTS:
                        at0 = (3 * n_ + c) * H
                        last = turn(pm[0:n, 0, at0:at0 + H], t[:, t0:t0 + n], H)
                last.then_inc(*gate_t.done("cols"))

            gates_mixer = gates_rows()
            pe_group(0, 0, h_hi, h_lo, islice(gates_mixer, GATE_STAGES // 2), GATE_STAGES // 2)
            pe_group(1, 1, h_hi, h_lo, gates_mixer, GATE_STAGES // 2)
            with pe.Fori(2, 6) as i:
                pe_group(i, i, h_hi, h_lo)

            def last_rows():
                for i in range(2):
                    pe.wait_ge(*lst_p.after("b", i))
                    pe.wait_ge(*lst_a.before(i))
                    for t in range(12):
                        last = turn(pm[0:GPAD * (1 + NB), t // 4, t % 4 * P:(t % 4 + 1) * P], g_last[:, t], P)
                    last.then_inc(*lst_t.done("tr"))
                    yield 0
                    yield 1

            pe_group(q_z, g_z, h_hi, h_lo, last_rows(), 4)

            def prepare(i, par):
                qe, ke, pt, kg, bv, xx, ec = handed[par]
                q_, k_, v_ = (qkv[:, t] for t in range(3))
                yield from range(6)
                pe.wait_ge(*prep_p.after("sq", i))
                pe.wait_ge(*prep_d.before(i))
                for t in range(2):
                    mm(pm[:, t, 0:T], ones[:], sq[:, t], start=True, stop=True)
                pe.wait_ge(*prep_d.after("rsel", i))
                mm(pm[:, 2, 0:T], ones[0:H], rsel[:], start=True, stop=True).then_inc(*prep_t.done("norm"))
                yield 2
                pe.wait_ge(*prep_d.after("q", i))
                for t, src in ((0, k_), (1, v_)):
                    for n, t0, c in PARTS:
                        last = turn(pm[0:n, t, c * P:(c + 1) * P], src[:, t0:t0 + n], P)
                last.then_inc(*prep_t.done("tr"))
                pe.wait_ge(*prep_d.after("d2", i))
                pe.wait_ge(*prep_a.after("egs", i))
                for n, t0, c in PARTS:
                    cc = slice(t0, t0 + n)
                    last = mm(pm[0:n, 2, cc], k_[:, cc], k_[:, cc], start=True, stop=True)
                last.then_inc(*prep_t.done("kk"))
                yield 3
                pe.wait_ge(*prep_a.after("kg2", i))
                for n, t0, c in PARTS:
                    cc = slice(t0, t0 + n)
                    last = mm(pm[0:n, 0, cc], k_[:, cc], q_[:, cc], start=True, stop=True)
                last.then_inc(*prep_t.done("kq"))
                pe.wait_ge(*prep_d.after("bv2", i))
                mm(pm[:, 1, 0:T], ones[0:H], rsel[:], start=True, stop=True).then_inc(*prep_t.done("beta"))
                yield 4
                pe.wait_ge(*prep_d.after("xt2", i))
                for n, t0, c in PARTS:
                    cc = slice(t0, t0 + n)
                    last = turn(pm[0:n, 1, cc], xx[0:n, 1, cc], n)
                last.then_inc(*prep_t.done("x0"))
                yield 5
                for l in LEVELS:
                    nt = (nt0, nt1)[l % 2]
                    parts = PARTS if l == 1 else PARTS[:2]
                    if l == 1:
                        pe.wait_ge(*prep_d.after("n1b", i))
                        pe.wait_ge(*prep_a.after("x0b", i))
                    else:
                        pe.wait_ge(*prep_d.after(f"n{l}", i))
                    for n, t0, c in parts:
                        cc = slice(t0, t0 + n)
                        last = mm(pm[0:n, 2, cc], nt[0:n, cc], xx[0:n, 0, cc], start=True, stop=True)
                    last.then_inc(*prep_t.done(f"p{l}"))
                    yield 2 * l + 4
                    pe.wait_ge(*prep_a.after(f"psb{l}", i))
                    for n, t0, c in parts:
                        cc = slice(t0, t0 + n)
                        mm(pm[0:n, 0, cc], xx[0:n, 1, cc], psb[0:n, cc], start=True, stop=True)
                        last = mm(pm[0:n, 1, cc], psb[0:n, cc], xx[0:n, 1, cc], start=True, stop=True)
                    last.then_inc(*prep_t.done(f"xx{l}"))
                    yield 2 * l + 5

            def scan(i, par):
                qe, ke, pt, kg, bv, xx, ec = handed[par]
                pe.wait_ge(*scan_d.before(i))
                pe.wait_ge(*scan_a.before(i))

                def k_s(n):
                    lo, cc = CH * (n % 2), slice(CH * n, CH * n + CH)
                    pe.wait_ge(*scan_d.after(f"S{n - 1}", i))
                    mm(bw[lo:lo + CH, P:2 * P], ke[:, cc], S[:], start=True, stop=True).then_inc(*scan_t.done(f"k{n}"))

                def t_r(n):
                    lo, cc, c = CH * (n % 2), slice(CH * n, CH * n + CH), n // 2
                    rhs = bv[lo:lo + CH, c] if n == 0 else rr[lo:lo + CH]
                    pe.wait_ge(*(prep_d.after("xx5", i) if n == 0 else scan_d.after(f"R{n}", i)))
                    apart(pe)
                    mm(bw[lo:lo + CH, 0:P], xx[lo:lo + CH, 1, cc], rhs, start=True, stop=True).then_inc(*scan_t.done(f"T{n}"))

                def update(n):
                    lo, cc, c = CH * (n % 2), slice(CH * n, CH * n + CH), n // 2
                    pe.wait_ge(*scan_a.after("ks_s" if n == 1 else f"vn{n}", i))
                    if n:
                        mm(bo[:, cc], S[:], qe[:, cc], start=True, stop=False)
                    mm(bo[:, cc], vn[lo:lo + CH], pt[lo:lo + CH, cc], start=n == 0, stop=True)
                    mm(bu[:, 0:P], kg[lo:lo + CH, c], vn[lo:lo + CH], start=True, stop=True).then_inc(*scan_t.done(f"u{n}"))

                t_r(0)
                yield 0
                update(0)
                yield 1
                k_s(1)
                yield 2
                t_r(1)
                pe.wait_ge(ss_in, 16 * i + 16)
                for b in range(NB):
                    cc = slice(TP + b * L, TP + b * L + L)
                    last = mm(bu[:, 2 * P + b * L:2 * P + (b + 1) * L], ss[:, b], ke[:, cc], start=True, stop=True)
                last.then_inc(*scan_t.done("ksS"))
                yield 3
                update(1)
                turn(bw[0:TS, 2 * P:3 * P], ks_s[:], P).then_inc(*scan_t.done("trS"))
                yield 4
                pe.wait_ge(*scan_d.after("rs", i))
                k_s(2)
                apart(pe)
                mm(bu[0:TS, P:2 * P], xx[0:TS, 1, TP:T], r_s[:], start=True, stop=True).then_inc(*scan_t.done("TS"))
                yield 5
                t_r(2)
                pe.wait_ge(*scan_a.after("vn_s", i))
                mm(bo[:, TP:T], vn_s[:], pt[0:TS, TP:T], start=True, stop=False)
                for b in range(NB):
                    cc = slice(TP + b * L, TP + b * L + L)
                    last = mm(bo[:, cc], ss[:, b], qe[:, cc], start=False, stop=b == NB - 1)
                last.then_inc(*scan_t.done("oS"))
                yield 6
                update(2)
                yield 7
                k_s(3)
                yield 8
                t_r(3)
                yield 9
                update(3)
                yield 10
                pe.wait_ge(*scan_p.after("vnm", i))

                def sample_update(half, bank):
                    mm(bank, kg[0:TS, 2], vnm[:, 4 * half:4 * half + 4].rearrange("p b v -> p (b v)"),
                       start=True, stop=True).then_inc(*scan_t.done(f"Ss{half + 1}"))
                sample_update(0, bw)
                pe.wait_ge(*scan_d.after("S3", i))
                pe.wait_ge(*scan_a.after("sqo", i))
                mm(bu[:, 0:T], ones[:], sqo[:], start=True, stop=True).then_inc(*scan_t.done("nrm"))
                yield 11
                pe.wait_ge(*scan_a.after("rs1", i))
                sample_update(1, bu)

            pe_group(q_z + 1, g_z + 1, h_hi, h_lo, beside(prep=prepare(0, 0), pace=GDN_FIRST_PACE), 16)
            pe.wait_ge(bank_free, 4 * g_heads + 4)

            def head(j, par):
                last = isinstance(j, int) and j == H - 1
                mixer = beside(scan(j, par), iter(()) if last else prepare(j + 1, 1 - par))
                pe_group(j + q_heads, j + g_heads, h_hi, h_lo, mixer, 16, banks=2)
            heads(pe, head)
            pe.wait_ge(bank_free, 4 * g_gate + 4)
            pe.wait_ge(*scan_d.before(H))

            def mlstm(i):
                q_t = one(zm, i)
                pe.wait_ge(*md_.after("v", i))
                pe.wait_ge(*ma.before(i))
                sel = mrsel[32:32 + H]
                for bank, cc in ((0, slice(0, T)), (1, slice(T, 2 * T)), (2, slice(2 * T, 3 * T + NC))):
                    last = mm(pm[:, bank, 0:cc.stop - cc.start], ones[32:32 + H], sel[:, cc], start=True, stop=True)
                last.then_inc(*mt.done("rows"))
                for n, t0, c in PARTS:
                    last = turn(pm[0:n, 3, c * P:(c + 1) * P], mk[:, t0:t0 + n], P)
                last.then_inc(*mt.done("ktr"))
                yield 0
                pe.wait_ge(*ma.after("kw2", i))
                for n, t0, c in PARTS:
                    last = turn(pm[0:n, 3, c * P:(c + 1) * P], mv[:, t0:t0 + n], P)
                last.then_inc(*mt.done("vtr"))
                pe.wait_ge(*md_.after("D2", i))
                for n, t0, c in PARTS:
                    cc = slice(t0, t0 + n)
                    last = mm(pm[0:n, 0, cc], mk[:, cc], q_t[:, cc], start=True, stop=True)
                last.then_inc(*mt.done("kq"))
                yield 1

                def turn_states(half):
                    for b in range(4):
                        last = turn(pm[:, 0, b * P:(b + 1) * P], cs[:, 4 * half + b], P)
                    last.then_inc(*mt.done(f"c{half}"))

                def chunk(n):
                    lo, cc, c = CH * (n % 2), slice(CH * n, CH * n + CH), n // 2
                    if n:
                        pe.wait_ge(*md_.after(f"pr{n}", i))
                        mm(pm[:, 1, cc], ctn[:, 0:P], qw[:, cc], start=True, stop=False)
                    mm(pm[:, 1, cc], vt[lo:lo + CH, c, 0:P], mpt[lo:lo + CH, cc], start=n == 0, stop=True)
                    if n:
                        mm(pm[:, 2, cc], ones[:], prd[:, cc], start=True, stop=False)
                    mm(pm[:, 2, cc], ones[lo:lo + CH], mpt[lo:lo + CH, cc], start=n == 0, stop=True)
                    mm(pm[:, 3, 0:P + 1], kw[lo:lo + CH, c], vt[lo:lo + CH, c], start=True, stop=True).then_inc(*mt.done(f"u{n}"))

                pe.wait_ge(cs_in, 16 * i + 16)
                pe.wait_ge(*md_.after("pt2", i))
                pe.wait_ge(*ma.after("v2", i))
                turn_states(0)
                chunk(0)
                yield 2
                pe.wait_ge(*ma.after("ct0", i))
                turn_states(1)
                chunk(1)
                yield 3
                chunk(2)
                yield 4
                chunk(3)
                pe.wait_ge(*ma.after("ct1", i))
                mm(pm[:, 0, 0:NB], kw[0:TS, 2], seq[:], start=True, stop=True).then_inc(*mt.done("ns"))
                mm(pm[:, 1, TP:T], vt[0:TS, 2, 0:P], mpt[0:TS, TP:T], start=True, stop=False)
                for b in range(NB):
                    cc = slice(TP + b * L, TP + b * L + L)
                    mm(pm[:, 1, cc], cts[:, b], qw[:, cc], start=False, stop=b == NB - 1)
                mm(pm[:, 2, TP:T], ones[:], prd[:, TP:T], start=True, stop=False)
                mm(pm[:, 2, TP:T], ones[0:TS], mpt[0:TS, TP:T], start=False, stop=True).then_inc(*mt.done("so"))
                yield 5
                pe.wait_ge(*md_.after("ns2", i))
                pe.wait_ge(*mp.after("km", i))
                for half, bank in enumerate((0, 3)):
                    last = mm(pm[:, bank], vt[0:TS, 2, 0:P], km[:, 4 * half:4 * half + 4].rearrange("p b k -> p (b k)"),
                              start=True, stop=True)
                last.then_inc(*mt.done("C"))
                yield 6
                pe.wait_ge(*ma.after("abs", i))
                turn(pm[:, 2, 0:P], ctn[:, 0:P], P).then_inc(*mt.done("cp"))

            with pe.Fori(0, H) as i:
                pe_group(i + q_gate, i + g_gate, h_hi, h_lo, mlstm(i), MLSTM_STAGES)

            pe.wait_ge(*md_.before(H))
            pe.wait_ge(*ma.before(H))
            turn(pm[0:NB * H, 0, 0:P], n_s[:].rearrange("p b h -> p (b h)"), P)
            turn(pm[0:H, 1, 0:P], n_p[:], P).then_inc(*no_t.done("tr"))

            with pe.Fori(0, 4) as i:
                for u in range(4):
                    x_hi, x_lo = ((go_hi, go_lo), (mh_hi, mh_lo))[u % 2]
                    pe.wait_ge(bank_free, 8 * i + (4 * g_branch + 2 * u + 2))
                    for j in range(4):
                        pe.wait_ge(lo_ready, 16 * (i + q_branch) + (4 * u + j + 1))
                        for k in range(4):
                            kk = 2 * j + k // 2
                            last = product(ps[:, 2 * (u % 2) + k % 2, 0:T], whi[:, j, k], wlo[:, j, k], x_hi[:, kk], x_lo[:, kk],
                                           kk == 0, kk == 7)
                        last.then_inc(blocks, 1)

            pe.wait_ge(*br_d.before(4))
            pe.wait_ge(*no_a.after("p"))

            def turn_input(i):
                pe.wait_ge(x_in2, 32 * i + 32)
                pe.wait_ge(*ot_a.before(i))
                for m in range(4):
                    for n, t0, c in PARTS:
                        last = turn(pm[:, m, t0:t0 + n], xg[0:n, c, m * P:(m + 1) * P], n)
                    last.then_inc(*ot_t.done(f"x{m}"))
                yield 0

            with pe.Fori(0, 4) as i:
                pe_group(i + q_out, i + g_out, mix_hi, mix_lo, turn_input(i), 16, ring=8)
            pe.wait_ge(fw_in, 16)
            pe.wait_ge(*ot_a.before(4))
            for j in range(FC):
                last = turn(pm[:, 1, j * 2 * FT:(j + 1) * 2 * FT], fw_rows[:, j], 2 * FT)
            last.then_inc(*n2_t.done("w"))
            pe.wait_ge(*ot_p.before(4))
            mm(pm[:, 0, 0:T], ones[:], ssq[:], start=True, stop=True).then_inc(*n2_t.done("sum"))
            pe.wait_ge(*ot_d.before(4))
            pe.wait_ge(*n2_d.after("w"))
            pe.wait_ge(*n2_a.after("ln"))

            q, g, g0, k0 = q_ffn, g_ffn, 0, 0
            for c, n in enumerate(CHUNKS):
                with pe.Fori(0, n) as i:
                    r = i + g0

                    def old_rows(half):
                        yield 0
                        pe.wait_ge(old_in, 32 * r + 16 * (half + 1))
                        apart(pe)
                        for m in range(4):
                            n_ = NB * FPAD
                            last = turn(pm[:, 2 + half, m * n_:(m + 1) * n_], st_rows[:, half, m * P:(m + 1) * P], n_)
                        last.then_inc(*up_t.done(f"old{half}"))
                        yield 0
                    pe_group(2 * i + q, 2 * i + g, f_hi, f_lo, old_rows(0), 16, ring=8)
                    pe_group(2 * i + (q + 1), 2 * i + (g + 1), f_hi, f_lo, old_rows(1), 16, ring=8)
                q, g, g0 = q + 2 * n, g + 2 * n, g0 + n

                def last_rows(r):
                    pe.wait_ge(*dn_p.after("sel", r))
                    pe.wait_ge(*dn_a.before(r))
                    for t in range(8):
                        last = turn(pm[0:FPAD * (1 + NB), t // 4, t % 4 * P:(t % 4 + 1) * P], u_out[:, t], P)
                    last.then_inc(*dn_t.done("tr"))
                    yield 0
                pe.wait_ge(*up_d.before(g0 - 1))
                x_last = up_d.before(g0)
                if n == 4:
                    with pe.Fori(0, 4) as i:
                        pe_group(i + q, i + g, u_hi, u_lo, last_rows(i + 4 * c), 16, ring=8, x_last=x_last)
                else:
                    for i in range(4):
                        pe_group(q, g + i, u_hi, u_lo, last_rows(4 * c + i) if i < n else None, 16 if i < n else 0,
                                 ring=8, b0=4 * n * i, n=n, x_last=x_last)
                q, g = q + n, g + 4
            pe.wait_ge(*fin_p.before(KT))
            mm(pm[:, 3, 0:T], ones[:], ssq[:], start=True, stop=True).then_inc(*y_t.done("sum"))
            pe.wait_ge(*dn_a.before(11))
            for k in range(4):
                if k >= 2:
                    pe.wait_ge(*y_a.after(f"r{k - 2}"))
                bank = (ps, pm)[k % 2]
                pe.wait_ge(*y_d.after(f"y{4 * k + 3}"))
                for m in range(4):
                    f = 4 * k + m
                    for n, t0, c in PARTS:
                        last = turn(bank[0:n, c, m * P:(m + 1) * P], yt[:, f % 8, t0:t0 + n], P)
                last.then_inc(*y_t.done(f"t{k}"))


_OUTS = ["y_p", "y_s", "p_gconv", "p_S", "p_C", "p_n", "p_m", "p_fconv", "s_gconv", "s_S", "s_C", "s_n", "s_m", "s_fconv"]


def kernel(**inputs):
    import numpy as np
    import concourse.bacc as bacc
    from concourse.bass_utils import run_bass_kernel_spmd

    nc = bacc.Bacc("TRN2", target_bir_lowering=False, num_devices=1)
    arrays = {n: np.ascontiguousarray(x) for n, x in inputs.items()}
    arrays["norm_final_w"] = arrays["norm_final_w"].reshape(1, -1)
    a = {n: nc.dram_tensor(f"in_{n}", x.shape, F32, kind="ExternalInput").ap() for n, x in arrays.items()}
    x, s = arrays["x_prompt"].shape, arrays["x_sample"].shape
    one = lambda n: (1, x[0]) + arrays[n].shape[2:]
    states = ["state_gdn_conv", "state_gdn_S", "state_ml_C", "state_ml_n", "state_ml_m", "state_ffn_conv"]
    shapes = [x, s] + [one(n) for n in states] + [arrays[n].shape for n in states]
    o = {n: nc.dram_tensor(f"out_{n}", shape, F32, kind="ExternalOutput").ap() for n, shape in zip(_OUTS, shapes)}
    build(nc, a, o)
    r = run_bass_kernel_spmd(nc, [{f"in_{n}": x for n, x in arrays.items()}], core_ids=[0])
    return tuple(r.results[0][f"out_{n}"] for n in _OUTS)
```
